# Optimizing a Trainium2 kernel written in Bass

```python
import jax, jax.numpy as jnp
from jax import lax
import numpy as np

D_MODEL = 1024
BATCH = 1
SEQ = 512
DEPTH = 1

GRID_W = 64
CTX_LEN = 256
MIX_WIDTH = D_MODEL
RWKV_WIDTH = MIX_WIDTH // 2
HEAD_SIZE = 64
RWKV_HEADS = RWKV_WIDTH // HEAD_SIZE
FNET_WIDTH = MIX_WIDTH - RWKV_WIDTH
FNET_GROUPS = 8
FNET_GROUP_W = FNET_WIDTH // FNET_GROUPS
DECAY_LORA = 64
ICLR_LORA = 64
GATE_LORA = 128
N_DIR = 2
SHIFT_WIDTH = 3 * RWKV_WIDTH + N_DIR * (DECAY_LORA + ICLR_LORA + GATE_LORA)
IN_WIDTH = SHIFT_WIDTH + FNET_WIDTH
N_EXPERTS = 32
TOP_K = 4
D_FF = D_MODEL
SWIGLU_LIMIT = 7.0
SWIGLU_ALPHA = 1.702
EXPERT_BLOCK = 128
DEEPNORM_ALPHA = (2.0 * DEPTH) ** 0.25
DEEPNORM_BETA = (8.0 * DEPTH) ** -0.25
LN_EPS = 1e-5
GN_EPS = 64e-5


def layer_norm(u, g, b):
    u32 = u.astype(jnp.float32)
    mean = jnp.mean(u32, -1, keepdims=True)
    var = jnp.mean(jnp.square(u32 - mean), -1, keepdims=True)
    return ((u32 - mean) * lax.rsqrt(var + LN_EPS) * g + b).astype(u.dtype)

def grid_shift(u):
    b_, t, ch = u.shape
    rows = t // GRID_W
    g = u.reshape(b_, rows, GRID_W, ch)
    p = jnp.pad(g, ((0, 0), (1, 1), (1, 1), (0, 0)))
    nb = (p[:, :-2, 1:-1] + p[:, 2:, 1:-1] + p[:, 1:-1, :-2] + p[:, 1:-1, 2:]) * 0.25
    return nb.reshape(b_, t, ch)

def seq_shift(u):
    p = jnp.pad(u, ((0, 0), (1, 1), (0, 0)))
    return (p[:, :-2] + p[:, 2:]) * 0.5

def heads(z):
    return z.reshape(z.shape[:-1] + (RWKV_HEADS, HEAD_SIZE))

def rwkv_prepare(m, w0, w2_decay, a0, a2_iclr, g2_gate, k_k, k_a):
    b_, t, _ = m.shape
    c = RWKV_WIDTH
    r = m[..., :c]
    k = m[..., c:2 * c]
    v = m[..., 2 * c:3 * c]
    o = 3 * c
    wd = m[..., o:o + N_DIR * DECAY_LORA].reshape(b_, t, N_DIR, DECAY_LORA)
    o += N_DIR * DECAY_LORA
    ad = m[..., o:o + N_DIR * ICLR_LORA].reshape(b_, t, N_DIR, ICLR_LORA)
    o += N_DIR * ICLR_LORA
    gd = m[..., o:o + N_DIR * GATE_LORA].reshape(b_, t, N_DIR, GATE_LORA)
    w_log = w0 + jnp.einsum('btdr,drc->btdc', jnp.tanh(wd), w2_decay)
    w = jnp.exp(-jnp.exp(-jax.nn.softplus(-w_log) - 0.5))
    a = jax.nn.sigmoid(a0 + jnp.einsum('btdr,drc->btdc', ad, a2_iclr))
    g = jnp.einsum('btdr,drc->btdc', jax.nn.sigmoid(gd), g2_gate)
    kk = heads(k * k_k)
    kk = kk / jnp.maximum(jnp.sqrt(jnp.sum(jnp.square(kk), -1, keepdims=True)), 1e-12)
    k_d = k[:, :, None] * (1.0 + (a - 1.0) * k_a)
    return heads(r), heads(k_d), heads(v), kk, heads(w), heads(a), g

def wkv_bidir(r, k_d, v, kk, w, a, state0):
    def both(u):
        return jnp.stack([u, jnp.flip(u, 1)], 0)

    def per(u):
        return jnp.stack([u[:, :, 0], jnp.flip(u[:, :, 1], 1)], 0)

    def tm(z):
        return jnp.moveaxis(z, 2, 0)

    xs = (tm(both(r)), tm(per(w)), tm(per(k_d)), tm(both(v)), tm(both(-kk)), tm(per(kk[:, :, None] * a)))

    def step(s, inp):
        r_t, w_t, k_t, v_t, aa_t, bb_t = inp
        sa = jnp.einsum('dbhij,dbhj->dbhi', s, aa_t)
        s = s * w_t[..., None, :] + sa[..., :, None] * bb_t[..., None, :] + v_t[..., :, None] * k_t[..., None, :]
        y_t = jnp.einsum('dbhij,dbhj->dbhi', s, r_t)
        return s, y_t

    state, ys = lax.scan(step, state0, xs)
    ys = jnp.moveaxis(ys, 0, 2)
    y = jnp.stack([ys[0], jnp.flip(ys[1], 1)], axis=2)
    return y, state

def rwkv_output(y, r, k_d, v, g, r_k, gn_g, gn_b):
    b_, t = y.shape[:2]
    mean = jnp.mean(y, -1, keepdims=True)
    var = jnp.mean(jnp.square(y - mean), -1, keepdims=True)
    yn = (y - mean) * lax.rsqrt(var + GN_EPS) * heads(gn_g) + heads(gn_b)
    bonus = jnp.sum(r[:, :, None] * k_d * r_k, -1, keepdims=True) * v[:, :, None]
    return jnp.sum((yn + bonus).reshape(b_, t, N_DIR, RWKV_WIDTH) * g, axis=2)

def fourier_mix(f, w_fno, b_fno):
    b_, t, _ = f.shape
    fg = f.reshape(b_, t, FNET_GROUPS, FNET_GROUP_W).astype(jnp.float32)
    spec = jnp.real(jnp.fft.fft2(fg, axes=(1, 3), norm='ortho'))
    y = jnp.einsum('btgc,gce->btge', spec, w_fno) + b_fno
    return y.reshape(b_, t, FNET_WIDTH)

def token_mixer(h_lat, h_ctx, w_in, mu_shift, w0, w2_decay, a0, a2_iclr, g2_gate, r_k, k_k, k_a,
                gn_g, gn_b, w_fno, b_fno, w_out, need_ctx):
    f32 = jnp.float32
    p_lat = jnp.einsum('btd,de->bte', h_lat, w_in).astype(f32)
    p_ctx = jnp.einsum('btd,de->bte', h_ctx, w_in).astype(f32)
    s_lat, f_lat = p_lat[..., :SHIFT_WIDTH], p_lat[..., SHIFT_WIDTH:]
    s_ctx, f_ctx = p_ctx[..., :SHIFT_WIDTH], p_ctx[..., SHIFT_WIDTH:]
    mu = mu_shift.astype(f32)
    m_lat = s_lat + mu * (grid_shift(s_lat) - s_lat)
    m_ctx = s_ctx + mu * (seq_shift(s_ctx) - s_ctx)
    dp = (w0, w2_decay, a0, a2_iclr, g2_gate, k_k, k_a)
    r_c, k_c, v_c, kk_c, w_c, a_c, g_c = rwkv_prepare(m_ctx, *dp)
    state0 = jnp.zeros((N_DIR, h_ctx.shape[0], RWKV_HEADS, HEAD_SIZE, HEAD_SIZE), f32)
    y_c, state_c = wkv_bidir(r_c, k_c, v_c, kk_c, w_c, a_c, state0)
    r_l, k_l, v_l, kk_l, w_l, a_l, g_l = rwkv_prepare(m_lat, *dp)
    y_l, _ = wkv_bidir(r_l, k_l, v_l, kk_l, w_l, a_l, state_c)
    rw_lat = rwkv_output(y_l, r_l, k_l, v_l, g_l, r_k, gn_g, gn_b)
    out_lat = jnp.concatenate([rw_lat, fourier_mix(f_lat, w_fno, b_fno)], -1) @ w_out.astype(f32)
    out_ctx = None
    if need_ctx:
        rw_ctx = rwkv_output(y_c, r_c, k_c, v_c, g_c, r_k, gn_g, gn_b)
        out_ctx = (jnp.concatenate([rw_ctx, fourier_mix(f_ctx, w_fno, b_fno)], -1) @ w_out.astype(f32)).astype(h_ctx.dtype)
    return out_lat.astype(h_lat.dtype), out_ctx

def moe_ffn(h, w_router, b_router, w1, b1, w2, b2):
    f32 = jnp.float32
    n_tok = h.shape[0]
    logits = h.astype(f32) @ w_router.astype(f32) + b_router.astype(f32)
    top_val, top_idx = lax.top_k(logits, TOP_K)
    gates = jax.nn.softmax(top_val, axis=-1)
    n_assign = n_tok * TOP_K
    e_flat = top_idx.reshape(-1).astype(jnp.int32)
    tok_flat = jnp.repeat(jnp.arange(n_tok, dtype=jnp.int32), TOP_K)
    g_flat = gates.reshape(-1)
    order = jnp.argsort(e_flat)
    e_s, tok_s, g_s = e_flat[order], tok_flat[order], g_flat[order]
    counts = jnp.bincount(e_flat, length=N_EXPERTS).astype(jnp.int32)
    starts = jnp.cumsum(counts) - counts
    padded = (counts + EXPERT_BLOCK - 1) // EXPERT_BLOCK * EXPERT_BLOCK
    pends = jnp.cumsum(padded)
    pstarts = pends - padded
    slot = pstarts[e_s] + jnp.arange(n_assign, dtype=jnp.int32) - starts[e_s]
    n_blocks = -(-n_assign // EXPERT_BLOCK) + N_EXPERTS
    n_slots = n_blocks * EXPERT_BLOCK
    slot_tok = jnp.zeros((n_slots,), jnp.int32).at[slot].set(tok_s)
    slot_gate = jnp.zeros((n_slots,), f32).at[slot].set(g_s)
    block_start = jnp.arange(n_blocks, dtype=jnp.int32) * EXPERT_BLOCK
    block_e = jnp.minimum(jnp.searchsorted(pends, block_start, side='right'), N_EXPERTS - 1)

    def expert_block(args):
        tok_b, e = args
        xb = h[tok_b]
        u = xb @ w1[e] + b1[e]
        glu = jnp.minimum(u[:, 0::2], SWIGLU_LIMIT)
        lin = jnp.clip(u[:, 1::2], -SWIGLU_LIMIT, SWIGLU_LIMIT)
        act = glu * jax.nn.sigmoid(SWIGLU_ALPHA * glu) * (lin + 1.0)
        return act @ w2[e] + b2[e]

    y = lax.map(expert_block, (slot_tok.reshape(n_blocks, EXPERT_BLOCK), block_e))
    out = jnp.zeros((n_tok, h.shape[1]), f32).at[slot_tok].add(slot_gate[:, None] * y.reshape(n_slots, -1))
    return out.astype(h.dtype)

def first_inputs(seed: int = 0) -> dict:
    key = jax.random.key(seed)
    ks = iter(jax.random.split(key, 48))
    f32 = jnp.float32

    def nrm(shape, scale):
        return scale * jax.random.normal(next(ks), shape, f32)

    L, C, H, N = DEPTH, RWKV_WIDTH, RWKV_HEADS, HEAD_SIZE
    x = nrm((BATCH, SEQ, D_MODEL), 1.0)
    c = nrm((BATCH, D_MODEL), 1.0)
    ctx = nrm((BATCH, CTX_LEN, D_MODEL), 1.0)
    c_ctx = nrm((D_MODEL,), 1.0)
    ln0_g = 1.0 + nrm((D_MODEL,), 0.05)
    ln0_b = nrm((D_MODEL,), 0.02)
    w_ada = nrm((L, D_MODEL, 6 * D_MODEL), 0.5 * D_MODEL ** -0.5)
    b_ada = nrm((L, 6 * D_MODEL), 0.02)
    w_in = nrm((L, D_MODEL, IN_WIDTH), D_MODEL ** -0.5)
    w_in = w_in.at[:, :, 2 * C:3 * C].multiply(DEEPNORM_BETA)
    mu_shift = jax.random.uniform(next(ks), (L, SHIFT_WIDTH), f32, 0.2, 0.8)
    w0 = jax.random.uniform(next(ks), (L, N_DIR, C), f32, -6.0, 1.0)
    w2_decay = nrm((L, N_DIR, DECAY_LORA, C), 0.5 * DECAY_LORA ** -0.5)
    a0 = nrm((L, N_DIR, C), 0.5)
    a2_iclr = nrm((L, N_DIR, ICLR_LORA, C), 0.5 * ICLR_LORA ** -0.5)
    g2_gate = nrm((L, N_DIR, GATE_LORA, C), GATE_LORA ** -0.5)
    r_k = nrm((L, N_DIR, H, N), 0.1)
    k_k = 0.85 + nrm((L, C), 0.05)
    k_a = 1.0 + nrm((L, C), 0.05)
    gn_g = 1.0 + nrm((L, C), 0.05)
    gn_b = nrm((L, C), 0.02)
    w_fno = nrm((L, FNET_GROUPS, FNET_GROUP_W, FNET_GROUP_W), FNET_GROUP_W ** -0.5)
    b_fno = nrm((L, FNET_GROUPS, FNET_GROUP_W), 0.02)
    w_out = nrm((L, MIX_WIDTH, D_MODEL), DEEPNORM_BETA * MIX_WIDTH ** -0.5)
    ln1_g = 1.0 + nrm((L, D_MODEL), 0.05)
    ln1_b = nrm((L, D_MODEL), 0.02)
    w_router = nrm((L, D_MODEL, N_EXPERTS), D_MODEL ** -0.5)
    b_router = nrm((L, N_EXPERTS), 0.01)
    w1 = nrm((L, N_EXPERTS, D_MODEL, 2 * D_FF), D_MODEL ** -0.5)
    b1 = nrm((L, N_EXPERTS, 2 * D_FF), 0.02)
    w2 = nrm((L, N_EXPERTS, D_FF, D_MODEL), DEEPNORM_BETA * D_FF ** -0.5)
    b2 = nrm((L, N_EXPERTS, D_MODEL), 0.02)
    ln2_g = 1.0 + nrm((L, D_MODEL), 0.05)
    ln2_b = nrm((L, D_MODEL), 0.02)
    return {"x": x, "c": c, "ctx": ctx, "c_ctx": c_ctx, "ln0_g": ln0_g, "ln0_b": ln0_b,
            "w_ada": w_ada, "b_ada": b_ada, "w_in": w_in, "mu_shift": mu_shift, "w0": w0,
            "w2_decay": w2_decay, "a0": a0, "a2_iclr": a2_iclr, "g2_gate": g2_gate, "r_k": r_k,
            "k_k": k_k, "k_a": k_a, "gn_g": gn_g, "gn_b": gn_b, "w_fno": w_fno, "b_fno": b_fno,
            "w_out": w_out, "ln1_g": ln1_g, "ln1_b": ln1_b, "w_router": w_router, "b_router": b_router,
            "w1": w1, "b1": b1, "w2": w2, "b2": b2, "ln2_g": ln2_g, "ln2_b": ln2_b}

def first_block(x, c, ctx, c_ctx, ln0_g, ln0_b, w_ada, b_ada, w_in, mu_shift, w0, w2_decay, a0, a2_iclr,
              g2_gate, r_k, k_k, k_a, gn_g, gn_b, w_fno, b_fno, w_out, ln1_g, ln1_b, w_router, b_router,
              w1, b1, w2, b2, ln2_g, ln2_b):
    x = layer_norm(x, ln0_g, ln0_b)
    ctx = layer_norm(ctx, ln0_g, ln0_b)
    for l in range(DEPTH):
        need_ctx = l < DEPTH - 1
        mod = (jax.nn.silu(c) @ w_ada[l] + b_ada[l])[:, None, :]
        sh1, sc1, gt1, sh2, sc2, gt2 = jnp.split(mod, 6, axis=-1)
        mod_c = jax.nn.silu(c_ctx) @ w_ada[l] + b_ada[l]
        sh1c, sc1c, gt1c, sh2c, sc2c, gt2c = jnp.split(mod_c, 6, axis=-1)
        h = x * (1.0 + sc1) + sh1
        hc = ctx * (1.0 + sc1c) + sh1c
        mo, mo_c = token_mixer(h, hc, w_in[l], mu_shift[l], w0[l], w2_decay[l], a0[l], a2_iclr[l], g2_gate[l],
                               r_k[l], k_k[l], k_a[l], gn_g[l], gn_b[l], w_fno[l], b_fno[l], w_out[l], need_ctx)
        x = layer_norm(DEEPNORM_ALPHA * x + gt1 * mo, ln1_g[l], ln1_b[l])
        h = x * (1.0 + sc2) + sh2
        f = moe_ffn(h.reshape(-1, D_MODEL), w_router[l], b_router[l], w1[l], b1[l], w2[l], b2[l]).reshape(x.shape)
        x = layer_norm(DEEPNORM_ALPHA * x + gt2 * f, ln2_g[l], ln2_b[l])
        if need_ctx:
            ctx = layer_norm(DEEPNORM_ALPHA * ctx + gt1c * mo_c, ln1_g[l], ln1_b[l])
            hc = ctx * (1.0 + sc2c) + sh2c
            fc = moe_ffn(hc.reshape(-1, D_MODEL), w_router[l], b_router[l], w1[l], b1[l], w2[l], b2[l]).reshape(ctx.shape)
            ctx = layer_norm(DEEPNORM_ALPHA * ctx + gt2c * fc, ln2_g[l], ln2_b[l])
    return x


DEPTH_2 = 2

HEAD_DIM = 64
Q_BLOCK = 128
ROPE_THETA = 10000.0
EPS = 1e-6
NSA_HEADS = 8
NSA_KV_GROUPS = 2
NSA_CMP_LEN = 32
NSA_CMP_STRIDE = 16
NSA_CMP_HIDDEN = 128
NSA_SEL_LEN = 64
NSA_SEL_TOPK = 16
NSA_WINDOW = 512
FORCE_SCORE = 1e9
NSA_WIDTH = NSA_HEADS * HEAD_DIM
NSA_KV_WIDTH = NSA_KV_GROUPS * HEAD_DIM
FOX_HEADS = 8
FOX_WIDTH = FOX_HEADS * HEAD_DIM
MEM_LEN = 256
MEM_HEADS = 4
MEM_HEAD_DIM = 128
MEM_WIDTH = MEM_HEADS * MEM_HEAD_DIM
N_BRANCH = 3
IN_SPLITS = (NSA_WIDTH, 6 * NSA_KV_WIDTH, 3 * NSA_HEADS, NSA_WIDTH,
             3 * FOX_WIDTH, FOX_HEADS, FOX_WIDTH,
             MEM_WIDTH, MEM_WIDTH,
             N_BRANCH * D_MODEL)
IN_WIDTH_2 = sum(IN_SPLITS)


def _rmsnorm(x, g):
    xf = x.astype(jnp.float32)
    y = xf * lax.rsqrt(jnp.mean(xf * xf, axis=-1, keepdims=True) + EPS)
    return (y * g.astype(jnp.float32)).astype(x.dtype)

def _rope(x, pos):
    half = x.shape[-1] // 2
    inv_freq = ROPE_THETA ** (-jnp.arange(half, dtype=jnp.float32) / half)
    ang = pos.astype(jnp.float32)[:, None] * inv_freq[None, :]
    cos = jnp.cos(ang)[None, :, None, :]
    sin = jnp.sin(ang)[None, :, None, :]
    xf = x.astype(jnp.float32)
    x1, x2 = xf[..., :half], xf[..., half:]
    return jnp.concatenate([x1 * cos - x2 * sin, x2 * cos + x1 * sin], axis=-1).astype(x.dtype)

def _masked_softmax(s, mask):
    s = jnp.where(mask, s.astype(jnp.float32), -jnp.inf)
    m = jnp.max(s, axis=-1, keepdims=True)
    m = jnp.where(jnp.isfinite(m), m, 0.0)
    e = jnp.exp(s - m)
    d = jnp.sum(e, axis=-1, keepdims=True)
    return e / jnp.where(d > 0.0, d, 1.0)

def _split(z, sizes):
    return jnp.split(z, np.cumsum(sizes)[:-1].tolist(), axis=-1)

def _compress(x, pe, w1, w2):
    B, T, G, dk = x.shape
    r = NSA_CMP_LEN // NSA_CMP_STRIDE
    n_chunk = T // NSA_CMP_STRIDE
    n_cmp = n_chunk - r + 1
    ch = x.reshape(B, n_chunk, NSA_CMP_STRIDE, G, dk)
    blk = jnp.concatenate([ch[:, i:i + n_cmp] for i in range(r)], axis=2)
    blk = blk + pe[None, None, :, None, :].astype(x.dtype)
    flat = blk.transpose(0, 1, 3, 2, 4).reshape(B, n_cmp, G, NSA_CMP_LEN * dk)
    return jax.nn.silu(flat @ w1) @ w2

def _overlap(n_cmp, n_slc):
    cs = np.arange(n_cmp)[:, None] * NSA_CMP_STRIDE
    ss = np.arange(n_slc)[None, :] * NSA_SEL_LEN
    ov = np.clip(np.minimum(cs + NSA_CMP_LEN, ss + NSA_SEL_LEN) - np.maximum(cs, ss), 0, None)
    return jnp.asarray(ov / NSA_CMP_LEN, dtype=jnp.float32)

def _nsa(q, kv, gate, pe_k, w1_k, w2_k, pe_v, w1_v, w2_v, q_g, k_g):
    B, T, _ = q.shape
    G, R, dk = NSA_KV_GROUPS, NSA_HEADS // NSA_KV_GROUPS, HEAD_DIM
    pos = jnp.arange(T)
    nqb = T // Q_BLOCK
    n_slc = T // NSA_SEL_LEN
    n_top = min(NSA_SEL_TOPK, n_slc)
    scale = dk ** -0.5
    qh = _rope(_rmsnorm(q.reshape(B, T, NSA_HEADS, dk), q_g), pos)
    k_c, v_c, k_s, v_s, k_w, v_w = [a.reshape(B, T, G, dk) for a in jnp.split(kv, 6, axis=-1)]
    k_c = _rmsnorm(_compress(_rope(k_c, pos), pe_k, w1_k, w2_k), k_g[0])
    v_c = _compress(v_c, pe_v, w1_v, w2_v)
    n_cmp = k_c.shape[1]
    k_s = _rope(_rmsnorm(k_s, k_g[1]), pos)
    k_w = _rope(_rmsnorm(k_w, k_g[2]), pos)
    ov = _overlap(n_cmp, n_slc)
    ks_blk = k_s.reshape(B, n_slc, NSA_SEL_LEN, G, dk).transpose(0, 3, 1, 2, 4)
    vs_blk = v_s.reshape(B, n_slc, NSA_SEL_LEN, G, dk).transpose(0, 3, 1, 2, 4)
    kw_pad = jnp.pad(k_w, ((0, 0), (NSA_WINDOW, 0), (0, 0), (0, 0)))
    vw_pad = jnp.pad(v_w, ((0, 0), (NSA_WINDOW, 0), (0, 0), (0, 0)))
    gather = jax.vmap(jax.vmap(lambda blocks, ix: blocks[ix]))
    cmp_end = jnp.arange(n_cmp) * NSA_CMP_STRIDE + NSA_CMP_LEN - 1
    jblk = jnp.arange(n_slc)
    qblocks = qh.reshape(B, nqb, Q_BLOCK, G, R, dk).transpose(1, 0, 2, 3, 4, 5)

    def block(args):
        qb, i = args
        t = i * Q_BLOCK + jnp.arange(Q_BLOCK)
        s = jnp.einsum('bqgrd,bngd->bgrqn', qb, k_c) * scale
        p_c = _masked_softmax(s, cmp_end[None, :] <= t[:, None])
        o_c = jnp.einsum('bgrqn,bngd->bqgrd', p_c.astype(v_c.dtype), v_c)
        imp = jnp.einsum('bgrqn,nj->bgqj', p_c, ov)
        cur = t // NSA_SEL_LEN
        forced = (jblk[None] == 0) | (jblk[None] == cur[:, None]) | (jblk[None] == cur[:, None] - 1)
        score = jnp.where(forced, FORCE_SCORE, imp)
        score = jnp.where(jblk[None] <= cur[:, None], score, -jnp.inf)
        _, idx = lax.top_k(score, n_top)
        sel_ok = idx <= cur[None, None, :, None]
        kg = gather(ks_blk, idx)
        vg = gather(vs_blk, idx)
        s = jnp.einsum('bqgrd,bgqnkd->bgrqnk', qb, kg) * scale
        kpos = idx[..., None] * NSA_SEL_LEN + jnp.arange(NSA_SEL_LEN)
        smask = sel_ok[..., None] & (kpos <= t[None, None, :, None, None])
        m_sel = n_top * NSA_SEL_LEN
        p_s = _masked_softmax(s.reshape(B, G, R, Q_BLOCK, m_sel),
                              smask[:, :, None].reshape(B, G, 1, Q_BLOCK, m_sel))
        o_s = jnp.einsum('bgrqm,bgqmd->bqgrd', p_s.astype(vg.dtype), vg.reshape(B, G, Q_BLOCK, m_sel, dk))
        kw = lax.dynamic_slice_in_dim(kw_pad, i * Q_BLOCK, Q_BLOCK + NSA_WINDOW, axis=1)
        vw = lax.dynamic_slice_in_dim(vw_pad, i * Q_BLOCK, Q_BLOCK + NSA_WINDOW, axis=1)
        spos = i * Q_BLOCK - NSA_WINDOW + jnp.arange(Q_BLOCK + NSA_WINDOW)
        diff = t[:, None] - spos[None, :]
        wmask = (diff >= 0) & (diff < NSA_WINDOW) & (spos[None, :] >= 0)
        s = jnp.einsum('bqgrd,bkgd->bgrqk', qb, kw) * scale
        p_w = _masked_softmax(s, wmask)
        o_w = jnp.einsum('bgrqk,bkgd->bqgrd', p_w.astype(vw.dtype), vw)
        return o_c, o_s, o_w

    o_c, o_s, o_w = lax.map(block, (qblocks, jnp.arange(nqb)))
    to_bthd = lambda o: o.transpose(1, 0, 2, 3, 4, 5).reshape(B, T, NSA_HEADS, dk)
    g = jax.nn.sigmoid(gate.astype(jnp.float32)).reshape(B, T, NSA_HEADS, 3, 1).astype(q.dtype)
    o = g[..., 0, :] * to_bthd(o_c) + g[..., 1, :] * to_bthd(o_s) + g[..., 2, :] * to_bthd(o_w)
    return o.reshape(B, T, NSA_WIDTH)

def _fox(qkv, f_logit, q_g, k_g, f_bias):
    B, T, _ = qkv.shape
    H, dk = FOX_HEADS, HEAD_DIM
    nqb = T // Q_BLOCK
    scale = dk ** -0.5
    q, k, v = [a.reshape(B, T, H, dk) for a in jnp.split(qkv, 3, axis=-1)]
    q = _rmsnorm(q, q_g)
    k = _rmsnorm(k, k_g)
    log_f = jax.nn.log_sigmoid(f_logit.astype(jnp.float32) + f_bias.astype(jnp.float32))
    c = jnp.cumsum(log_f, axis=1).transpose(0, 2, 1)
    qblocks = q.reshape(B, nqb, Q_BLOCK, H, dk).transpose(1, 0, 2, 3, 4)
    cblocks = c.reshape(B, H, nqb, Q_BLOCK).transpose(2, 0, 1, 3)
    kpos = jnp.arange(T)

    def block(args):
        qb, cq, i = args
        t = i * Q_BLOCK + jnp.arange(Q_BLOCK)
        s = jnp.einsum('bqhd,bkhd->bhqk', qb, k).astype(jnp.float32) * scale
        s = s + cq[..., None] - c[:, :, None, :]
        p = _masked_softmax(s, kpos[None, :] <= t[:, None])
        return jnp.einsum('bhqk,bkhd->bqhd', p.astype(v.dtype), v)

    o = lax.map(block, (qblocks, cblocks, jnp.arange(nqb)))
    return o.transpose(1, 0, 2, 3, 4).reshape(B, T, FOX_WIDTH)

def _memory_xattn(q, mem_kv, q_g, k_g):
    B, T, _ = q.shape
    M = mem_kv.shape[1]
    q = _rmsnorm(q.reshape(B, T, MEM_HEADS, MEM_HEAD_DIM), q_g)
    k, v = [a.reshape(B, M, MEM_HEADS, MEM_HEAD_DIM) for a in jnp.split(mem_kv, 2, axis=-1)]
    k = _rmsnorm(k, k_g)
    s = jnp.einsum('bthd,bmhd->bhtm', q, k).astype(jnp.float32) * (MEM_HEAD_DIM ** -0.5)
    p = jax.nn.softmax(s, axis=-1)
    return jnp.einsum('bhtm,bmhd->bthd', p.astype(v.dtype), v).reshape(B, T, MEM_WIDTH)

def second_inputs(seed: int = 0) -> dict:
    key = jax.random.key(seed)
    ks = jax.random.split(key, 24)
    f32 = jnp.float32
    L = DEPTH_2

    def nrm(k, shape, scale):
        return jax.random.normal(k, shape, f32) * scale

    def gain(k, shape):
        return 1.0 + 0.05 * jax.random.normal(k, shape, f32)

    cmp_in = NSA_CMP_LEN * HEAD_DIM
    return {
        'x': nrm(ks[0], (BATCH, SEQ, D_MODEL), 1.0),
        'mem': nrm(ks[1], (BATCH, MEM_LEN, D_MODEL), 1.0),
        'norm_g': gain(ks[2], (L, D_MODEL)),
        'mem_norm_g': gain(ks[3], (L, D_MODEL)),
        'w_in': nrm(ks[4], (L, D_MODEL, IN_WIDTH_2), D_MODEL ** -0.5),
        'nsa_q_norm': gain(ks[5], (L, HEAD_DIM)),
        'nsa_k_norm': gain(ks[6], (L, 3, HEAD_DIM)),
        'cmp_pe_k': nrm(ks[7], (L, NSA_CMP_LEN, HEAD_DIM), 0.1),
        'cmp_w1_k': nrm(ks[8], (L, cmp_in, NSA_CMP_HIDDEN), cmp_in ** -0.5),
        'cmp_w2_k': nrm(ks[9], (L, NSA_CMP_HIDDEN, HEAD_DIM), NSA_CMP_HIDDEN ** -0.5),
        'cmp_pe_v': nrm(ks[10], (L, NSA_CMP_LEN, HEAD_DIM), 0.1),
        'cmp_w1_v': nrm(ks[11], (L, cmp_in, NSA_CMP_HIDDEN), cmp_in ** -0.5),
        'cmp_w2_v': nrm(ks[12], (L, NSA_CMP_HIDDEN, HEAD_DIM), NSA_CMP_HIDDEN ** -0.5),
        'fox_q_norm': gain(ks[13], (L, HEAD_DIM)),
        'fox_k_norm': gain(ks[14], (L, HEAD_DIM)),
        'fox_f_bias': jax.random.uniform(ks[15], (L, FOX_HEADS), f32, 1.0, 4.0),
        'mem_q_norm': gain(ks[16], (L, MEM_HEAD_DIM)),
        'mem_k_norm': gain(ks[17], (L, MEM_HEAD_DIM)),
        'w_mem_kv': nrm(ks[18], (L, D_MODEL, 2 * MEM_WIDTH), D_MODEL ** -0.5),
        'w_branch_a': nrm(ks[19], (L, NSA_WIDTH, D_MODEL), NSA_WIDTH ** -0.5),
        'w_branch_b': nrm(ks[20], (L, FOX_WIDTH, D_MODEL), FOX_WIDTH ** -0.5),
        'w_branch_m': nrm(ks[21], (L, MEM_WIDTH, D_MODEL), MEM_WIDTH ** -0.5),
        'w_out': nrm(ks[22], (L, D_MODEL, D_MODEL), D_MODEL ** -0.5),
    }

def second_block(x, mem, norm_g, mem_norm_g, w_in, nsa_q_norm, nsa_k_norm,
              cmp_pe_k, cmp_w1_k, cmp_w2_k, cmp_pe_v, cmp_w1_v, cmp_w2_v,
              fox_q_norm, fox_k_norm, fox_f_bias, mem_q_norm, mem_k_norm, w_mem_kv,
              w_branch_a, w_branch_b, w_branch_m, w_out):
    B, T, D = x.shape
    for l in range(DEPTH_2):
        h = _rmsnorm(x, norm_g[l])
        z = h @ w_in[l]
        (nsa_q, nsa_kv, nsa_gate, nsa_silu, fox_qkv, fox_f, fox_silu,
         mem_q, mem_silu, merge_g) = _split(z, IN_SPLITS)
        o_a = _nsa(nsa_q, nsa_kv, nsa_gate, cmp_pe_k[l], cmp_w1_k[l], cmp_w2_k[l],
                   cmp_pe_v[l], cmp_w1_v[l], cmp_w2_v[l], nsa_q_norm[l], nsa_k_norm[l])
        o_a = o_a * jax.nn.silu(nsa_silu)
        o_b = _fox(fox_qkv, fox_f, fox_q_norm[l], fox_k_norm[l], fox_f_bias[l]) * jax.nn.silu(fox_silu)
        mem_kv = _rmsnorm(mem, mem_norm_g[l]) @ w_mem_kv[l]
        o_m = _memory_xattn(mem_q, mem_kv, mem_q_norm[l], mem_k_norm[l]) * jax.nn.silu(mem_silu)
        g = jax.nn.sigmoid(merge_g.astype(jnp.float32)).reshape(B, T, N_BRANCH, D).astype(x.dtype)
        u = (g[:, :, 0] * (o_a @ w_branch_a[l])
             + g[:, :, 1] * (o_b @ w_branch_b[l])
             + g[:, :, 2] * (o_m @ w_branch_m[l]))
        x = x + u @ w_out[l]
    return x


def setup_inputs(seed=0):
    out = dict(first_inputs(seed))
    for name, value in second_inputs(seed + 1).items():
        if name != "x":
            out[name + "_2"] = value
    return out


def reference(
    x, c, ctx, c_ctx, ln0_g, ln0_b, w_ada, b_ada, w_in, mu_shift, w0, w2_decay, a0, a2_iclr,
    g2_gate, r_k, k_k, k_a, gn_g, gn_b, w_fno, b_fno, w_out, ln1_g, ln1_b, w_router, b_router,
    w1, b1, w2, b2, ln2_g, ln2_b, mem_2, norm_g_2, mem_norm_g_2, w_in_2, nsa_q_norm_2,
    nsa_k_norm_2, cmp_pe_k_2, cmp_w1_k_2, cmp_w2_k_2, cmp_pe_v_2, cmp_w1_v_2, cmp_w2_v_2,
    fox_q_norm_2, fox_k_norm_2, fox_f_bias_2, mem_q_norm_2, mem_k_norm_2, w_mem_kv_2,
    w_branch_a_2, w_branch_b_2, w_branch_m_2, w_out_2,
):
    x = first_block(
        x, c, ctx, c_ctx, ln0_g, ln0_b, w_ada, b_ada, w_in, mu_shift, w0, w2_decay, a0, a2_iclr,
        g2_gate, r_k, k_k, k_a, gn_g, gn_b, w_fno, b_fno, w_out, ln1_g, ln1_b, w_router,
        b_router, w1, b1, w2, b2, ln2_g, ln2_b,
    )
    return second_block(
        x, mem_2, norm_g_2, mem_norm_g_2, w_in_2, nsa_q_norm_2, nsa_k_norm_2, cmp_pe_k_2,
        cmp_w1_k_2, cmp_w2_k_2, cmp_pe_v_2, cmp_w1_v_2, cmp_w2_v_2, fox_q_norm_2, fox_k_norm_2,
        fox_f_bias_2, mem_q_norm_2, mem_k_norm_2, w_mem_kv_2, w_branch_a_2, w_branch_b_2,
        w_branch_m_2, w_out_2,
    )


_drawn_inputs = setup_inputs


def setup_inputs(seed=0):
    import zlib

    import numpy as np

    out = dict(_drawn_inputs(seed))
    spreads = {}
    factors = {'c_ctx': 2.88,
     'b_ada': 3.591,
     'w2_decay': 8.0,
     'a0': 3.39,
     'a2_iclr': 3.948,
     'r_k': 7.457,
     'k_k': 5.135,
     'k_a': 5.708,
     'gn_g': 8.0,
     'gn_b': 8.0,
     'b_fno': 8.0,
     'b_router': 8.0,
     'b1': 8.0,
     'b2': 8.0,
     'norm_g_2': 3.075,
     'mem_norm_g_2': 8.0,
     'nsa_q_norm_2': 8.0,
     'nsa_k_norm_2': 8.0,
     'cmp_pe_k_2': 8.0,
     'cmp_pe_v_2': 4.24,
     'fox_q_norm_2': 8.0,
     'fox_k_norm_2': 8.0,
     'mem_q_norm_2': 8.0,
     'mem_k_norm_2': 8.0}
    for name, (base, spread) in spreads.items():
        noise = np.random.default_rng([zlib.crc32(name.encode()), seed]).standard_normal(out[name].shape)
        drawn = base * np.exp(spread * noise) if base else spread * noise
        out[name] = __import__('jax').numpy.asarray(drawn.astype(out[name].dtype))
    for name, factor in factors.items():
        out[name] = (out[name] * factor).astype(out[name].dtype)
    return out
```

```python
from contextlib import ExitStack, contextmanager

import numpy as np

import concourse.bass as bass
from concourse import mybir

F32 = mybir.dt.float32
F32R = mybir.dt.float32r
I32 = mybir.dt.int32
U32 = mybir.dt.uint32
ALU = mybir.AluOpType
ACT = mybir.ActivationFunctionType
AX_X = mybir.AxisListType.X

P = 128
D = 1024
KD = D // P
SEQ = 512
CTX = 256
TT = SEQ // P
ALLT = SEQ + CTX
TA = ALLT // P
GRID_W = 64
GRID_H = SEQ // GRID_W
C = 512
HS = 64
SHIFT = 2048
FN = 512
E = 32
TOPK = 4
CH = 64
NCH = ALLT // CH
LATCH = SEQ // CH
LN_EPS = 1e-5
GN_EPS = 64e-5
RMS_EPS = 1e-6
ALPHA = 2.0 ** 0.25
LIMIT = 7.0
SW_ALPHA = 1.702
DECAY = -float(np.exp(-0.5))
NEG = -1e30
LAYERS = 2
ZW = 4896
MERGE0 = ZW
NCMP = 31


def constants():
    p = np.arange(P)[:, None]
    f = np.arange(P)[None, :]
    same = (p // CH) == (f // CH)
    small = {
        "ident": p == f,
        "headones": same,
        "dir0": np.concatenate([same & (p < f), same & (p <= f)] * 2, 1),
        "dir1": np.concatenate([same & (p > f), same & (p >= f)] * 2, 1),
        "upto": p <= f,
        "before": p < f,
        "ones": np.ones((P, P)),
        "iota": np.broadcast_to(f, (P, P)),
        "causal": np.where(f <= p, 0.0, NEG),
        "restart": np.broadcast_to(np.arange(ALLT) % CH != 0, (P, ALLT)),
        "step": np.full((P, TT), P),
        "eye32": (p % E) == np.arange(E)[None, :],
        "eye2": (p % CH) == np.arange(CH)[None, :],
    }
    for b in (1, 2, 4, 8, 16, 32):
        low = ((p // (2 * b)) == (f // (2 * b))) & ((p // b) % 2 == 1) & ((f // b) % 2 == 0)
        small[f"low{b}"] = low
        small[f"up{b}"] = low.T
    t = np.arange(SEQ)
    n = np.arange(32)
    ok = (n[None, :] < NCMP) & (n[None, :] * 16 + 31 <= t[:, None])

    def rows(a):
        return a.reshape(TT, P, -1).transpose(1, 0, 2).reshape(P, -1)

    small["cmpok"] = rows(ok)
    small["cmpadd"] = rows(np.where(ok, 0.0, NEG))
    half = 32
    ang = t[:, None].astype(np.float32) * (np.float32(10000.0) ** (-np.arange(half, dtype=np.float32) / half))
    small["cos"] = rows(np.cos(ang))
    small["sin"] = rows(np.sin(ang))
    k = 2 * np.pi * ((t[:, None] * t[None, :]) % SEQ) / SEQ
    j = np.arange(CH)
    q = 2 * np.pi * ((j[:, None] * j[None, :]) % CH) / CH
    norm = 1.0 / np.sqrt(SEQ * CH)
    big = {
        "dftc": rows(np.cos(k)),
        "dfts": rows(np.sin(k)),
        "chc": np.kron(np.eye(2), np.cos(q) * norm),
        "chs": np.kron(np.eye(2), -np.sin(q) * norm),
    }

    def pack(tables):
        at, where, parts = 0, {}, []
        for name, a in tables.items():
            a = np.asarray(a, np.float32)
            where[name] = (at, a.shape[1])
            at += a.shape[1]
            parts.append(a)
        return np.ascontiguousarray(np.concatenate(parts, 1)), where

    return pack(small), pack(big)


(SMALL, SMALL_AT), (BIG, BIG_AT) = constants()


class Chain:

    def __init__(self, eng, sem):
        self.eng, self.sem, self.n = eng, sem, 0

    def __call__(self, ins):
        ins.then_inc(self.sem, 1)
        self.n += 1
        self.eng.wait_ge(self.sem, self.n)


@contextmanager
def stage(nc, *names):
    with ExitStack() as keep:
        sems = [keep.enter_context(nc.semaphore(n)) for n in names]
        with nc.Block() as block:
            yield (block, *sems)
        for s in sems:
            nc.sync.sem_clear(s)
        nc.all_engine_barrier()


def bc(ap, axis, n):
    ap = ap.unsqueeze(axis)
    shape = list(ap.shape)
    shape[axis] = n
    return ap.to_broadcast(shape)


def turn(nc, bank, ident, groups):
    with stage(nc, "turned", "evac_v", "evac_a") as (block, turned, evac_v, evac_a):
        @block.tensor
        def _(pe):
            for g, (srcs, _) in enumerate(groups):
                if g >= 4:
                    pe.wait_ge(evac_v if g % 2 == 0 else evac_a, (g - 4) // 2 + 1)
                at = 0
                for s in srcs:
                    n, m = s.shape[0], s.shape[1]
                    last = pe.transpose(bank[g % 4][0:m, at:at + n], s, ident[0:n, 0:n])
                    at += n
                last.then_inc(turned, 1)

        def copies(eng, g):
            dst = groups[g][1]
            return dst, bank[g % 4][0:dst.shape[0], 0:dst.size() // dst.shape[0]]

        @block.vector
        def _(dve):
            for g in range(0, len(groups), 2):
                dve.wait_ge(turned, g + 1)
                dst, src = copies(dve, g)
                dve.tensor_copy(dst, src if dst.ndim == 2 else src.rearrange("p (a b) -> p a b", a=dst.shape[1])).then_inc(evac_v, 1)

        @block.scalar
        def _(act):
            for g in range(1, len(groups), 2):
                act.wait_ge(turned, g + 1)
                dst, src = copies(act, g)
                act.activation(dst, src if dst.ndim == 2 else src.rearrange("p (a b) -> p a b", a=dst.shape[1]), ACT.Copy).then_inc(evac_a, 1)


def ring_gemm(nc, bank, w_piece, width, pieces, rows, lhs, kt, ring, evac):
    nb = len(ring)
    with stage(nc, *[f"w_in{i}" for i in range(nb)], "prod", "prod_out") as sems:
        block, w_in, (prod, prod_out) = sems[0], sems[1:1 + nb], sems[1 + nb:]

        @block.sync
        def _(sp):
            for n in range(pieces):
                if n >= nb:
                    sp.wait_ge(prod, rows * (n - nb + 1))
                w = w_piece(n)
                sp.dma_start(ring[n % nb][:, 0:kt, 0:w.shape[2]], w).then_inc(w_in[n % nb], 16)

        @block.tensor
        def _(pe):
            for n in range(pieces):
                pe.wait_ge(w_in[n % nb], 16 * (n // nb + 1))
                for m in range(rows):
                    i = n * rows + m
                    if i >= 4:
                        pe.wait_ge(prod_out, i - 3)
                    for k in range(kt):
                        last = pe.matmul(bank[i % 4][:, 0:width(n)], lhs(k, m), ring[n % nb][:, k, 0:width(n)],
                                         start=(k == 0), stop=(k == kt - 1))
                    last.then_inc(prod, 1)

        @block.scalar
        def _(act):
            for n in range(pieces):
                for m in range(rows):
                    i = n * rows + m
                    act.wait_ge(prod, i + 1)
                    evac(act, n, m, bank[i % 4][:, 0:width(n)]).then_inc(prod_out, 1)


def layer_norm_stage(nc, x, n, gain, bias, stats, eps=LN_EPS):
    mv = stats[:, 0:2 * n].rearrange("p (t s) -> p t s", s=2)
    six = stats[:, 16:16 + 12 * n].rearrange("p (t h s) -> p t h s", h=2, s=6)
    with stage(nc, "dve_step", "var_ready", "root_ready") as (block, dve_step, var_ready, root_ready):
        @block.vector
        def _(dve):
            done = Chain(dve, dve_step)
            for t in range(n):
                for h in range(2):
                    done(dve.bn_stats(six[:, t, h, :], x[:, t, h * 512:(h + 1) * 512]))
                done(dve.bn_aggr(mv[:, t, :], six[:, t, :, :]))
            dve.tensor_scalar(mv[:, :, 1], mv[:, :, 1], eps, None, ALU.add).then_inc(var_ready, 1)
            dve.wait_ge(root_ready, 1)
            done(dve.reciprocal(mv[:, :, 1], mv[:, :, 1]))
            for t in range(n):
                done(dve.tensor_scalar(x[:, t, :], x[:, t, :], mv[:, t, 0:1], mv[:, t, 1:2], ALU.subtract, ALU.mult))
            done(dve.tensor_tensor(x[:, 0:n, :], x[:, 0:n, :], bc(gain, 1, n), ALU.mult))
            done(dve.tensor_tensor(x[:, 0:n, :], x[:, 0:n, :], bc(bias, 1, n), ALU.add))

        @block.scalar
        def _(act):
            act.wait_ge(var_ready, 1)
            act.activation(mv[:, :, 1], mv[:, :, 1], ACT.Sqrt).then_inc(root_ready, 1)


def modulation(nc, A, bank, T, ring):
    nb = len(ring)
    mod_names = [f"ada_in{i}" for i in range(nb)]
    with stage(nc, *mod_names, "small_in", "c_in", "bias_in", "sig_ready", "wide_ready", "prod", "prod_out", "dve_step") as sems:
        block, ada_in = sems[0], sems[1:1 + nb]
        small_in, c_in, bias_in, sig_ready, wide_ready, prod, prod_out, dve_step = sems[1 + nb:]
        w = A["w_ada"][0].rearrange("(k p) n -> p k n", p=P)
        jobs = [(n, 0) for n in range(4) for _ in (0,)] + []
        jobs = [(n, v) for n in range(12) for v in ((0, 1) if n < 4 else (0,))]
        last_job = {n: max(i for i, (m, _) in enumerate(jobs) if m == n) for n in range(12)}

        @block.sync
        def _(sp):
            sp.dma_start(T["c2"][:, 0:KD], A["c"][0].rearrange("(k p) -> p k", p=P)).then_inc(c_in, 16)
            sp.dma_start(T["c2"][:, KD:2 * KD], A["c_ctx"].rearrange("(k p) -> p k", p=P)).then_inc(c_in, 16)
            sp.dma_start(T["adab"][:, :], A["b_ada"]).then_inc(bias_in, 16)
            for n in range(12):
                if n >= nb:
                    sp.wait_ge(prod, last_job[n - nb] + 1)
                sp.dma_start(ring[n % nb][:, :, :], w[:, :, n * 512:(n + 1) * 512]).then_inc(ada_in[n % nb], 16)

        @block.scalar
        def _(act):
            act.dma_start(T["small"][:, :], A["small"]).then_inc(small_in, 16)
            act.dma_start(T["xn"][:, 0:TT, :], A["x"][0].rearrange("(t p) d -> p t d", p=P)).then_inc(small_in, 16)
            act.dma_start(T["xn"][:, TT:TA, :], A["ctx"][0].rearrange("(t p) d -> p t d", p=P)).then_inc(small_in, 16)
            act.dma_start(T["gain"][:, :], A["ln0_g"].partition_broadcast(P)).then_inc(small_in, 16)
            act.dma_start(T["bias"][:, :], A["ln0_b"].partition_broadcast(P)).then_inc(small_in, 16)
            act.wait_ge(c_in, 32)
            act.activation(T["csig"][:, :], T["c2"][:, :], ACT.Sigmoid).then_inc(sig_ready, 1)
            for i, (n, v) in enumerate(jobs):
                act.wait_ge(prod, i + 1)
                dst = (T["modc"] if v else T["modb"])[:, n * 512:(n + 1) * 512]
                plus = 1.0 if n // 2 in (1, 4) else 0.0
                act.activation(dst, bank[i % 4][:, :], ACT.Copy, bias=plus).then_inc(prod_out, 1)
            act.wait_ge(small_in, 16 * 5)

        @block.vector
        def _(dve):
            done = Chain(dve, dve_step)
            done(dve.memset(T["onerow"][:, :], 1.0))
            dve.wait_ge(sig_ready, 1)
            done(dve.tensor_tensor(T["csig"][:, :], T["csig"][:, :], T["c2"][:, :], ALU.mult))
            dve.tensor_copy(T["cwide"][:, :, :], bc(T["csig"][:, :], 2, P)).then_inc(wide_ready, 1)

        @block.tensor
        def _(pe):
            pe.wait_ge(wide_ready, 1)
            pe.wait_ge(bias_in, 16)
            for i, (n, v) in enumerate(jobs):
                if v == 0:
                    pe.wait_ge(ada_in[n % nb], 16 * (n // nb + 1))
                if i >= 4:
                    pe.wait_ge(prod_out, i - 3)
                for k in range(KD):
                    pe.matmul(bank[i % 4][:, :], T["cwide"][:, KD * v + k, :], ring[n % nb][:, k, :], start=(k == 0), stop=False)
                pe.matmul(bank[i % 4][:, :], T["onerow"][:, :], T["adab"][:, n * 512:(n + 1) * 512],
                          start=False, stop=True).then_inc(prod, 1)


def modulate_stage(nc, dst, src, n, scale, shift):
    with stage(nc, "dve_step") as (block, dve_step):
        @block.vector
        def _(dve):
            done = Chain(dve, dve_step)
            done(dve.tensor_tensor(dst, src, bc(scale, 1, n), ALU.mult))
            done(dve.tensor_tensor(dst, dst, bc(shift, 1, n), ALU.add))


def project_in(nc, A, bank, T, hT, ring):
    nb = len(ring)
    names = [f"w_in{i}" for i in range(nb)]
    tiles = (SHIFT + FN) // P
    with stage(nc, *names, "mu_in", "mu_ready", "lat", "ctx", "padded", "kept", "dve_step", "padded_used", "shift_done") as sems:
        block, w_in = sems[0], sems[1:1 + nb]
        mu_in, mu_ready, lat, ctx, padded, kept, dve_step, padded_used, shift_done = sems[1 + nb:]
        w = A["w_in"][0].rearrange("(k p) n -> p k n", p=P)
        nshift = SHIFT // P

        @block.sync
        def _(sp):
            sp.dma_start(T["mu"][:, 0, :], A["mu_shift"][0].rearrange("(j p) -> p j", p=P)).then_inc(mu_in, 16)
            for n in range(tiles // 2):
                if n >= nb:
                    sp.wait_ge(lat, 2 * (n - nb) + 2)
                    if 2 * (n - nb) + 2 <= nshift:
                        sp.wait_ge(ctx, 2 * (n - nb) + 2)
                sp.dma_start(ring[n % nb][:, :, 0:256], w[:, :, n * 256:(n + 1) * 256]).then_inc(w_in[n % nb], 16)

        @block.tensor
        def _(pe):
            for j in range(tiles):
                if j % 2 == 0:
                    pe.wait_ge(w_in[j // 2 % nb], 16 * (j // 2 // nb + 1))
                if j >= 2:
                    pe.wait_ge(kept, j - 1)
                at = (j % 2) * P
                for k in range(KD):
                    last = pe.matmul(bank[2 * (j % 2)][:, :], ring[j // 2 % nb][:, k, at:at + P], hT[:, k, 0:SEQ],
                                     start=(k == 0), stop=(k == KD - 1))
                last.then_inc(lat, 1)
                if j < nshift:
                    for k in range(KD):
                        last = pe.matmul(bank[2 * (j % 2) + 1][:, 0:CTX], ring[j // 2 % nb][:, k, at:at + P],
                                         hT[:, k, SEQ:ALLT], start=(k == 0), stop=(k == KD - 1))
                    last.then_inc(ctx, 1)

        @block.scalar
        def _(act):
            act.wait_ge(mu_ready, 1)
            for j in range(tiles):
                g, c = T["padg"][j % 2], T["padc"][j % 2]
                act.wait_ge(lat, j + 1)
                src = bank[2 * (j % 2)][:, :]
                if j >= nshift:
                    act.activation(T["fT"][:, j - nshift, :], src, ACT.Copy).then_inc(kept, 1)
                    continue
                act.wait_ge(ctx, j + 1)
                if j >= 2:
                    act.wait_ge(padded_used, j - 1)
                act.activation(g[:, 1:1 + GRID_H, 1:1 + GRID_W], src.rearrange("p (a b) -> p a b", b=GRID_W), ACT.Copy)
                act.activation(c[:, 1:1 + CTX], bank[2 * (j % 2) + 1][:, 0:CTX], ACT.Copy).then_inc(padded, 1)
                act.activation(T["mT"][:, j, 0:SEQ], src, ACT.Copy, scale=T["mu"][:, 1, j:j + 1])
                act.activation(T["mT"][:, j, SEQ:ALLT], bank[2 * (j % 2) + 1][:, 0:CTX], ACT.Copy,
                               scale=T["mu"][:, 1, j:j + 1]).then_inc(kept, 1)

        @block.vector
        def _(dve):
            done = Chain(dve, dve_step)
            for i in range(2):
                done(dve.memset(T["padg"][i][:, :, :], 0.0))
                done(dve.memset(T["padc"][i][:, :], 0.0))
            dve.wait_ge(mu_in, 16)
            done(dve.tensor_scalar(T["mu"][:, 2, :], T["mu"][:, 0, :], 0.25, None, ALU.mult))
            done(dve.tensor_scalar(T["mu"][:, 3, :], T["mu"][:, 0, :], 0.5, None, ALU.mult))
            dve.tensor_scalar(T["mu"][:, 1, :], T["mu"][:, 0, :], -1.0, 1.0, ALU.mult, ALU.add).then_inc(mu_ready, 1)
            for j in range(nshift):
                g, c = T["padg"][j % 2], T["padc"][j % 2]
                nb1 = T["nbr"][:, 0:SEQ].rearrange("p (a b) -> p a b", b=GRID_W)
                nb2 = T["nbr"][:, SEQ:2 * SEQ].rearrange("p (a b) -> p a b", b=GRID_W)
                nc1 = T["nbr"][:, 2 * SEQ:2 * SEQ + CTX]
                dve.wait_ge(padded, j + 1)
                dve.tensor_tensor(nc1, c[:, 0:CTX], c[:, 2:2 + CTX], ALU.add)
                dve.tensor_tensor(nb1, g[:, 0:GRID_H, 1:1 + GRID_W], g[:, 2:2 + GRID_H, 1:1 + GRID_W], ALU.add)
                done(dve.tensor_tensor(nb2, g[:, 1:1 + GRID_H, 0:GRID_W], g[:, 1:1 + GRID_H, 2:2 + GRID_W], ALU.add))
                dve.tensor_tensor(nb1, nb1, nb2, ALU.add).then_inc(padded_used, 1)
                dve.wait_ge(kept, j + 1)
                dve.wait_ge(padded_used, j + 1)
                dve.scalar_tensor_tensor(out=T["mT"][:, j, SEQ:ALLT], in0=nc1, scalar=T["mu"][:, 3, j:j + 1],
                                         in1=T["mT"][:, j, SEQ:ALLT], op0=ALU.mult, op1=ALU.add)
                done(dve.scalar_tensor_tensor(out=T["mT"][:, j, 0:SEQ], in0=T["nbr"][:, 0:SEQ], scalar=T["mu"][:, 2, j:j + 1],
                                              in1=T["mT"][:, j, 0:SEQ], op0=ALU.mult, op1=ALU.add))


def rwkv_params(nc, A, T):
    with stage(nc, "par_in", "squashed") as (block, par_in, squashed):
        @block.sync
        def _(sp):
            n = 0
            for i, name in enumerate(("w0", "a0", "r_k")):
                for d in range(2):
                    v = A[name][0, d] if name != "r_k" else A[name][0, d].rearrange("h n -> (h n)")
                    sp.dma_start(T["par"][:, :, 2 * i + d], v.rearrange("(c p) -> p c", p=P)).then_inc(par_in, 16)
                    n += 1
            for i, name in enumerate(("k_k", "k_a")):
                sp.dma_start(T["par"][:, :, 6 + i], A[name][0].rearrange("(c p) -> p c", p=P)).then_inc(par_in, 16)
                n += 1
            sp.dma_start(T["w2"][:, :], A["w2_decay"][0].rearrange("d r c -> (d r) c")).then_inc(par_in, 16)
            sp.dma_start(T["a2"][:, :], A["a2_iclr"][0].rearrange("d r c -> (d r) c")).then_inc(par_in, 16)
            sp.dma_start(T["g2"][:, :, :], A["g2_gate"][0].rearrange("d r c -> r d c")).then_inc(par_in, 16)
            sp.dma_start(T["gng"][:, :], A["gn_g"][0].partition_broadcast(P)).then_inc(par_in, 16)
            sp.dma_start(T["gnb"][:, :], A["gn_b"][0].partition_broadcast(P)).then_inc(par_in, 16)
            n += 5
            sp.wait_ge(par_in, 16 * n)

        @block.scalar
        def _(act):
            act.activation(T["mT"][:, 12, :], T["mT"][:, 12, :], ACT.Tanh).then_inc(squashed, 1)
            act.activation(T["mT"][:, 14:16, 0:SEQ], T["mT"][:, 14:16, 0:SEQ], ACT.Sigmoid).then_inc(squashed, 1)
            act.wait_ge(squashed, 2)


def rwkv_prepare(nc, ps, T, W, c):
    S = T["s"]
    r, k = T["mT"][:, c, :], T["mT"][:, c + 4, :]
    par = W["par"]
    with stage(nc, "cur", "low", "sig", "sq_in", "sumsq", "capped", "root", "exp_in", "exps", "rk_ready", "rk_sum",
               "dve_step", "act_step") as (
            block, cur, low, sig, sq_in, sumsq, capped, root, exp_in, exps, rk_ready, rk_sum, dve_step, act_step):
        @block.gpsimd
        def _(pool):
            pool.tensor_copy(W["w2"][:, :], T["w2"][:, bass.ts(c, P)]).then_inc(cur, 1)
            pool.tensor_copy(W["a2"][:, :], T["a2"][:, bass.ts(c, P)]).then_inc(cur, 1)
            pool.tensor_copy(par[:, :], T["par"][:, c, :]).then_inc(cur, 1)
            pool.tensor_copy(W["v"][:, :], T["mT"][:, c + 8, :]).then_inc(cur, 1)
            pool.wait_ge(cur, 4)

        @block.tensor
        def _(pe):
            pe.wait_ge(cur, 2)
            for d in range(2):
                lo, hi = HS * d, HS * d + HS
                for i, (wt, row) in enumerate(((W["w2"], 12), (W["a2"], 13))):
                    b = 4 * d + 2 * i
                    pe.matmul(ps[:, b, :], wt[lo:hi, :], T["mT"][lo:hi, row, 0:SEQ], start=True, stop=True)
                    pe.matmul(ps[:, b + 1, 0:CTX], wt[lo:hi, :], T["mT"][lo:hi, row, SEQ:ALLT],
                              start=True, stop=True).then_inc(low, 1)
            pe.wait_ge(sq_in, 1)
            pe.wait_ge(sig, 1)
            pe.matmul(ps[:, 0, :], S("headones"), W["t0"][:, 0:SEQ], start=True, stop=True)
            pe.matmul(ps[:, 1, 0:CTX], S("headones"), W["t0"][:, SEQ:ALLT], start=True, stop=True).then_inc(sumsq, 1)
            pe.wait_ge(sig, 2)
            sel = S("headones").rearrange("p (h n) -> p h n", h=2)[:, :, 0]
            for d in range(2):
                pe.wait_ge(rk_ready, d + 1)
                for tt in range(TT):
                    at = (tt * 2 + d) * 2
                    last = pe.matmul(ps[:, 2, at:at + 2], W["rk"][:, d, tt * P:(tt + 1) * P], sel, start=True, stop=True)
            last.then_inc(rk_sum, 1)

        def wide(b):
            return ps[:, b:b + 2, :].rearrange("p a b -> p (a b)")[:, 0:ALLT]

        @block.scalar
        def _(act):
            act.wait_ge(cur, 3)
            for d in range(2):
                act.wait_ge(low, 2 * d + 1)
                act.activation(W["lw"][:, d, :], wide(4 * d), ACT.Sigmoid, bias=par[:, d:d + 1]).then_inc(sig, 1)
                act.wait_ge(low, 2 * d + 2)
                act.activation(W["a"][:, d, :], wide(4 * d + 2), ACT.Sigmoid, bias=par[:, 2 + d:3 + d]).then_inc(sig, 1)
            act.wait_ge(capped, 1)
            act.activation(W["t0"][:, :], W["t0"][:, :], ACT.Sqrt).then_inc(root, 1)
            act.wait_ge(exp_in, 1)
            act.activation(W["pc"][:, :, :], W["tot"][:, :, :], ACT.Exp)
            for d in range(2):
                act.activation(W["e1"][:, d, :], W["e1"][:, d, :], ACT.Exp)
                act.activation(W["lw"][:, d, :], W["ci"][:, d, :], ACT.Exp, scale=-1.0).then_inc(act_step, 1)
                act.wait_ge(act_step, d + 1)
                act.activation(W["ci"][:, d, :], W["ci"][:, d, :], ACT.Exp).then_inc(exps, 1)
            act.wait_ge(rk_sum, 1)
            act.activation(W["bon"][:, :], ps[:, 2, 0:16], ACT.Copy).then_inc(act_step, 1)
            act.wait_ge(act_step, 3)

        @block.vector
        def _(dve):
            done = Chain(dve, dve_step)
            dve.wait_ge(cur, 3)
            done(dve.tensor_scalar(W["kk"][:, :], k, par[:, 6:7], None, ALU.mult))
            dve.tensor_tensor(W["t0"][:, :], W["kk"][:, :], W["kk"][:, :], ALU.mult).then_inc(sq_in, 1)
            for d in range(2):
                dve.wait_ge(sig, 2 * d + 1)
                lw, ci = W["lw"][:, d, :], W["ci"][:, d, :]
                tot = W["tot"][:, d, :]
                done(dve.tensor_scalar(lw, lw, DECAY, None, ALU.mult))
                done(dve.tensor_tensor_scan(ci, S("restart"), lw, 0.0, ALU.mult, ALU.add))
                done(dve.tensor_copy(tot, ci.rearrange("p (n s) -> p n s", s=CH)[:, :, CH - 1]))
                if d == 1:
                    done(dve.tensor_tensor(ci, lw, ci, ALU.subtract))
                    v3 = ci.rearrange("p (n s) -> p n s", s=CH)
                    done(dve.tensor_tensor(v3, v3, bc(tot, 2, CH), ALU.add))
                done(dve.tensor_tensor(W["e1"][:, d, :], ci, lw, ALU.subtract))
            dve.wait_ge(sumsq, 1)
            dve.tensor_scalar(W["t0"][:, :], wide(0), 1e-24, None, ALU.max).then_inc(capped, 1)
            dve.wait_ge(root, 1)
            dve.reciprocal(W["t0"][:, :], W["t0"][:, :]).then_inc(exp_in, 1)
            dve.wait_ge(exp_in, 1)
            done(dve.tensor_tensor(W["kk"][:, :], W["kk"][:, :], W["t0"][:, :], ALU.mult))
            dve.wait_ge(sig, 4)
            for d in range(2):
                a, kd = W["a"][:, d, :], W["kd"][:, d, :]
                done(dve.tensor_scalar(kd, a, -1.0, par[:, 7:8], ALU.add, ALU.mult))
                done(dve.scalar_tensor_tensor(out=kd, in0=kd, scalar=1.0, in1=k, op0=ALU.add, op1=ALU.mult))
                dve.scalar_tensor_tensor(out=W["rk"][:, d, :], in0=kd[:, 0:SEQ], scalar=par[:, 4 + d:5 + d],
                                         in1=r[:, 0:SEQ], op0=ALU.mult, op1=ALU.mult).then_inc(rk_ready, 1)
                done(dve.tensor_tensor(a, a, W["kk"][:, :], ALU.mult))
            for d in range(2):
                dve.wait_ge(exps, d + 1)
                ar = W["ar"][:, d, :, :, :]

                def tiles(x):
                    return x.rearrange("p (t s) -> p t s", s=P)

                done(dve.scalar_tensor_tensor(out=ar[:, :, 0, :], in0=tiles(W["kk"][:, :]), scalar=-1.0,
                                              in1=tiles(W["e1"][:, d, :]), op0=ALU.mult, op1=ALU.mult))
                done(dve.tensor_tensor(ar[:, :, 1, :], tiles(r), tiles(W["ci"][:, d, :]), ALU.mult))
                done(dve.tensor_tensor(W["bt"][:, d, :], W["a"][:, d, :], W["lw"][:, d, :], ALU.mult))
                done(dve.tensor_tensor(W["kt"][:, d, :], W["kd"][:, d, :], W["lw"][:, d, :], ALU.mult))


def rwkv_chunks(nc, ps, T, W):
    S = T["s"]
    levels = (2, 4, 8, 16, 32)
    names = []
    for s in range(2):
        names += [f"scores{s}", f"masked{s}", f"near{s}", f"start{s}", f"y_prod{s}", f"y_out{s}", f"x_prod{s}", f"x_out{s}",
                  f"akv{s}", f"akv_out{s}", f"wu{s}", f"wu_out{s}", f"last{s}", f"last_v{s}", f"last_a{s}"]
    with stage(nc, *names, "dve_step") as sems:
        block, dve_step = sems[0], sems[-1]
        q = [dict(zip(("scores", "masked", "near", "start", "y_prod", "y_out", "x_prod", "x_out", "akv", "akv_out",
                       "wu", "wu_out", "last", "last_v", "last_a"), sems[1 + 15 * s:16 + 15 * s])) for s in range(2)]
        nq, nl = TA // 2, len(levels)

        def units(g):
            return [(u, 2 * g + u // 2, u % 2) for u in range(4)]

        @block.tensor
        def _(pe):
            for g in range(nq):
                for d in range(2):
                    if g:
                        pe.wait_ge(q[d]["last_v"], g)
                        pe.wait_ge(q[d]["last_a"], min(g, TT // 2))
                    for u, tt, h in units(g):
                        lo, hi = HS * h, HS * h + HS
                        tk = slice(tt * P, (tt + 1) * P)
                        both = W["ar"][lo:hi, d, tt, :, :].rearrange("p a b -> p (a b)")
                        pe.matmul(ps[:, 4 * d + u, 0:256], W["kt"][lo:hi, d, tk], both, start=True, stop=True)
                        last = pe.matmul(ps[:, 4 * d + u, 256:512], W["bt"][lo:hi, d, tk], both, start=True, stop=True)
                    last.then_inc(q[d]["scores"], 1)
                for d in range(2):
                    pe.wait_ge(q[d]["masked"], g + 1)
                    for u, tt, h in units(g):
                        lo, hi = HS * h, HS * h + HS
                        last = pe.matmul(ps[:, 4 * d + h, u // 2 * P:(u // 2 + 1) * P], W["ar"][lo:hi, d, tt, 0, :],
                                         W["bt"][lo:hi, d, tt * P:(tt + 1) * P], start=True, stop=True)
                    last.then_inc(q[d]["near"], 1)
                for l in range(nl):
                    for d in range(2):
                        pe.wait_ge(q[d]["start"], g + 1)
                        if g * nl + l:
                            pe.wait_ge(q[d]["x_out"], g * nl + l)
                        for u in range(4):
                            last = pe.matmul(ps[:, 4 * d + 1, u * P:(u + 1) * P], W["m"][:, d, u, 256:384],
                                             W["x"][:, d, u, :], start=True, stop=True)
                        last.then_inc(q[d]["y_prod"], 1)
                    for d in range(2):
                        pe.wait_ge(q[d]["y_out"], g * nl + l + 1)
                        for u in range(4):
                            if l < nl - 1:
                                pe.matmul(ps[:, 4 * d + 2, u * P:(u + 1) * P], W["xt"][:, d, u, :], W["y"][:, d, u, :],
                                          start=True, stop=True)
                            last = pe.matmul(ps[:, 4 * d + 3, u * P:(u + 1) * P], W["y"][:, d, u, :], W["xt"][:, d, u, :],
                                             start=True, stop=True)
                        last.then_inc(q[d]["x_prod"], 1)
                for d in range(2):
                    for u, tt, h in units(g):
                        last = pe.matmul(ps[:, 4 * d, u * HS:(u + 1) * HS], W["m"][:, d, u, 0:128],
                                         W["vrow"][:, tt, h * HS:(h + 1) * HS], start=True, stop=True)
                    last.then_inc(q[d]["akv"], 1)
                for d in range(2):
                    pe.wait_ge(q[d]["x_out"], (g + 1) * nl)
                    pe.wait_ge(q[d]["akv_out"], g + 1)
                    for u in range(4):
                        last = pe.matmul(ps[:, 4 * d + 1, u * P:(u + 1) * P], W["xt"][:, d, u, :], W["rhs"][:, d, u, :],
                                         start=True, stop=True)
                    last.then_inc(q[d]["wu"], 1)
                for d in range(2):
                    pe.wait_ge(q[d]["wu_out"], g + 1)
                    for u, tt, h in units(g):
                        lo, hi = HS * h, HS * h + HS
                        w, u2 = W["wu"][:, d, u, 0:HS], W["wu"][:, d, u, HS:P]
                        vr = W["vrow"][:, tt, lo:hi]
                        if 2 * g < TT:
                            pe.matmul(ps[lo:hi, 4 * d + 2, (u // 2) * P:(u // 2 + 1) * P], w, W["m"][:, d, u, 384:512],
                                      start=True, stop=True)
                            pe.matmul(ps[:, 4 * d + 3, u * HS:(u + 1) * HS], W["m"][:, d, u, 384:512], u2, start=True, stop=False)
                            pe.matmul(ps[:, 4 * d + 3, u * HS:(u + 1) * HS], W["m"][:, d, u, 128:256], vr, start=False, stop=True)
                        for c2 in range(2):
                            a, b = CH * c2, CH * c2 + CH
                            at = (u // 2) * HS
                            bk = 4 * d + c2
                            br, kr = W["brow"][a:b, d, tt, lo:hi], W["krow"][a:b, d, tt, lo:hi]
                            pe.matmul(ps[lo:hi, bk, at:at + HS], w[a:b, :], br, start=True, stop=True)
                            pe.matmul(ps[lo:hi, bk, P + at:P + at + HS], br, u2[a:b, :], start=True, stop=False)
                            last = pe.matmul(ps[lo:hi, bk, P + at:P + at + HS], kr, vr[a:b, :], start=False, stop=True)
                    last.then_inc(q[d]["last"], 1)

        @block.scalar
        def _(act):
            for g in range(nq):
                for l in range(nl):
                    for d in range(2):
                        act.wait_ge(q[d]["y_prod"], g * nl + l + 1)
                        act.activation(W["y"][:, d, :, :], ps[:, 4 * d + 1, :].rearrange("p (u s) -> p u s", u=4),
                                       ACT.Copy).then_inc(q[d]["y_out"], 1)
                for d in range(2):
                    act.wait_ge(q[d]["akv"], g + 1)
                    act.activation(W["rhs"][:, d, :, 0:HS],
                                   W["arow"][:, d, 2 * g:2 * g + 2, :].rearrange("p t (h s) -> p (t h) s", h=2), ACT.Copy)
                    act.activation(W["rhs"][:, d, :, HS:P], ps[:, 4 * d, 0:256].rearrange("p (u s) -> p u s", u=4),
                                   ACT.Copy).then_inc(q[d]["akv_out"], 1)
                for d in range(2):
                    act.wait_ge(q[d]["wu"], g + 1)
                    act.activation(W["wu"][:, d, :, :], ps[:, 4 * d + 1, :].rearrange("p (u s) -> p u s", u=4),
                                   ACT.Copy).then_inc(q[d]["wu_out"], 1)
                for d in range(2):
                    act.wait_ge(q[d]["last"], g + 1)
                    if 2 * g < TT:
                        act.activation(W["yr"][:, 2 * g:2 * g + 2, d, :],
                                       ps[:, 4 * d + 3, 0:256].rearrange("p (t s) -> p t s", t=2), ACT.Copy).then_inc(q[d]["last_a"], 1)

        @block.vector
        def _(dve):
            done = Chain(dve, dve_step)
            for g in range(nq):
                for d in range(2):
                    lowm, upm = ("low", "up") if d == 0 else ("up", "low")
                    dve.wait_ge(q[d]["scores"], g + 1)
                    dve.tensor_tensor(W["m"][:, d, :, :], ps[:, 4 * d:4 * d + 4, :], bc(S(f"dir{d}"), 1, 4),
                                      ALU.mult).then_inc(q[d]["masked"], 1)
                    done(dve.tensor_copy(W["x"][:, d, :, :], bc(S("ident"), 1, 4)))
                    done(dve.tensor_copy(W["xt"][:, d, :, :], bc(S("ident"), 1, 4)))
                    dve.wait_ge(q[d]["masked"], g + 1)
                    done(dve.copy_predicated(W["xt"][:, d, :, :], bc(S(f"{upm}1").bitcast(U32), 1, 4), W["m"][:, d, :, 256:384]))
                for d in range(2):
                    lowm, upm = ("low", "up") if d == 0 else ("up", "low")
                    dve.wait_ge(q[d]["near"], g + 1)
                    for h in range(2):
                        last = dve.copy_predicated(W["x"][:, d, h:4:2, :], bc(S(f"{lowm}1").bitcast(U32), 1, 2),
                                                   ps[:, 4 * d + h, 0:256].rearrange("p (u s) -> p u s", u=2))
                    last.then_inc(q[d]["start"], 1)
                for l, b in enumerate(levels):
                    for d in range(2):
                        lowm, upm = ("low", "up") if d == 0 else ("up", "low")
                        dve.wait_ge(q[d]["x_prod"], g * nl + l + 1)
                        if l < nl - 1:
                            done(dve.copy_predicated(W["x"][:, d, :, :], bc(S(f"{lowm}{b}").bitcast(U32), 1, 4),
                                                     ps[:, 4 * d + 2, :].rearrange("p (u s) -> p u s", u=4)))
                        dve.copy_predicated(W["xt"][:, d, :, :], bc(S(f"{upm}{b}").bitcast(U32), 1, 4),
                                            ps[:, 4 * d + 3, :].rearrange("p (u s) -> p u s", u=4)).then_inc(q[d]["x_out"], 1)
                for d in range(2):
                    dve.wait_ge(q[d]["last"], g + 1)
                    if 2 * g < TT:
                        done(dve.tensor_tensor(W["qt"][:, d, 2 * g:2 * g + 2, :],
                                               ps[:, 4 * d + 2, 0:256].rearrange("p (t s) -> p t s", t=2),
                                               W["ar"][:, d, 2 * g:2 * g + 2, 1, :], ALU.add))
                    for c2 in range(2):
                        last = dve.tensor_tensor(W["gt"][:, d, 4 * g + c2:4 * g + 4:2, :],
                                                 ps[:, 4 * d + c2, 0:P].rearrange("p (n s) -> p n s", n=2),
                                                 bc(S("eye2"), 1, 2), ALU.add)
                        mine = slice(4 * g + c2, 4 * g + 4, 2)
                        last = dve.tensor_tensor(W["hp"][:, d, mine, :], ps[:, 4 * d + c2, P:2 * P].rearrange("p (n s) -> p n s", n=2),
                                                 bc(W["pc"][:, d, mine], 2, HS), ALU.mult)
                    last.then_inc(q[d]["last_v"], 1)


def rwkv_scan(nc, ps, T, W):
    order = [[LATCH + i for i in range(NCH - LATCH)] + list(range(LATCH)),
             [NCH - 1 - i for i in range(NCH - LATCH)] + [LATCH - 1 - i for i in range(LATCH)]]
    first = NCH - LATCH
    with stage(nc, "zeroed", "moved", "state", "seen", "added") as (block, zeroed, moved, state, seen, added):
        @block.tensor
        def _(pe):
            pe.wait_ge(zeroed, 1)
            for n in range(NCH):
                if n:
                    pe.wait_ge(state, n)
                b = n % 2
                for d in range(2):
                    for h in range(2):
                        lo, hi = HS * h, HS * h + HS
                        last = pe.matmul(ps[lo:hi, b, d * HS:(d + 1) * HS], W["gt"][lo:hi, d, order[d][n], :],
                                         W["st"][lo:hi, b, d, :], start=True, stop=True)
                last.then_inc(moved, 1)
                if n >= first:
                    if n >= first + 2:
                        pe.wait_ge(added, n - first - 1)
                    for d in range(2):
                        ch = order[d][n]
                        tk = CH * (ch % 2)
                        for h in range(2):
                            lo, hi = HS * h, HS * h + HS
                            last = pe.matmul(ps[tk:tk + CH, 2 + 2 * b + h, d * HS:(d + 1) * HS],
                                             W["qt"][lo:hi, d, ch // 2, tk:tk + CH], W["st"][lo:hi, b, d, :], start=True, stop=True)
                    last.then_inc(seen, 1)

        @block.vector
        def _(dve):
            dve.memset(W["st"][:, 0, :, :], 0.0).then_inc(zeroed, 1)
            for n in range(NCH):
                dve.wait_ge(moved, n + 1)
                if n >= first + 1:
                    dve.wait_ge(seen, n - first)
                for d in range(2):
                    ch = order[d][n]
                    last = dve.scalar_tensor_tensor(out=W["st"][:, (n + 1) % 2, d, :], in0=ps[:, n % 2, d * HS:(d + 1) * HS],
                                                    scalar=W["pc"][:, d, ch:ch + 1], in1=W["hp"][:, d, ch, :],
                                                    op0=ALU.mult, op1=ALU.add)
                last.then_inc(state, 1)
                if n >= first:
                    dve.wait_ge(seen, n - first + 1)
                    for d in range(2):
                        ch = order[d][n]
                        tk = CH * (ch % 2)
                        y = W["yr"][tk:tk + CH, ch // 2, d, :].rearrange("p (h s) -> p h s", h=2)
                        at = 2 + 2 * (n % 2)
                        last = dve.tensor_tensor(y, ps[tk:tk + CH, at:at + 2, d * HS:(d + 1) * HS], y, ALU.add)
                    last.then_inc(added, 1)


def rwkv_output(nc, ps, T, W, c):
    S = T["s"]
    with stage(nc, "gates", "var_in", "root", "rw", "turned", "dve_step", "act_step") as (
            block, gates, var_in, root, rw, turned, dve_step, act_step):
        y = W["yr"][:, :, :, :].rearrange("p t d (h s) -> p (t d h) s", h=2)
        sq = W["big"][:, :].rearrange("p (g s) -> p g s", s=HS)

        @block.tensor
        def _(pe):
            for d in range(2):
                for tt in range(TT):
                    last = pe.matmul(ps[:, tt // 2, (tt % 2 * 2 + d) * P:(tt % 2 * 2 + d + 1) * P],
                                     T["mT"][:, 14 + d, tt * P:(tt + 1) * P], T["g2"][:, d, bass.ts(c, P)], start=True, stop=True)
            last.then_inc(gates, 1)
            pe.wait_ge(rw, 1)
            for tt in range(TT):
                last = pe.transpose(ps[:, 2, tt * P:(tt + 1) * P], W["rw"][:, tt, :], S("ident"))
            last.then_inc(turned, 1)

        @block.scalar
        def _(act):
            act.wait_ge(var_in, 1)
            act.activation(W["var"][:, :], W["var"][:, :], ACT.Sqrt).then_inc(root, 1)
            act.wait_ge(turned, 1)
            act.activation(T["mixT"][:, c, :], ps[:, 2, :], ACT.Copy).then_inc(act_step, 1)
            act.wait_ge(act_step, 1)

        @block.vector
        def _(dve):
            done = Chain(dve, dve_step)
            done(dve.tensor_reduce(W["mean"][:, :], y, AX_X, ALU.add))
            done(dve.tensor_scalar(W["mean"][:, :], W["mean"][:, :], 1.0 / HS, None, ALU.mult))
            done(dve.tensor_tensor(y, y, bc(W["mean"][:, :], 2, HS), ALU.subtract))
            done(dve.tensor_tensor(sq, y, y, ALU.mult))
            done(dve.tensor_reduce(W["var"][:, :], sq, AX_X, ALU.add))
            dve.tensor_scalar(W["var"][:, :], W["var"][:, :], 1.0 / HS, GN_EPS, ALU.mult, ALU.add).then_inc(var_in, 1)
            dve.wait_ge(root, 1)
            done(dve.reciprocal(W["var"][:, :], W["var"][:, :]))
            done(dve.tensor_tensor(y, y, bc(W["var"][:, :], 2, HS), ALU.mult))
            y3 = W["yr"][:, :, :, :].rearrange("p t d s -> p (t d) s")
            done(dve.tensor_tensor(y3, y3, bc(T["gng"][:, bass.ts(c, P)], 1, 8), ALU.mult))
            done(dve.tensor_tensor(y3, y3, bc(T["gnb"][:, bass.ts(c, P)], 1, 8), ALU.add))
            big = W["big"][:, :].rearrange("p (t d h s) -> p t d h s", d=2, h=2, s=HS)
            bon = W["bon"][:, :].rearrange("p (t d h) -> p t d h", d=2, h=2)
            for d in range(2):
                done(dve.tensor_tensor(big[:, :, d, :, :], W["vrow"][:, 0:TT, :].rearrange("p t (h s) -> p t h s", h=2),
                                       bc(bon[:, :, d, :], 3, HS), ALU.mult))
            done(dve.tensor_tensor(y3, y3, W["big"][:, :].rearrange("p (g s) -> p g s", s=P), ALU.add))
            dve.wait_ge(gates, 1)
            done(dve.tensor_tensor(y3, y3, ps[:, 0:2, :].rearrange("p a (g s) -> p (a g) s", s=P), ALU.mult))
            dve.tensor_tensor(W["rw"][:, :, :], W["yr"][:, :, 0, :], W["yr"][:, :, 1, :], ALU.add).then_inc(rw, 1)


def fourier(nc, A, ps, T, B):
    F = T["b"]
    with stage(nc, "tab_in", "zeroed", "wf_in", "chan", "chan_out", "pos", "pos_out", "maps", "maps_out") as (
            block, tab_in, zeroed, wf_in, chan, chan_out, pos, pos_out, maps, maps_out):
        @block.sync
        def _(sp):
            sp.dma_start(B["tab"][:, :], A["big"]).then_inc(tab_in, 16)
            sp.dma_start(B["bf"][:, :], A["b_fno"][0].rearrange("(j g) e -> (g e) j", g=2)).then_inc(tab_in, 16)
            sp.wait_ge(zeroed, 1)
            wf = A["w_fno"][0].rearrange("(j g) c e -> g c j e", g=2)
            for g in range(2):
                sp.dma_start(B["wf"][g * HS:(g + 1) * HS, :, g * HS:(g + 1) * HS], wf[g]).then_inc(wf_in, 16)

        @block.vector
        def _(dve):
            dve.memset(B["wf"][:, :, :], 0.0).then_inc(zeroed, 1)
            for j in range(4):
                dve.wait_ge(maps, j + 1)
                dve.tensor_scalar(T["mixT"][:, 4 + j, :], ps[:, 6 + j % 2, :], B["bf"][:, j:j + 1], None, ALU.add).then_inc(maps_out, 1)

        @block.tensor
        def _(pe):
            pe.wait_ge(tab_in, 32)
            for i in range(2 * TT):
                tt, part = i // 2, i % 2
                if i >= 2:
                    pe.wait_ge(chan_out, i - 1)
                for j in range(4):
                    last = pe.matmul(ps[:, i % 2, j * P:(j + 1) * P], T["fT"][:, j, tt * P:(tt + 1) * P],
                                     F("chs" if part else "chc"), start=True, stop=True)
                last.then_inc(chan, 1)
            pe.wait_ge(chan_out, 2 * TT)
            for j in range(4):
                if j >= 2:
                    pe.wait_ge(pos_out, j - 1)
                for part in range(2):
                    tab = F("dfts" if part else "dftc").rearrange("p (k t) -> p k t", k=TT)
                    for k in range(TT):
                        last = pe.matmul(ps[:, 4 + j % 2, :], B["f12"][:, part, k, j * P:(j + 1) * P], tab[:, k, :],
                                         start=(part + k == 0), stop=(part == 1 and k == TT - 1))
                last.then_inc(pos, 1)
            pe.wait_ge(wf_in, 32)
            for j in range(4):
                pe.wait_ge(pos_out, j + 1)
                if j >= 2:
                    pe.wait_ge(maps_out, j - 1)
                pe.matmul(ps[:, 6 + j % 2, :], B["wf"][:, j, :], B["spec"][:, j, :], start=True, stop=True).then_inc(maps, 1)

        @block.scalar
        def _(act):
            for i in range(2 * TT):
                act.wait_ge(chan, i + 1)
                act.activation(B["f12"][:, i % 2, i // 2, :], ps[:, i % 2, :], ACT.Copy).then_inc(chan_out, 1)
            for j in range(4):
                act.wait_ge(pos, j + 1)
                act.activation(B["spec"][:, j, :], ps[:, 4 + j % 2, :], ACT.Copy).then_inc(pos_out, 1)


def residual_stage(nc, x, y, gate, n):
    with stage(nc, "dve_step") as (block, dve_step):
        @block.vector
        def _(dve):
            done = Chain(dve, dve_step)
            done(dve.tensor_tensor(y, y, bc(gate, 1, n), ALU.mult))
            done(dve.scalar_tensor_tensor(out=x, in0=x, scalar=ALPHA, in1=y, op0=ALU.mult, op1=ALU.add))


def router(nc, A, ps, T, R):
    S = T["s"]
    with stage(nc, "in_", "logit", "logit_out", "top", "e4", "sel", "rank", "count", "gt_turned", "gt_out", "b2_prod", "dve_step") as (
            block, in_, logit, logit_out, top, e4, sel, rank, count, gt_turned, gt_out, b2_prod, dve_step):
        @block.sync
        def _(sp):
            sp.dma_start(R["wr"][:, :, :], A["w_router"][0].rearrange("(k p) e -> p k e", p=P)).then_inc(in_, 16)
            sp.dma_start(R["br"][:, :], A["b_router"]).then_inc(in_, 16)
            sp.dma_start(R["b2"][:, :], A["b2"][0]).then_inc(in_, 16)

        @block.tensor
        def _(pe):
            pe.wait_ge(in_, 48)
            for tt in range(TT):
                o = ps[:, 0, tt * E:(tt + 1) * E]
                for k in range(KD):
                    pe.matmul(o, T["hT"][:, k, tt * P:(tt + 1) * P], R["wr"][:, k, :], start=(k == 0), stop=False)
                last = pe.matmul(o, T["onerow"][:, :], R["br"][:, :], start=False, stop=True)
            last.then_inc(logit, 1)
            pe.wait_ge(sel, 1)
            for tt in range(TT):
                o = ps[:, 1, tt * E:(tt + 1) * E]
                for t2 in range(tt):
                    pe.matmul(o, S("ones"), R["sel"][:, t2, :], start=(t2 == 0), stop=False)
                pe.matmul(o, S("before"), R["sel"][:, tt, :], start=(tt == 0), stop=True)
            for tt in range(TT):
                last = pe.matmul(ps[:, 1, P:P + E], S("ones"), R["sel"][:, tt, :], start=(tt == 0), stop=(tt == TT - 1))
            last.then_inc(rank, 1)
            for tt in range(TT):
                last = pe.transpose(ps[0:E, 2, tt * P:(tt + 1) * P], R["gates"][:, tt, :], S("ident"))
            last.then_inc(gt_turned, 1)
            pe.wait_ge(gt_out, 1)
            for half in range(2):
                if half:
                    pe.wait_ge(b2_prod, 1)
                    pe.wait_ge(gt_out, 2)
                for tt in range(TT):
                    last = pe.matmul(ps[:, 4 + tt, :], R["gT"][:, tt * P:(tt + 1) * P], R["b2"][:, half * 512:(half + 1) * 512],
                                     start=True, stop=True)
                last.then_inc(b2_prod, 1)

        @block.scalar
        def _(act):
            act.wait_ge(logit, 1)
            act.activation(R["lg"][:, :, :], ps[:, 0, 0:TT * E].rearrange("p (t e) -> p t e", e=E), ACT.Copy).then_inc(logit_out, 1)
            act.wait_ge(top, 1)
            act.activation(R["g4"][:, :, :], R["g4"][:, :, :], ACT.Exp).then_inc(e4, 1)
            act.wait_ge(gt_turned, 1)
            act.activation(R["gT"][:, :], ps[0:E, 2, :], ACT.Copy).then_inc(gt_out, 1)
            for half in range(2):
                act.wait_ge(b2_prod, half + 1)
                act.activation(T["f"][:, :, half * 512:(half + 1) * 512], ps[:, 4:8, :], ACT.Copy).then_inc(gt_out, 1)
            act.wait_ge(gt_out, 3)

        @block.vector
        def _(dve):
            done = Chain(dve, dve_step)
            dve.wait_ge(logit_out, 1)
            for tt in range(TT):
                done(dve.max(R["m8"][:, tt, :], R["lg"][:, tt, :]))
                done(dve.max_index(R["i8"][:, tt, :], R["m8"][:, tt, :], R["lg"][:, tt, :]))
            done(dve.tensor_copy(R["i8f"][:, :, :], R["i8"][:, :, :]))
            dve.tensor_tensor(R["g4"][:, :, :], R["m8"][:, :, 0:TOPK], bc(R["m8"][:, :, 0], 2, TOPK), ALU.subtract).then_inc(top, 1)
            dve.wait_ge(e4, 1)
            done(dve.tensor_reduce(R["sum4"][:, :], R["g4"][:, :, :], AX_X, ALU.add))
            done(dve.reciprocal(R["sum4"][:, :], R["sum4"][:, :]))
            done(dve.tensor_tensor(R["g4"][:, :, :], R["g4"][:, :, :], bc(R["sum4"][:, :], 2, TOPK), ALU.mult))
            i32f = S("iota")[:, 0:E]
            for tt in range(TT):
                for k in range(TOPK):
                    ix, gv = R["i8f"][:, tt, k:k + 1], R["g4"][:, tt, k:k + 1]
                    if k == 0:
                        done(dve.tensor_scalar(R["gates"][:, tt, :], i32f, ix, gv, ALU.is_equal, ALU.mult))
                        done(dve.tensor_scalar(R["sel"][:, tt, :], i32f, ix, None, ALU.is_equal))
                    else:
                        done(dve.tensor_scalar(R["tmp"][:, :], i32f, ix, gv, ALU.is_equal, ALU.mult))
                        done(dve.tensor_tensor(R["gates"][:, tt, :], R["gates"][:, tt, :], R["tmp"][:, :], ALU.add))
                        last = dve.scalar_tensor_tensor(out=R["sel"][:, tt, :], in0=i32f, scalar=ix, in1=R["sel"][:, tt, :],
                                                        op0=ALU.is_equal, op1=ALU.add)
                        if (tt, k) == (TT - 1, TOPK - 1):
                            last.then_inc(sel, 1)
                        else:
                            done(last)
            dve.wait_ge(rank, 1)
            rk = ps[:, 1, 0:TT * E].rearrange("p (t e) -> p t e", e=E)
            done(dve.tensor_scalar(R["place"][:, :, :], rk, 1.0, None, ALU.add))
            done(dve.tensor_tensor(R["place"][:, :, :], R["place"][:, :, :], R["sel"][:, :, :], ALU.mult))
            done(dve.tensor_scalar(R["place"][:, :, :], R["place"][:, :, :], -1.0, None, ALU.add))
            cnt = ps[:, 1, P:P + E]
            done(dve.tensor_scalar(R["nblk"][:, :], cnt, float(P), 1.0, ALU.is_gt, ALU.add))
            for b in (2, 3):
                done(dve.tensor_scalar(R["tmp"][:, :], cnt, float(b * P), None, ALU.is_gt))
                done(dve.tensor_tensor(R["nblk"][:, :], R["nblk"][:, :], R["tmp"][:, :], ALU.add))
            done(dve.tensor_copy(R["nblki"][:, :], R["nblk"][:, :]))


def experts(nc, A, ps, T, R, M):
    S = T["s"]
    NS = 12
    NR = len(M["raw"])
    NH = len(M["hi"])
    POOL = M["pool_pieces"]
    nv, npool = NS - len(POOL), len(POOL)
    low_at = {s: (s in POOL, sum((q in POOL) == (s in POOL) for q in range(s))) for s in range(NS)}
    with stage(nc, *[f"raw_in{i}" for i in range(NR)], "hi_done", "lo_v", "lo_p", "used", "perm", "stepped", "cur_p", "picked",
               "gath", "x_hi", "x_done", "pt", "pt_out", "biased", "mixed", "sig", "acted", "at", "at_hi", "at_lo",
               "y_hi", "y_lo", "spread", "added", "cur") as sems:
        block, raw_in = sems[0], sems[1:1 + NR]
        (hi_done, lo_v, lo_p, used, perm, stepped, cur_p, picked, gath, x_hi, x_done, pt, pt_out, biased, mixed, sig, acted,
         at, at_hi, at_lo, y_hi, y_lo, spread, added, cur) = sems[1 + NR:]


        def counter(eng, name):
            r = eng.alloc_register(name)
            eng.reg_mov(r, 0)
            return r, lambda: eng.snap(r, min_val=0, max_val=E * TT)

        def blocks_of(eng, e):
            return eng.value_load(R["nblki"][0:1, bass.ds(e, 1)], min_val=1, max_val=TT)

        def wait_low(eng, w, s, back=0):
            at_, wrap = (s - back, 1) if s >= back else (s - back + NS, 0)
            pool, n = low_at[at_]
            if pool:
                eng.wait_ge(lo_p, (w + wrap) * npool + n + 1)
            else:
                eng.wait_ge(lo_v, (w + wrap) * nv + n + 1)

        @block.sync
        def _(sp):
            r, now = counter(sp, "sp_blocks")
            with sp.Fori(0, E) as e:
                w1 = A["w1"][0, e].rearrange("(k p) n -> p k n", p=P)
                w2 = A["w2"][0, e].rearrange("(k p) n -> p k n", p=P)
                with sp.Fori(0, blocks_of(sp, e)) as _:
                    w = now()
                    for s in range(NS):
                        wait_low(sp, w, s, NR)
                        src, c, half = (w1, s // 2, s % 2) if s < 8 else (w2, s % 2, (s - 8) // 2)
                        sp.dma_start(M["raw"][s % NR][:, :, :], src[:, 4 * half:4 * half + 4, c * 512:(c + 1) * 512])\
                          .then_inc(raw_in[s % NR], 16)
                    sp.reg_add(r, r, 1)

        @block.gpsimd
        def _(pool):
            r, now = counter(pool, "pool_blocks")
            pool.sem_inc(lo_p, npool)
            with pool.Fori(0, E) as e:
                pool.tensor_copy(M["place"][:, :], R["place"][:, :, e]).then_inc(cur_p, 1)
                pool.wait_ge(cur_p, now() + e + 1)
                with pool.Fori(0, blocks_of(pool, e)) as _:
                    w = now()

                    def low(s):
                        pool.wait_ge(hi_done, w * NS + s + 1)
                        pool.wait_ge(used, w * NS + s + 1)
                        pool.tensor_tensor(M["lo"][s % NH][:, :, :], M["raw"][s % NR][:, :, :], M["hi"][s % NH][:, :, :].bitcast(F32),
                                           ALU.subtract).then_inc(lo_p, 1)

                    pool.wait_ge(pt, w + 1)
                    pool.tensor_tensor(M["next"][:, :], M["place"][:, :], S("step"), ALU.subtract).then_inc(stepped, 1)
                    for tt in range(TT):
                        last = pool.tensor_scalar(M["pm"][:, tt, :], S("iota"), M["place"][:, tt:tt + 1], None, ALU.is_equal)
                    last.then_inc(perm, 1)
                    pool.wait_ge(perm, w + 1)
                    pool.wait_ge(stepped, w + 1)
                    pool.tensor_tensor(M["place"][:, :], M["next"][:, :], S("ones")[:, 0:TT], ALU.mult).then_inc(cur_p, 1)
                    pool.wait_ge(cur_p, w + e + 2)
                    pool.wait_ge(used, w * NS + NH)
                    pool.tensor_tensor(M["pick"][:, :], S("eye32")[0:2 * E, bass.ds(e, 1)].to_broadcast([2 * E, P]), S("ones")[0:2 * E, :],
                                       ALU.mult).then_inc(picked, 1)
                    for s in POOL:
                        low(s)
                    pool.reg_add(r, r, 1)

        @block.tensor
        def _(pe):
            r, now = counter(pe, "pe_blocks")
            pe.sem_inc(used, NH)
            pe.sem_inc(pt, 1)
            with pe.Fori(0, E) as e:
                with pe.Fori(0, blocks_of(pe, e)) as _:
                    w = now()

                    def piece(s):
                        wait_low(pe, w, s)
                        hi, lo = M["hi"][s % NH], M["lo"][s % NH]
                        if s < 8:
                            b, half, xh, xl = s // 2, s % 2, M["xh"], M["xl"]
                        else:
                            b, half, xh, xl = 4 + s % 2, (s - 8) // 2, M["ah"], M["al"]
                        if s < 8 and half == 0:
                            pe.matmul(ps[:, b, :], M["pick"][:, :], M["b12"][:, b * 512:(b + 1) * 512], start=True, stop=False)
                        for k in range(4):
                            first = s >= 8 and half == 0 and k == 0
                            pe.matmul(ps[:, b, :], xh[:, 4 * half + k, :], hi[:, k, :], start=first, stop=False)
                            pe.matmul(ps[:, b, :], xh[:, 4 * half + k, :], lo[:, k, :], start=False, stop=False)
                            mm = pe.matmul(ps[:, b, :], xl[:, 4 * half + k, :], hi[:, k, :], start=False, stop=(half == 1 and k == 3))
                        mm.then_inc(used, 1)

                    def turn_act(p):
                        pe.wait_ge(acted, 4 * w + p + 1)
                        if p >= 2:
                            pe.wait_ge(at_lo, 4 * w + p - 1)
                        for i in range(2):
                            mm = pe.transpose(ps[:, 6 + p % 2, i * P:(i + 1) * P], M["arow"][:, p % 2, i * P:(i + 1) * P], S("ident"))
                        mm.then_inc(at, 1)

                    pe.wait_ge(perm, w + 1)
                    pe.wait_ge(added, (w + 1) * 8)
                    for half in range(2):
                        for k in range(4 * half, 4 * half + 4):
                            o = ps[:, 6 + half, (k % 4) * P:(k % 4 + 1) * P]
                            for tt in range(TT):
                                pe.matmul(o, M["hh"][:, tt, k * P:(k + 1) * P], M["pm"][:, tt, :], start=(tt == 0), stop=False)
                                mm = pe.matmul(o, M["hl"][:, tt, k * P:(k + 1) * P], M["pm"][:, tt, :], start=False, stop=(tt == TT - 1))
                        mm.then_inc(gath, 1)
                    for tt in range(TT):
                        mm = pe.transpose(ps[:, 5, tt * P:(tt + 1) * P], M["pm"][:, tt, :].bitcast(F32), S("ident"))
                    mm.then_inc(pt, 1)
                    pe.wait_ge(picked, w + 1)
                    pe.wait_ge(x_done, 2 * w + 2)
                    for s in range(8):
                        piece(s)
                        if s % 2 and s >= 3:
                            turn_act(s // 2 - 1)
                    pe.wait_ge(pt_out, w + 1)
                    pe.wait_ge(at_lo, 4 * w + 2)
                    piece(8)
                    turn_act(3)
                    piece(9)
                    pe.wait_ge(at_lo, 4 * w + 4)
                    piece(10)
                    piece(11)
                    for half in range(2):
                        pe.wait_ge(y_lo, 2 * w + half + 1)
                        for tt in range(TT):
                            i = half * TT + tt
                            if i >= 6:
                                pe.wait_ge(added, w * 8 + 8 + i - 5)
                            o = ps[:, (6, 7, 0, 1, 2, 3, 6, 7)[i], :]
                            pe.matmul(o, M["pT"][:, tt * P:(tt + 1) * P], M["yh"][:, half * 512:(half + 1) * 512], start=True, stop=False)
                            pe.matmul(o, M["pT"][:, tt * P:(tt + 1) * P], M["yl"][:, half * 512:(half + 1) * 512],
                                      start=False, stop=True).then_inc(spread, 1)
                    pe.reg_add(r, r, 1)

        @block.scalar
        def _(act):
            r, now = counter(act, "act_blocks")
            with act.Fori(0, E) as e:
                with act.Fori(0, blocks_of(act, e)) as _:
                    w = now()

                    def high(s):
                        act.wait_ge(raw_in[s % NR], 16 * (w * (NS // NR) + s // NR + 1))
                        act.wait_ge(used, w * NS + s + 1)
                        act.activation(M["hi"][s % NH][:, :, :], M["raw"][s % NR][:, :, :], ACT.Copy).then_inc(hi_done, 1)

                    def sigmoid(p):
                        act.wait_ge(biased, 4 * w + p + 1)
                        act.activation(M["sg"][:, p % 2, :], M["gl"][:, p % 2, 0, :], ACT.Sigmoid, scale=SW_ALPHA).then_inc(sig, 1)

                    def act_high(p):
                        act.wait_ge(at, 4 * w + p + 1)
                        act.activation(M["ah"][:, 2 * p:2 * p + 2, :], ps[:, 6 + p % 2, 0:256].rearrange("p (k s) -> p k s", k=2),
                                       ACT.Copy).then_inc(at_hi, 1)

                    for s in range(3):
                        high(s)
                    for half in range(2):
                        act.wait_ge(gath, w * 2 + half + 1)
                        act.activation(M["xh"][:, 4 * half:4 * half + 4, :], ps[:, 6 + half, :].rearrange("p (k s) -> p k s", k=4),
                                       ACT.Copy).then_inc(x_hi, 1)
                    act.wait_ge(pt, w + 2)
                    act.activation(M["pT"][:, :], ps[:, 5, :], ACT.Copy).then_inc(pt_out, 1)
                    high(3)
                    high(4)
                    sigmoid(0)
                    high(5)
                    high(6)
                    sigmoid(1)
                    act_high(0)
                    high(7)
                    high(8)
                    sigmoid(2)
                    act_high(1)
                    high(9)
                    high(10)
                    sigmoid(3)
                    act_high(2)
                    high(11)
                    act_high(3)
                    for half in range(2):
                        act.wait_ge(used, w * NS + NH + 11 + half)
                        act.activation(M["yh"][:, half * 512:(half + 1) * 512], ps[:, 4 + half, :], ACT.Copy).then_inc(y_hi, 1)
                    act.reg_add(r, r, 1)

        @block.vector
        def _(dve):
            r, now = counter(dve, "dve_blocks")
            dve.sem_inc(lo_v, nv)
            dve.sem_inc(added, 8)
            with dve.Fori(0, E) as e:
                with dve.Fori(0, blocks_of(dve, e)) as _:
                    w = now()

                    def low(s):
                        if s in POOL:
                            return
                        dve.wait_ge(hi_done, w * NS + s + 1)
                        dve.wait_ge(used, w * NS + s + 1)
                        dve.tensor_tensor(M["lo"][s % NH][:, :, :], M["raw"][s % NR][:, :, :], M["hi"][s % NH][:, :, :].bitcast(F32),
                                          ALU.subtract).then_inc(lo_v, 1)

                    def swiglu(p):
                        dve.wait_ge(used, w * NS + NH + 2 * p + 2)
                        gl, li = M["gl"][:, p % 2, 0, :], M["gl"][:, p % 2, 1, :]
                        dve.tensor_scalar(li, ps[:, p, 1:512:2], LIMIT, -LIMIT, ALU.min, ALU.max)
                        dve.tensor_scalar(gl, ps[:, p, 0:511:2], LIMIT, None, ALU.min).then_inc(biased, 1)
                        dve.wait_ge(biased, 4 * w + p + 1)
                        dve.scalar_tensor_tensor(out=li, in0=li, scalar=1.0, in1=gl, op0=ALU.add, op1=ALU.mult).then_inc(mixed, 1)
                        dve.wait_ge(mixed, 4 * w + p + 1)
                        dve.wait_ge(sig, 4 * w + p + 1)
                        dve.tensor_tensor(M["arow"][:, p % 2, :], li, M["sg"][:, p % 2, :], ALU.mult).then_inc(acted, 1)

                    def act_low(p):
                        dve.wait_ge(at_hi, 4 * w + p + 1)
                        src = ps[:, 6 + p % 2, 0:256].rearrange("p (k s) -> p k s", k=2)
                        dve.tensor_tensor(M["al"][:, 2 * p:2 * p + 2, :], src, M["ah"][:, 2 * p:2 * p + 2, :].bitcast(F32),
                                          ALU.subtract).then_inc(at_lo, 1)

                    dve.wait_ge(added, w * 8 + 8)
                    dve.tensor_copy(M["gate"][:, :], R["gates"][:, :, e]).then_inc(cur, 1)
                    for s in range(3):
                        low(s)
                    for half in range(2):
                        dve.wait_ge(x_hi, 2 * w + half + 1)
                        dve.tensor_tensor(M["xl"][:, 4 * half:4 * half + 4, :], ps[:, 6 + half, :].rearrange("p (k s) -> p k s", k=4),
                                          M["xh"][:, 4 * half:4 * half + 4, :].bitcast(F32), ALU.subtract).then_inc(x_done, 1)
                    low(3)
                    low(4)
                    swiglu(0)
                    low(5)
                    low(6)
                    swiglu(1)
                    act_low(0)
                    low(7)
                    low(8)
                    swiglu(2)
                    act_low(1)
                    low(9)
                    low(10)
                    swiglu(3)
                    act_low(2)
                    low(11)
                    act_low(3)
                    for half in range(2):
                        dve.wait_ge(y_hi, 2 * w + half + 1)
                        at_ = slice(half * 512, (half + 1) * 512)
                        dve.tensor_tensor(M["yl"][:, at_], ps[:, 4 + half, :], M["yh"][:, at_].bitcast(F32), ALU.subtract).then_inc(y_lo, 1)
                    dve.wait_ge(cur, w + 1)
                    for i in range(8):
                        half, tt = i // TT, i % TT
                        dve.wait_ge(spread, w * 8 + i + 1)
                        f = T["f"][:, tt, half * 512:(half + 1) * 512]
                        dve.scalar_tensor_tensor(out=f, in0=ps[:, (6, 7, 0, 1, 2, 3, 6, 7)[i], :], scalar=M["gate"][:, tt:tt + 1], in1=f,
                                                 op0=ALU.mult, op1=ALU.add).then_inc(added, 1)
                    dve.reg_add(r, r, 1)


def split_stage(nc, src, hi, lo):
    with stage(nc, "hi_done", "lo_done") as (block, hi_done, lo_done):
        @block.scalar
        def _(act):
            act.activation(hi, src, ACT.Copy).then_inc(hi_done, 1)

        @block.vector
        def _(dve):
            dve.wait_ge(hi_done, 1)
            dve.tensor_tensor(lo, src, hi.bitcast(F32), ALU.subtract).then_inc(lo_done, 1)
            dve.wait_ge(lo_done, 1)


def rms_rows(nc, h, x, gain, tmp, ss, n, width=D):
    with stage(nc, "sums", "mean_in", "root", "dve_step") as (block, sums, mean_in, root, dve_step):
        @block.scalar
        def _(act):
            for t in range(n):
                if t:
                    act.wait_ge(sums, t)
                act.activation(tmp[:, 0:width], x[:, t, :], ACT.Square, accum_out=ss[:, t:t + 1]).then_inc(sums, 1)
            act.wait_ge(mean_in, 1)
            act.activation(ss[:, 0:n], ss[:, 0:n], ACT.Sqrt).then_inc(root, 1)

        @block.vector
        def _(dve):
            done = Chain(dve, dve_step)
            dve.wait_ge(sums, n)
            dve.tensor_scalar(ss[:, 0:n], ss[:, 0:n], 1.0 / width, RMS_EPS, ALU.mult, ALU.add).then_inc(mean_in, 1)
            dve.wait_ge(root, 1)
            done(dve.reciprocal(ss[:, 0:n], ss[:, 0:n]))
            for t in range(n):
                done(dve.scalar_tensor_tensor(out=h[:, t, :], in0=x[:, t, :], scalar=ss[:, t:t + 1], in1=gain,
                                              op0=ALU.mult, op1=ALU.mult))


def head_norms(nc, jobs, sq, r):
    with stage(nc, "mean_in", "root", "dve_step") as (block, mean_in, root, dve_step):
        at, spans = 0, []
        for src, dsts, gain, size in jobs:
            n = src.shape[1] * src.shape[2]
            spans.append((at, n))
            at += n

        @block.vector
        def _(dve):
            done = Chain(dve, dve_step)
            np_ = jobs[0][0].shape[0]
            for (src, dsts, gain, size), (a, n) in zip(jobs, spans):
                t, h = src.shape[1], src.shape[2]
                s4 = sq[0:np_, 0:n * size].rearrange("p (t h s) -> p t h s", t=t, h=h)
                done(dve.tensor_tensor(s4, src, src, ALU.mult))
                done(dve.tensor_reduce(r[0:np_, a:a + n].rearrange("p (t h) -> p t h", t=t), s4, AX_X, ALU.add))
                done(dve.tensor_scalar(r[0:np_, a:a + n], r[0:np_, a:a + n], 1.0 / size, RMS_EPS, ALU.mult, ALU.add))
            dve.tensor_copy(r[0:np_, at:at + 1], r[0:np_, 0:1]).then_inc(mean_in, 1)
            dve.wait_ge(root, 1)
            done(dve.reciprocal(r[0:np_, 0:at], r[0:np_, 0:at]))
            for (src, dsts, gain, size), (a, n) in zip(jobs, spans):
                t, h = src.shape[1], src.shape[2]
                r3 = r[0:np_, a:a + n].rearrange("p (t h) -> p t h", t=t)
                done(dve.tensor_tensor(src, src, bc(r3, 3, size), ALU.mult))
                for part, dst in dsts:
                    g3 = bc(bc(gain, 1, part.shape[2]), 1, t)
                    done(dve.tensor_tensor(dst, part, g3, ALU.mult))

        @block.scalar
        def _(act):
            act.wait_ge(mean_in, 1)
            act.activation(r[0:jobs[0][0].shape[0], 0:at], r[0:jobs[0][0].shape[0], 0:at], ACT.Sqrt).then_inc(root, 1)


def rope(nc, T, views, tmp):
    S = T["s"]
    with stage(nc, "dve_step") as (block, dve_step):
        @block.vector
        def _(dve):
            done = Chain(dve, dve_step)
            for v in views:
                h = v.shape[2]
                cos = bc(S("cos").rearrange("p (t s) -> p t s", t=TT), 2, h)
                sin = bc(S("sin").rearrange("p (t s) -> p t s", t=TT), 2, h)
                x1, x2 = v[:, :, :, 0:32], v[:, :, :, 32:64]
                n = TT * h * 32
                t1 = tmp[:, 0:n].rearrange("p (t h s) -> p t h s", t=TT, h=h)
                t2 = tmp[:, n:2 * n].rearrange("p (t h s) -> p t h s", t=TT, h=h)
                done(dve.tensor_tensor(t1, x1, sin, ALU.mult))
                done(dve.tensor_tensor(t2, x2, sin, ALU.mult))
                done(dve.tensor_tensor(x1, x1, cos, ALU.mult))
                done(dve.tensor_tensor(x2, x2, cos, ALU.mult))
                done(dve.tensor_tensor(x1, x1, t2, ALU.subtract))
                done(dve.tensor_tensor(x2, x2, t1, ALU.add))


def compress(nc, ps, T, L, Z):
    with stage(nc, "pe_t", "pe_out", "blk", "hid", "sg", "silu", "two", "two_out", "dve_step") as (
            block, pe_t, pe_out, blk, hid, sg, silu, two, two_out, dve_step):
        S = T["s"]

        @block.tensor
        def _(pe):
            for i in range(2):
                last = pe.transpose(ps[:, 0, i * 32:(i + 1) * 32], L["pe"][:, i, :, :].rearrange("p g d -> p (g d)"), S("ident")[0:32, 0:32])
            last.then_inc(pe_t, 1)
            for i in range(2):
                pe.wait_ge(blk, i + 1)
                for g in range(2):
                    for l in range(32):
                        last = pe.matmul(ps[:, 1 + 2 * i + g, 0:NCMP], L["cw1"][i][g * HS:(g + 1) * HS, l, :],
                                         Z["blk"][g * HS:(g + 1) * HS, i, l, 0:NCMP], start=(l == 0), stop=(l == 31))
                last.then_inc(hid, 1)
            pe.wait_ge(silu, 2)
            for g in range(2):
                pe.matmul(ps[0:32, 5, g * HS:(g + 1) * HS], Z["hid"][:, 0, g, :], L["cw2"][:, 0, :], start=True, stop=True)
                for o in range(4):
                    last = pe.matmul(ps[32 * o:32 * o + 32, 6, g * HS:(g + 1) * HS], Z["hid"][:, 1, g, :], L["cw2"][:, 1, :],
                                     start=True, stop=True)
            last.then_inc(two, 1)

        @block.vector
        def _(dve):
            done = Chain(dve, dve_step)
            done(dve.memset(Z["hid"][:, :, :, :], 0.0))
            dve.wait_ge(pe_out, 1)
            for i, src in enumerate((Z["kcT"], Z["vcT"])):
                v = src[:, :].rearrange("p (n s) -> p s n", s=16)
                dve.tensor_tensor(Z["blk"][:, i, 0:16, 0:NCMP], v[:, :, 0:NCMP], bc(Z["peT"][:, i, 0:16], 2, NCMP), ALU.add)
                dve.tensor_tensor(Z["blk"][:, i, 16:32, 0:NCMP], v[:, :, 1:NCMP + 1], bc(Z["peT"][:, i, 16:32], 2, NCMP),
                                  ALU.add).then_inc(blk, 1)
            for i in range(2):
                dve.wait_ge(sg, i + 1)
                dve.tensor_tensor(Z["hid"][:, i, :, 0:NCMP], ps[:, 1 + 2 * i:3 + 2 * i, 0:NCMP],
                                  Z["hsg"][:, i, :, 0:NCMP], ALU.mult).then_inc(silu, 1)

        @block.scalar
        def _(act):
            act.wait_ge(pe_t, 1)
            act.activation(Z["peT"][:, :, :], ps[:, 0, 0:64].rearrange("p (i l) -> p i l", i=2), ACT.Copy).then_inc(pe_out, 1)
            for i in range(2):
                act.wait_ge(hid, i + 1)
                act.activation(Z["hsg"][:, i, :, 0:NCMP], ps[:, 1 + 2 * i:3 + 2 * i, 0:NCMP],
                               ACT.Sigmoid).then_inc(sg, 1)
            act.wait_ge(two, 1)
            act.activation(Z["kcr"][:, :], ps[0:32, 5, 0:P], ACT.Copy).then_inc(two_out, 1)
            act.activation(Z["vc"][:, :], ps[:, 6, 0:P], ACT.Copy).then_inc(two_out, 1)
            act.wait_ge(two_out, 2)


def compressed_attention(nc, ps, T, Z):
    S = T["s"]
    with stage(nc, "scores", "shifted", "expd", "probs", "pt", "pt_out", "pv", "pv_out", "dve_step") as (
            block, scores, shifted, expd, probs, pt, pt_out, pv, pv_out, dve_step):
        @block.tensor
        def _(pe):
            for tt in range(TT):
                for h in range(8):
                    g, r = h // 4, h % 4
                    last = pe.matmul(ps[:, 4 * g + tt, r * 32:(r + 1) * 32],
                                     Z["qT"][g * HS:(g + 1) * HS, r, tt * P:(tt + 1) * P], Z["kc"][g * HS:(g + 1) * HS, :],
                                     start=True, stop=True)
            last.then_inc(scores, 1)
            pe.wait_ge(probs, 1)
            for tt in range(TT):
                for g in range(2):
                    last = pe.transpose(ps[:, 2 + g, tt * P:(tt + 1) * P],
                                        Z["cp"][:, tt, g * P:(g + 1) * P], S("ident"))
            last.then_inc(pt, 1)
            pe.wait_ge(pt_out, 1)
            for tt in range(TT):
                for h in range(8):
                    g, r = h // 4, h % 4
                    at = (tt * 2 + g) * HS
                    last = pe.matmul(ps[:, 4 + r, at:at + HS], Z["cpT"][32 * r:32 * r + 32, g, tt * P:(tt + 1) * P],
                                     Z["vc"][32 * r:32 * r + 32, g * HS:(g + 1) * HS], start=True, stop=True)
            last.then_inc(pv, 1)

        s4 = Z["cp"][:, :, :].rearrange("p t (h n) -> p t h n", n=32)
        s3 = Z["cp"][:, :, :].rearrange("p t (h n) -> p (t h) n", n=32)

        @block.vector
        def _(dve):
            done = Chain(dve, dve_step)
            dve.wait_ge(scores, 1)
            add = S("cmpadd").rearrange("p (t n) -> p t n", t=TT)
            ok = S("cmpok").rearrange("p (t n) -> p t n", t=TT)
            for g in range(2):
                done(dve.tensor_tensor(s4[:, :, 4 * g:4 * g + 4, :], ps[:, 4 * g:4 * g + 4, 0:P].rearrange("p t (r n) -> p t r n", r=4),
                                       bc(add, 2, 4), ALU.add))
            done(dve.tensor_reduce(Z["cm"][:, 0, :], s3, AX_X, ALU.max))
            dve.tensor_tensor(s3, s3, bc(Z["cm"][:, 0, :], 2, 32), ALU.subtract).then_inc(shifted, 1)
            dve.wait_ge(expd, 1)
            done(dve.tensor_tensor(s4, s4, bc(ok, 2, 8), ALU.mult))
            done(dve.tensor_reduce(Z["cm"][:, 0, :], s3, AX_X, ALU.add))
            done(dve.tensor_scalar(Z["cm"][:, 0, :], Z["cm"][:, 0, :], 1e-30, None, ALU.max))
            done(dve.reciprocal(Z["cm"][:, 0, :], Z["cm"][:, 0, :]))
            g0 = Z["gate"][:, :, :].rearrange("p t (h b) -> p t h b", b=3)[:, :, :, 0]
            c3 = Z["cm"][:, 0, :].rearrange("p (t h) -> p t h", t=TT)
            done(dve.tensor_tensor(c3, c3, g0, ALU.mult))
            dve.tensor_tensor(s3, s3, bc(Z["cm"][:, 0, :], 2, 32), ALU.mult).then_inc(probs, 1)

        @block.scalar
        def _(act):
            act.wait_ge(shifted, 1)
            act.activation(s3, s3, ACT.Exp).then_inc(expd, 1)
            act.wait_ge(pt, 1)
            act.activation(Z["cpT"][:, :, :], ps[:, 2:4, :], ACT.Copy).then_inc(pt_out, 1)
            act.wait_ge(pv, 1)
            for r in range(4):
                o = Z["o"][0].rearrange("p t (g r s) -> p t g r s", g=2, r=4)[:, :, :, r, :]
                act.activation(o, ps[:, 4 + r, :].rearrange("p (t g s) -> p t g s", t=TT, g=2), ACT.Copy).then_inc(pv_out, 1)
            act.wait_ge(pv_out, 4)


def attention(nc, ps, T, Z, units):
    S = T["s"]
    with stage(nc, "scores", "top", "probs", "pt", "pt_v", "pt_a", "pv", "pv_out", "dve_step") as (
            block, scores, top, probs, pt, pt_v, pt_a, pv, pv_out, dve_step):
        n = len(units)

        @block.tensor
        def _(pe):
            def score(i):
                u = units[i]
                if i >= 2:
                    pe.wait_ge(probs, i - 1)
                o = ps[:, i % 2, 0:u["n"]]
                mm = pe.matmul(o, u["q"], u["k"], start=True, stop=not u["extra"])
                for x, (a, b, lo, hi) in enumerate(u["extra"]):
                    mm = pe.matmul(ps[:, i % 2, lo:hi], a, b, start=False, stop=(x == len(u["extra"]) - 1))
                mm.then_inc(scores, 1)

            def rest(i):
                u = units[i]
                nk = u["n"] // P
                pe.wait_ge(probs, i + 1)
                for b in range(nk):
                    mm = pe.transpose(ps[:, 2 + i % 2, b * P:(b + 1) * P], Z["p"][:, i % 2, b * P:(b + 1) * P], S("ident"))
                mm.then_inc(pt, 1)
                pe.wait_ge(pt_v, i + 1)
                if i >= 2:
                    pe.wait_ge(pv_out, i - 1)
                for b in range(nk):
                    mm = pe.matmul(ps[:, 4 + i % 2, 0:u["w"]], Z["pT"][:, i % 2, b * P:(b + 1) * P], u["v"][b],
                                   start=(b == 0), stop=(b == nk - 1))
                mm.then_inc(pv, 1)

            score(0)
            for i in range(n):
                if i + 1 < n:
                    score(i + 1)
                rest(i)

        @block.scalar
        def _(act):
            for i, u in enumerate(units):
                act.wait_ge(top, i + 1)
                act.activation(Z["p"][:, i % 2, 0:u["n"]], ps[:, i % 2, 0:u["n"]], ACT.Exp, bias=Z["nm"][:, i % 4:i % 4 + 1],
                               accum_out=Z["sum"][:, i % 4:i % 4 + 1]).then_inc(probs, 1)

        @block.vector
        def _(dve):
            done = Chain(dve, dve_step)

            def maximum(i):
                u = units[i]
                dve.wait_ge(scores, i + 1)
                done(dve.tensor_reduce(Z["mx"][:, i % 4:i % 4 + 1], ps[:, i % 2, 0:u["n"]], AX_X, ALU.max))
                dve.tensor_scalar(Z["nm"][:, i % 4:i % 4 + 1], Z["mx"][:, i % 4:i % 4 + 1], -1.0, None, ALU.mult).then_inc(top, 1)

            maximum(0)
            for i, u in enumerate(units):
                if i + 1 < n:
                    maximum(i + 1)
                dve.wait_ge(pt, i + 1)
                dve.tensor_copy(Z["pT"][:, i % 2, 0:u["n"]], ps[:, 2 + i % 2, 0:u["n"]]).then_inc(pt_v, 1)
                rs = Z["rs"][:, i % 4:i % 4 + 1]
                done(dve.reciprocal(rs, Z["sum"][:, i % 4:i % 4 + 1]))
                dve.wait_ge(pv, i + 1)
                src = ps[:, 4 + i % 2, 0:u["w"]]
                if u["gate"] is None:
                    dve.tensor_scalar(u["o"], src, rs, None, ALU.mult).then_inc(pv_out, 1)
                else:
                    done(dve.tensor_scalar(rs, rs, u["gate"], None, ALU.mult))
                    dve.scalar_tensor_tensor(out=u["o"], in0=src, scalar=rs, in1=u["o"], op0=ALU.mult, op1=ALU.add).then_inc(pv_out, 1)


def forget_bias(nc, ps, T, Z, L):
    S = T["s"]
    with stage(nc, "eased", "sq", "logf", "cum", "cum_out", "dve_step") as (
            block, eased, sq, logf, cum, cum_out, dve_step):
        f = Z["z"][:, :, 3352:3360]

        @block.vector
        def _(dve):
            done = Chain(dve, dve_step)
            done(dve.tensor_tensor(Z["lf"][:, 0, :, :], f, bc(L["fb"][:, :], 1, TT), ALU.add))
            done(dve.tensor_scalar(Z["lf"][:, 1, :, :], Z["lf"][:, 0, :, :], -1.0, None, ALU.mult))
            dve.tensor_tensor(Z["lf"][:, 1, :, :], Z["lf"][:, 0, :, :], Z["lf"][:, 1, :, :], ALU.min).then_inc(eased, 1)
            dve.wait_ge(sq, 2)
            done(dve.tensor_scalar(Z["lf"][:, 0, :, :], Z["lf"][:, 0, :, :], 0.0, None, ALU.min))
            dve.tensor_tensor(Z["lf"][:, 0, :, :], Z["lf"][:, 0, :, :], Z["lf"][:, 1, :, :], ALU.subtract).then_inc(logf, 1)

        @block.scalar
        def _(act):
            act.wait_ge(eased, 1)
            act.activation(Z["lf"][:, 1, :, :], Z["lf"][:, 1, :, :], ACT.Exp).then_inc(sq, 1)
            act.wait_ge(sq, 1)
            act.activation(Z["lf"][:, 1, :, :], Z["lf"][:, 1, :, :], ACT.Ln, bias=1.0).then_inc(sq, 1)
            act.wait_ge(cum, 1)
            act.activation(Z["cT"][:, 0, :], ps[0:8, 0, :], ACT.Copy).then_inc(cum_out, 1)
            act.activation(Z["cT"][:, 1, :], ps[0:8, 0, :], ACT.Copy, scale=-1.0).then_inc(cum_out, 1)
            act.wait_ge(cum_out, 2)

        @block.tensor
        def _(pe):
            pe.wait_ge(logf, 1)
            for tt in range(TT):
                for t2 in range(tt + 1):
                    last = pe.matmul(ps[0:8, 0, tt * P:(tt + 1) * P], Z["lf"][:, 0, t2, :],
                                     S("ones") if t2 < tt else S("upto"), start=(t2 == 0), stop=(t2 == tt))
            last.then_inc(cum, 1)


def gate_outputs(nc, Z):
    cols = (1304, 3360, 4384)
    with stage(nc, "sg", "dve_step") as (block, sg, dve_step):
        @block.scalar
        def _(act):
            for b, c in enumerate(cols):
                act.activation(Z["sgl"][:, b, :, :], Z["z"][:, :, c:c + 512], ACT.Sigmoid).then_inc(sg, 1)

        @block.vector
        def _(dve):
            done = Chain(dve, dve_step)
            for b, c in enumerate(cols):
                dve.wait_ge(sg, b + 1)
                o = Z["o"][b]
                done(dve.tensor_tensor(o, o, Z["z"][:, :, c:c + 512], ALU.mult))
                done(dve.tensor_tensor(o, o, Z["sgl"][:, b, :, :], ALU.mult))


def merge(nc, A, ps, T, U, l, ring):
    nb = len(ring)
    jobs = [(n, b) for n in range(2) for b in range(3)]
    names = ("w_branch_a_2", "w_branch_b_2", "w_branch_m_2")
    with stage(nc, *[f"w_in{i}" for i in range(nb)], "gates", "branch", "sg", "mul", "done_", "dve_step") as sems:
        block, w_in, (gates, branch, sg, mul, done_, dve_step) = sems[0], sems[1:1 + nb], sems[1 + nb:]
        nt = len(jobs) * TT

        @block.sync
        def _(sp):
            for i, (n, b) in enumerate(jobs):
                for part in range(2):
                    q = 2 * i + part
                    if q >= nb:
                        sp.wait_ge(branch if (q - nb) % 2 else gates, TT * ((q - nb) // 2 + 1))
                    if part == 0:
                        a = MERGE0 + b * D + n * 512
                        src = A["w_in_2"][l].rearrange("(k p) n -> p k n", p=P)[:, :, a:a + 512]
                        sp.dma_start(ring[q % nb][:, :, :], src).then_inc(w_in[q % nb], 16)
                    else:
                        src = A[names[b]][l].rearrange("(k p) n -> p k n", p=P)[:, :, n * 512:(n + 1) * 512]
                        sp.dma_start(ring[q % nb][:, 0:4, :], src).then_inc(w_in[q % nb], 16)

        @block.tensor
        def _(pe):
            for i, (n, b) in enumerate(jobs):
                q = 2 * i
                for tt in range(TT):
                    m = i * TT + tt
                    if tt == 0:
                        pe.wait_ge(w_in[q % nb], 16 * (q // nb + 1))
                    if m >= 2:
                        pe.wait_ge(sg, m - 1)
                    for k in range(KD):
                        mm = pe.matmul(ps[:, m % 2, :], U["hT"][:, k, tt * P:(tt + 1) * P], ring[q % nb][:, k, :],
                                       start=(k == 0), stop=(k == KD - 1))
                    mm.then_inc(gates, 1)
                    if tt == 0:
                        pe.wait_ge(w_in[(q + 1) % nb], 16 * ((q + 1) // nb + 1))
                    if m >= 2:
                        pe.wait_ge(mul, m - 1)
                    for k in range(4):
                        mm = pe.matmul(ps[:, 2 + m % 2, :], U["oT"][:, b * 4 + k, tt * P:(tt + 1) * P], ring[(q + 1) % nb][:, k, :],
                                       start=(k == 0), stop=(k == 3))
                    mm.then_inc(branch, 1)

        @block.scalar
        def _(act):
            for m in range(nt):
                act.wait_ge(gates, m + 1)
                if m >= 2:
                    act.wait_ge(mul, m - 1)
                act.activation(U["sg"][:, m % 2, :], ps[:, m % 2, :], ACT.Sigmoid).then_inc(sg, 1)

        @block.vector
        def _(dve):
            done = Chain(dve, dve_step)
            for m in range(nt):
                n, b = jobs[m // TT]
                tt = m % TT
                dve.wait_ge(sg, m + 1)
                dve.wait_ge(branch, m + 1)
                u = U["u"][:, tt, n * 512:(n + 1) * 512]
                if b == 0:
                    dve.tensor_tensor(u, U["sg"][:, m % 2, :], ps[:, 2 + m % 2, :], ALU.mult).then_inc(mul, 1)
                else:
                    dve.tensor_tensor(U["tmp"][:, :], U["sg"][:, m % 2, :], ps[:, 2 + m % 2, :], ALU.mult).then_inc(mul, 1)
                    dve.wait_ge(mul, m + 1)
                    done(dve.tensor_tensor(u, u, U["tmp"][:, :], ALU.add))


def add_stage(nc, x, y):
    with stage(nc, "dve_step") as (block, dve_step):
        @block.vector
        def _(dve):
            Chain(dve, dve_step)(dve.tensor_tensor(x, x, y, ALU.add))


def load_stage(nc, pairs):
    with stage(nc, "moved") as (block, moved):
        @block.sync
        def _(sp):
            for dst, src in pairs:
                sp.dma_start(dst, src).then_inc(moved, 16)
            sp.wait_ge(moved, 16 * len(pairs))


def copy_evac(dst):
    def evac(act, n, m, psum):
        return act.activation(dst(n, m), psum, ACT.Copy)
    return evac


def tiles4(dst, src, cols, nt):
    out = []
    for c in range(cols):
        for t0 in range(0, nt, 4):
            ts = range(t0, min(t0 + 4, nt))
            out.append(([src(t, c) for t in ts], dst[:, c, t0 * P:(t0 + len(ts)) * P]))
    return out


def program(nc, A, out, probe=None):
    probe = probe or (lambda name, ap: None)
    spill = nc.dram_tensor("kept_rows", (P, 8192), F32).ap()
    with ExitStack() as top:
        def sb(ctx, name, shape, dt=F32):
            return ctx.enter_context(nc.sbuf_tensor(name, shape, dt))

        top.enter_context(nc.allow_non_contiguous_dma(reason="vectors of a few thousand elements, channel by partition"))
        psum = top.enter_context(nc.psum_tensor("ps", [P, 8, 512], F32))
        ps = psum[:, :, :]
        bank = [psum[:, i, :] for i in range(8)]
        T = {}
        T["small"] = sb(top, "small", [P, SMALL.shape[1]])
        T["s"] = lambda n: T["small"][:, SMALL_AT[n][0]:SMALL_AT[n][0] + SMALL_AT[n][1]]
        T["onerow"] = sb(top, "onerow", [1, P])
        ident = T["s"]("ident")

        with ExitStack() as mix:
            T["mixT"] = sb(mix, "mixT", [P, KD, SEQ])
            with ExitStack() as mt:
                T["mT"] = sb(mt, "mT", [P, SHIFT // P, ALLT])
                with ExitStack() as ft:
                    T["fT"] = sb(ft, "fT", [P, FN // P, SEQ])
                    with ExitStack() as one:
                        T["xn"] = sb(one, "xn", [P, TA, D])
                        T["modb"] = sb(one, "modb", [P, 6 * D])
                        T["modc"] = sb(one, "modc", [P, 2 * D])
                        with ExitStack() as s:
                            T["c2"] = sb(s, "c2", [P, 2 * KD])
                            T["csig"] = sb(s, "csig", [P, 2 * KD])
                            T["cwide"] = sb(s, "cwide", [P, 2 * KD, P])
                            T["adab"] = T["fT"][0:1, :, :].rearrange("p a b -> p (a b)")
                            T["gain"] = sb(s, "gain", [P, D])
                            T["bias"] = sb(s, "bias", [P, D])
                            T["stats"] = sb(s, "stats", [P, 96])
                            mt_flat = T["mT"][:, :, :].rearrange("p a b -> p (a b)")
                            ring = [mt_flat[:, i * 4096:(i + 1) * 4096].rearrange("p (k n) -> p k n", k=KD) for i in range(3)]
                            mx_flat = T["mixT"][0:1, :, :].rearrange("p a b -> p (a b)")
                            T["adab"] = sb(s, "adab", [1, 6 * D])
                            modulation(nc, A, bank, T, ring)
                            layer_norm_stage(nc, T["xn"][:, :, :], TA, T["gain"][:, :], T["bias"][:, :], T["stats"])
                        probe("x0", T["xn"][:, :, :])
                        probe("modb", T["modb"][:, :])
                        probe("modc", T["modc"][:, :])
                        load_stage(nc, [(spill[:, 0:4096].rearrange("p (t d) -> p t d", t=TT), T["xn"][:, 0:TT, :]),
                                        (spill[:, 4096:8192], T["modb"][:, 2 * D:6 * D])])
                        modulate_stage(nc, T["xn"][:, 0:TT, :], T["xn"][:, 0:TT, :], TT, T["modb"][:, D:2 * D], T["modb"][:, 0:D])
                        modulate_stage(nc, T["xn"][:, TT:TA, :], T["xn"][:, TT:TA, :], 2, T["modc"][:, D:2 * D], T["modc"][:, 0:D])
                        with ExitStack() as s:
                            hT = sb(s, "hT", [P, KD, ALLT])
                            turn(nc, bank, ident, tiles4(hT, lambda t, c: T["xn"][:, t, c * P:(c + 1) * P], KD, TA))
                            T["mu"] = sb(s, "mu", [P, 4, SHIFT // P])
                            T["padg"] = [sb(s, f"padg{i}", [P, GRID_H + 2, GRID_W + 2]) for i in range(2)]
                            T["padc"] = [sb(s, f"padc{i}", [P, CTX + 2]) for i in range(2)]
                            T["nbr"] = sb(s, "nbr", [P, 2 * SEQ + CTX])
                            ring_flat = T["modb"][:, :]
                            ring = [ring_flat[:, i * 2048:(i + 1) * 2048].rearrange("p (k n) -> p k n", k=KD) for i in range(3)]
                            project_in(nc, A, bank, T, hT, ring)
                    probe("mT", T["mT"][:, :, :])
                    with ExitStack() as s:
                        B = {"tab": sb(s, "tab", [P, BIG.shape[1]]), "bf": sb(s, "bf", [P, 4]), "wf": sb(s, "wf", [P, 4, P]),
                             "f12": sb(s, "f12", [P, 2, TT, FN]), "spec": sb(s, "spec", [P, 4, SEQ])}
                        T["b"] = lambda n: B["tab"][:, BIG_AT[n][0]:BIG_AT[n][0] + BIG_AT[n][1]]
                        fourier(nc, A, ps, T, B)
                with ExitStack() as s:
                    T["par"] = sb(s, "par", [P, 4, 8])
                    T["w2"] = sb(s, "w2", [P, C])
                    T["a2"] = sb(s, "a2", [P, C])
                    T["g2"] = sb(s, "g2", [P, 2, C])
                    T["gng"] = sb(s, "gng", [P, C])
                    T["gnb"] = sb(s, "gnb", [P, C])
                    rwkv_params(nc, A, T)
                    W = {n: sb(s, "cur_" + n, shape) for n, shape in {
                        "w2": [P, P], "a2": [P, P], "par": [P, 8], "ar": [P, 2, TA, 2, P], "bt": [P, 2, ALLT], "kt": [P, 2, ALLT],
                        "vrow": [P, TA, P], "arow": [P, 2, TA, P], "brow": [P, 2, TA, P], "krow": [P, 2, TA, P],
                        "qt": [P, 2, TT, P], "gt": [P, 2, NCH, HS], "hp": [P, 2, NCH, HS], "yr": [P, TT, 2, P],
                        "pc": [P, 2, NCH], "tot": [P, 2, NCH], "bon": [P, 16], "st": [P, 2, 2, HS]}.items()}
                    with nc.Fori(0, 4) as c:
                        with ExitStack() as q:
                            for n, shape in {"v": [P, ALLT], "lw": [P, 2, ALLT], "a": [P, 2, ALLT], "ci": [P, 2, ALLT],
                                             "e1": [P, 2, ALLT], "kd": [P, 2, ALLT], "kk": [P, ALLT], "t0": [P, ALLT],
                                             "rk": [P, 2, SEQ]}.items():
                                W[n] = sb(q, "prep_" + n, shape)
                            rwkv_prepare(nc, ps, T, W, c)
                            groups = []
                            for t0 in (0, 4):
                                ts = range(t0, min(t0 + 4, TA))
                                groups.append(([W["v"][:, t * P:(t + 1) * P] for t in ts], W["vrow"][:, ts[0]:ts[-1] + 1, :]))
                                for d in range(2):
                                    groups.append(([W["ar"][:, d, t, 0, :] for t in ts], W["arow"][:, d, ts[0]:ts[-1] + 1, :]))
                                    groups.append(([W["bt"][:, d, t * P:(t + 1) * P] for t in ts], W["brow"][:, d, ts[0]:ts[-1] + 1, :]))
                                    groups.append(([W["kt"][:, d, t * P:(t + 1) * P] for t in ts], W["krow"][:, d, ts[0]:ts[-1] + 1, :]))
                            turn(nc, bank, ident, groups)
                        with ExitStack() as q:
                            for n, shape in {"m": [P, 2, 4, 512], "x": [P, 2, 4, P], "xt": [P, 2, 4, P], "y": [P, 2, 4, P],
                                             "rhs": [P, 2, 4, P], "wu": [P, 2, 4, P]}.items():
                                W[n] = sb(q, "unit_" + n, shape)
                            rwkv_chunks(nc, ps, T, W)
                        rwkv_scan(nc, ps, T, W)
                        with ExitStack() as q:
                            for n, shape in {"mean": [P, 16], "var": [P, 16], "big": [P, 1024], "rw": [P, TT, P]}.items():
                                W[n] = sb(q, "out_" + n, shape)
                            rwkv_output(nc, ps, T, W, c)
            probe("mixT", T["mixT"][:, :, :])
            x = None
            with ExitStack() as s:
                mo = sb(s, "mo", [P, TT, D])
                ring = [sb(s, f"ring{i}", [P, KD, 512]) for i in range(2)]
                w = A["w_out"][0].rearrange("(k p) n -> p k n", p=P)
                ring_gemm(nc, bank, lambda n: w[:, :, n * 512:(n + 1) * 512], lambda n: 512, 2, TT,
                          lambda k, m: T["mixT"][:, k, m * P:(m + 1) * P], KD, ring,
                          copy_evac(lambda n, m: mo[:, m, n * 512:(n + 1) * 512]))
                load_stage(nc, [(spill[:, 0:1], spill[:, 0:1])]) if False else None
                x1 = sb(s, "x1", [P, TT, D])
                g1 = sb(s, "g1", [P, D])
                gain = sb(s, "gain1", [P, D])
                bias = sb(s, "bias1", [P, D])
                stats = sb(s, "stats1", [P, 96])
                load_stage(nc, [(x1[:, :, :], spill[:, 0:4096].rearrange("p (t d) -> p t d", t=TT)),
                                (g1[:, :], spill[:, 4096:5120]),
                                (gain[:, :], A["ln1_g"][0].partition_broadcast(P)), (bias[:, :], A["ln1_b"][0].partition_broadcast(P))])
                residual_stage(nc, x1[:, :, :], mo[:, :, :], g1[:, :], TT)
                layer_norm_stage(nc, x1[:, :, :], TT, gain[:, :], bias[:, :], stats)
                load_stage(nc, [(spill[:, 0:4096].rearrange("p (t d) -> p t d", t=TT), x1[:, :, :])])
        with ExitStack() as moe:
            T["f"] = sb(moe, "f", [P, TT, D])
            R = {"gates": sb(moe, "gates", [P, TT, E]), "place": sb(moe, "place", [P, TT, E]), "nblki": sb(moe, "nblki", [P, E], I32)}
            M = {n: sb(moe, "ex_" + n, shape, F32R) for n, shape in {"hh": [P, TT, D], "hl": [P, TT, D], "b12": [2 * E, 2 * D]}.items()}
            with ExitStack() as s:
                mod = sb(s, "mod2", [P, 2 * D])
                hrow = sb(s, "hrow", [P, TT, D])
                b1r = sb(s, "b1r", [2 * E, 2 * D])
                load_stage(nc, [(mod[:, :], spill[:, 5120:7168]), (hrow[:, :, :], spill[:, 0:4096].rearrange("p (t d) -> p t d", t=TT)),
                                (b1r[0:E, :], A["b1"][0]), (b1r[E:2 * E, :], A["b1"][0])])
                probe("x1", hrow[:, :, :])
                modulate_stage(nc, hrow[:, :, :], hrow[:, :, :], TT, mod[:, D:2 * D], mod[:, 0:D])
                split_stage(nc, hrow[:, :, :], M["hh"][:, :, :], M["hl"][:, :, :])
                with stage(nc, "high", "low_") as (block, high, low_):
                    @block.scalar
                    def _(act):
                        act.activation(M["b12"][:, :], b1r[:, :], ACT.Copy).then_inc(high, 1)

                    @block.vector
                    def _(dve):
                        dve.wait_ge(high, 1)
                        dve.tensor_tensor(M["b12"][E:2 * E, :], b1r[E:2 * E, :], M["b12"][E:2 * E, :].bitcast(F32),
                                          ALU.subtract).then_inc(low_, 1)
                        dve.wait_ge(low_, 1)
                T["hT"] = sb(s, "hT2", [P, KD, SEQ])
                turn(nc, bank, ident, tiles4(T["hT"], lambda t, c: hrow[:, t, c * P:(c + 1) * P], KD, TT))
                for n, shape in {"wr": [P, KD, E], "br": [1, E], "b2": [E, D], "lg": [P, TT, E], "m8": [P, TT, 8], "i8f": [P, TT, 8],
                                 "g4": [P, TT, TOPK], "sum4": [P, TT], "sel": [P, TT, E], "tmp": [P, E], "nblk": [P, E],
                                 "gT": [E, SEQ]}.items():
                    R[n] = sb(s, "rt_" + n, shape)
                R["i8"] = sb(s, "rt_i8", [P, TT, 8], U32)
                router(nc, A, ps, T, R)
            probe("gates", R["gates"][:, :, :])
            with ExitStack() as s:
                for n, shape in {"arow": [P, 2, 256], "gl": [P, 2, 2, 256], "sg": [P, 2, 256], "place": [P, TT], "next": [P, TT], "gate": [P, TT]}.items():
                    M[n] = sb(s, "ex_" + n, shape)
                for n, shape in {"xh": [P, KD, P], "xl": [P, KD, P], "ah": [P, KD, P], "al": [P, KD, P], "yh": [P, D], "yl": [P, D],
                                 "pm": [P, TT, P], "pT": [P, SEQ], "pick": [2 * E, P]}.items():
                    M[n] = sb(s, "ex_" + n, shape, F32R)
                M["raw"] = [sb(s, f"raw{i}", [P, 4, 512]) for i in range(4)]
                M["hi"] = [sb(s, f"whi{i}", [P, 4, 512], F32R) for i in range(3)]
                M["lo"] = [sb(s, f"wlo{i}", [P, 4, 512], F32R) for i in range(3)]
                M["pool_pieces"] = (2, 6, 10)
                experts(nc, A, ps, T, R, M)
            probe("f", T["f"][:, :, :])
            x1 = sb(moe, "x1b", [P, TT, D])
            g2 = sb(moe, "g2f", [P, D])
            gain = sb(moe, "gain2", [P, D])
            bias = sb(moe, "bias2", [P, D])
            stats = sb(moe, "stats2", [P, 96])
            load_stage(nc, [(g2[:, :], spill[:, 7168:8192]), (gain[:, :], A["ln2_g"][0].partition_broadcast(P)),
                            (bias[:, :], A["ln2_b"][0].partition_broadcast(P)),
                            (x1[:, :, :], spill[:, 0:4096].rearrange("p (t d) -> p t d", t=TT))])
            residual_stage(nc, x1[:, :, :], T["f"][:, :, :], g2[:, :], TT)
            layer_norm_stage(nc, x1[:, :, :], TT, gain[:, :], bias[:, :], stats)
            load_stage(nc, [(spill[:, 0:4096].rearrange("p (t d) -> p t d", t=TT), x1[:, :, :])])
        x = sb(top, "x", [P, TT, D])
        load_stage(nc, [(x[:, :, :], spill[:, 0:4096].rearrange("p (t d) -> p t d", t=TT))])
        probe("x2", x[:, :, :])

        with nc.Fori(0, LAYERS) as l:
            layer(nc, A, ps, bank, T, x, l, sb)
        load_stage(nc, [(out[0].rearrange("(t p) d -> p t d", p=P), x[:, :, :])])


def layer(nc, A, ps, bank, T, x, l, sb):
    S = T["s"]
    ident = S("ident")
    with ExitStack() as lay:
        L = {n: sb(lay, "ly_" + n, shape) for n, shape in {
            "qg": [P, HS], "kg": [P, 3, HS], "fqg": [P, HS], "fkg": [P, HS], "mqg": [P, P], "mkg": [P, P], "fb": [P, 8]}.items()}
        kmT = sb(lay, "kmT", [P, 4, 256])
        vm = sb(lay, "vm", [P, 2, 512])
        hT = sb(lay, "hT3", [P, KD, SEQ])
        oT = sb(lay, "oT", [P, 12, SEQ])
        ss = sb(lay, "ss", [P, 4])
        r = sb(lay, "headr", [P, 100])
        with ExitStack() as s:
            ng, mg = sb(s, "ng", [P, D]), sb(s, "mg", [P, D])
            mem, memT = sb(s, "mem", [P, 2, D]), sb(s, "memT", [P, KD, 256])
            kv = sb(s, "kv", [P, 2, D])
            h = sb(s, "h3", [P, TT, D])
            tmp = sb(s, "tmp3", [P, D])
            load_stage(nc, [(mem[:, :, :], A["mem_2"][0].rearrange("(t p) d -> p t d", p=P)),
                            (ng[:, :], A["norm_g_2"][l].partition_broadcast(P)), (mg[:, :], A["mem_norm_g_2"][l].partition_broadcast(P)),
                            (L["qg"][:, :], A["nsa_q_norm_2"][l].partition_broadcast(P)),
                            (L["kg"][:, :, :], A["nsa_k_norm_2"][l].partition_broadcast(P)),
                            (L["fqg"][:, :], A["fox_q_norm_2"][l].partition_broadcast(P)),
                            (L["fkg"][:, :], A["fox_k_norm_2"][l].partition_broadcast(P)),
                            (L["mqg"][:, :], A["mem_q_norm_2"][l].partition_broadcast(P)),
                            (L["mkg"][:, :], A["mem_k_norm_2"][l].partition_broadcast(P)),
                            (L["fb"][:, :], A["fox_f_bias_2"][l].partition_broadcast(P))])
            with stage(nc, "scaled") as (block, scaled):
                @block.vector
                def _(dve):
                    dve.tensor_scalar(L["qg"][:, :], L["qg"][:, :], HS ** -0.5, None, ALU.mult).then_inc(scaled, 1)
                    dve.tensor_scalar(L["fqg"][:, :], L["fqg"][:, :], HS ** -0.5, None, ALU.mult).then_inc(scaled, 1)
                    dve.tensor_scalar(L["mqg"][:, :], L["mqg"][:, :], P ** -0.5, None, ALU.mult).then_inc(scaled, 1)
                    dve.wait_ge(scaled, 3)
            rms_rows(nc, mem, mem, mg[:, :], tmp, ss, 2)
            rms_rows(nc, h, x, ng[:, :], tmp, ss, TT)
            turn(nc, bank, ident, tiles4(memT, lambda t, c: mem[:, t, c * P:(c + 1) * P], KD, 2)
                 + tiles4(hT, lambda t, c: h[:, t, c * P:(c + 1) * P], KD, TT))
            ring = [sb(s, f"mring{i}", [P, KD, 512]) for i in range(2)]
            w = A["w_mem_kv_2"][l].rearrange("(k p) n -> p k n", p=P)
            ring_gemm(nc, bank, lambda n: w[:, :, n * 512:(n + 1) * 512], lambda n: 512, 2, 2,
                      lambda k, m: memT[:, k, m * P:(m + 1) * P], KD, ring,
                      copy_evac(lambda n, m: kv[:, m, 0:512] if n == 0 else vm[:, m, :]))
            km = kv[:, :, 0:512].rearrange("p t (h s) -> p t h s", h=4)
            head_norms(nc, [(km, [(km, km)], L["mkg"][:, :], P)], h[:, :, :].rearrange("p a b -> p (a b)"), r)
            turn(nc, bank, ident, tiles4(kmT, lambda t, c: kv[:, t, c * P:(c + 1) * P], 4, 2))
        with ExitStack() as zs:
            z = sb(zs, "z", [P, TT, ZW])
            Z = {"z": z, "gate": sb(zs, "gate", [P, TT, 24])}
            with ExitStack() as s:
                ring = [sb(s, f"zring{i}", [P, KD, 512]) for i in range(2)] + [oT[:, 0:KD, :]]
                w = A["w_in_2"][l].rearrange("(k p) n -> p k n", p=P)
                npc = -(-ZW // 512)
                ring_gemm(nc, bank, lambda n: w[:, :, n * 512:min(n * 512 + 512, ZW)], lambda n: min(512, ZW - n * 512), npc, TT,
                          lambda k, m: hT[:, k, m * P:(m + 1) * P], KD, ring,
                          copy_evac(lambda n, m: z[:, m, n * 512:min(n * 512 + 512, ZW)]))

            def cols(a, heads, size=HS):
                return z[:, :, a:a + heads * size].rearrange("p t (h s) -> p t h s", h=heads)

            Z["o"] = [z[:, :, 0:512], z[:, :, 1816:2328], z[:, :, 3872:4384]]
            with ExitStack() as nsa:
                Z["qT"] = sb(nsa, "qT", [P, 4, SEQ])
                for n in ("kcT", "vcT", "ksT", "kwT"):
                    Z[n] = sb(nsa, n, [P, SEQ])
                with ExitStack() as s:
                    qn = sb(s, "qn", [P, TT, 4, 2, HS])
                    sq = sb(s, "sqh", [P, 2048])
                    jobs = [(cols(0, 8), [(cols(g * 256, 4), qn[:, :, :, g, :]) for g in range(2)], L["qg"][:, :], HS)]
                    for a, i in ((768, 1), (1024, 2)):
                        jobs.append((cols(a, 2), [(cols(a, 2), cols(a, 2))], L["kg"][:, i, :], HS))
                    head_norms(nc, jobs, sq, r)
                    qr = qn[:, :, :, :, :].rearrange("p t r g s -> p t (r g) s")
                    rope(nc, T, [qr, cols(512, 2), cols(768, 2), cols(1024, 2)], sq)
                    q2 = qn[:, :, :, :, :].rearrange("p t r g s -> p t r (g s)")
                    groups = tiles4(Z["qT"], lambda t, c: q2[:, t, c, :], 4, TT)
                    for n, a in (("kcT", 512), ("vcT", 640), ("ksT", 768), ("kwT", 1024)):
                        groups.append(([z[:, t, a:a + P] for t in range(TT)], Z[n][:, :]))
                    turn(nc, bank, ident, groups)
                    with stage(nc, "sg") as (block, sg):
                        @block.scalar
                        def _(act):
                            act.activation(Z["gate"][:, :, :], z[:, :, 1280:1304], ACT.Sigmoid).then_inc(sg, 1)
                            act.wait_ge(sg, 1)
                with ExitStack() as s:
                    for n, shape in {"blk": [P, 2, 32, 32], "hid": [P, 2, 2, 32], "hsg": [P, 2, 2, 32], "peT": [P, 2, 32],
                                     "kcr": [32, P], "vc": [P, P], "kc": [P, 32]}.items():
                        Z[n] = sb(s, "cp_" + n, shape)
                    with ExitStack() as s2:
                        L["cw1"] = [oT[:, 0:KD, :].rearrange("p a b -> p (a b)").rearrange("p (l h) -> p l h", h=P),
                                    sb(s2, "cw1", [P, 32, P])[:, :, :]]
                        L["cw2"] = sb(s2, "cw2", [P, 2, HS])
                        L["pe"] = sb(s2, "pe", [32, 2, 2, HS])
                        loads = []
                        for i, name in enumerate("kv"):
                            for g in range(2):
                                w1 = A[f"cmp_w1_{name}_2"][l].rearrange("(l d) h -> d l h", d=HS)
                                loads.append((L["cw1"][i][g * HS:(g + 1) * HS, :, :], w1))
                                loads.append((L["pe"][:, i, g, :], A[f"cmp_pe_{name}_2"][l]))
                            loads.append((L["cw2"][:, i, :], A[f"cmp_w2_{name}_2"][l]))
                        load_stage(nc, loads)
                        compress(nc, ps, T, L, Z)
                    sq = sb(s, "sqc", [P, P])
                    kc4 = Z["kcr"][:, :].rearrange("p (t h s) -> p t h s", t=1, h=2)
                    head_norms(nc, [(kc4, [(kc4, kc4)], L["kg"][0:32, 0, :], HS)], sq, r)
                    turn(nc, bank, ident, [([Z["kcr"][:, :]], Z["kc"][:, :])])
                    Z["cp"] = sb(s, "cp", [P, TT, 256])
                    Z["cpT"] = sb(s, "cpT", [P, 2, SEQ])
                    Z["cm"] = sb(s, "cm", [P, 1, 32])
                    compressed_attention(nc, ps, T, Z)

                def common(s, tag):
                    for n, shape in {"p": [P, 2, SEQ], "pT": [P, 2, SEQ], "nm": [P, 4], "mx": [P, 4], "sum": [P, 4], "rs": [P, 4]}.items():
                        Z[n] = sb(s, f"{tag}_{n}", shape)

                causal = S("causal")
                with ExitStack() as s:
                    common(s, "nsa")
                    units = []
                    for kT, va, b in ((Z["ksT"], 896, 1), (Z["kwT"], 1152, 2)):
                        for h in range(8):
                            g, rr = h // 4, h % 4
                            for i in range(TT):
                                n = (i + 1) * P
                                units.append({
                                    "n": n, "w": HS, "q": Z["qT"][g * HS:(g + 1) * HS, rr, i * P:n], "k": kT[g * HS:(g + 1) * HS, 0:n],
                                    "extra": [(ident, causal, i * P, n)],
                                    "v": [z[:, kb, va + g * HS:va + (g + 1) * HS] for kb in range(i + 1)],
                                    "gate": Z["gate"][:, i, 3 * h + b:3 * h + b + 1], "o": Z["o"][0][:, i, h * HS:(h + 1) * HS]})
                    attention(nc, ps, T, Z, units)
            with ExitStack() as fox:
                fq, fk = sb(fox, "fqT", [P, 4, SEQ]), sb(fox, "fkT", [P, 4, SEQ])
                Z["lf"] = sb(fox, "lf", [P, 2, TT, 8])
                Z["cT"] = sb(fox, "cT", [8, 2, SEQ])
                with ExitStack() as s:
                    sq = sb(s, "sqf", [P, 2048])
                    head_norms(nc, [(cols(1816, 8), [(cols(1816, 8), cols(1816, 8))], L["fqg"][:, :], HS),
                                    (cols(2328, 8), [(cols(2328, 8), cols(2328, 8))], L["fkg"][:, :], HS)], sq, r)
                turn(nc, bank, ident, tiles4(fq, lambda t, c: z[:, t, 1816 + c * P:1816 + (c + 1) * P], 4, TT)
                     + tiles4(fk, lambda t, c: z[:, t, 2328 + c * P:2328 + (c + 1) * P], 4, TT))
                forget_bias(nc, ps, T, Z, L)
                common(fox, "fox")
                units = []
                for h in range(8):
                    lo, hi = HS * (h % 2), HS * (h % 2) + HS
                    pick = ident[0:8, h:h + 1]
                    for i in range(TT):
                        n = (i + 1) * P
                        units.append({
                            "n": n, "w": HS, "q": fq[lo:hi, h // 2, i * P:n], "k": fk[lo:hi, h // 2, 0:n],
                            "extra": [(Z["cT"][:, 0, i * P:n], pick.to_broadcast([8, n]), 0, n),
                                      (pick.to_broadcast([8, P]), Z["cT"][:, 1, 0:n], 0, n), (ident, causal, i * P, n)],
                            "v": [z[:, kb, 2840 + h * HS:2840 + (h + 1) * HS] for kb in range(i + 1)],
                            "gate": None, "o": Z["o"][1][:, i, h * HS:(h + 1) * HS]})
                attention(nc, ps, T, Z, units)
            with ExitStack() as mm:
                mq = sb(mm, "mqT", [P, 4, SEQ])
                common(mm, "mem")
                sq = sb(mm, "sqm", [P, 2048])
                head_norms(nc, [(cols(3872, 4, P), [(cols(3872, 4, P), cols(3872, 4, P))], L["mqg"][:, :], P)], sq, r)
                turn(nc, bank, ident, tiles4(mq, lambda t, c: z[:, t, 3872 + c * P:3872 + (c + 1) * P], 4, TT))
                units = []
                for h in range(4):
                    for i in range(TT):
                        units.append({
                            "n": 256, "w": P, "q": mq[:, h, i * P:(i + 1) * P], "k": kmT[:, h, :], "extra": [],
                            "v": [vm[:, kb, h * P:(h + 1) * P] for kb in range(2)],
                            "gate": None, "o": Z["o"][2][:, i, h * P:(h + 1) * P]})
                attention(nc, ps, T, Z, units)
            with ExitStack() as s:
                Z["sgl"] = sb(s, "sgl", [P, 3, TT, 512])
                gate_outputs(nc, Z)
            groups = []
            for b in range(3):
                groups += tiles4(oT[:, 4 * b:4 * b + 4, :], lambda t, c, b=b: Z["o"][b][:, t, c * P:(c + 1) * P], 4, TT)
            turn(nc, bank, ident, groups)
        with ExitStack() as s:
            U = {"hT": hT, "oT": oT, "u": sb(s, "u", [P, TT, D]), "sg": sb(s, "usg", [P, 2, 512]), "tmp": sb(s, "utmp", [P, 512])}
            uT = sb(s, "uT", [P, KD, SEQ])
            ring = [sb(s, f"uring{i}", [P, KD, 512]) for i in range(3)]
            merge(nc, A, ps, T, U, l, ring)
            turn(nc, bank, ident, tiles4(uT, lambda t, c: U["u"][:, t, c * P:(c + 1) * P], KD, TT))
            w = A["w_out_2"][l].rearrange("(k p) n -> p k n", p=P)
            ring_gemm(nc, bank, lambda n: w[:, :, n * 512:(n + 1) * 512], lambda n: 512, 2, TT,
                      lambda k, m: uT[:, k, m * P:(m + 1) * P], KD, ring,
                      copy_evac(lambda n, m: U["u"][:, m, n * 512:(n + 1) * 512]))
            add_stage(nc, x[:, :, :], U["u"][:, :, :])


_INS = ["x", "c", "ctx", "c_ctx", "ln0_g", "ln0_b", "w_ada", "b_ada", "w_in", "mu_shift", "w0", "w2_decay", "a0", "a2_iclr",
        "g2_gate", "r_k", "k_k", "k_a", "gn_g", "gn_b", "w_fno", "b_fno", "w_out", "ln1_g", "ln1_b", "w_router", "b_router",
        "w1", "b1", "w2", "b2", "ln2_g", "ln2_b", "mem_2", "norm_g_2", "mem_norm_g_2", "w_in_2", "nsa_q_norm_2",
        "nsa_k_norm_2", "cmp_pe_k_2", "cmp_w1_k_2", "cmp_w2_k_2", "cmp_pe_v_2", "cmp_w1_v_2", "cmp_w2_v_2", "fox_q_norm_2",
        "fox_k_norm_2", "fox_f_bias_2", "mem_q_norm_2", "mem_k_norm_2", "w_mem_kv_2", "w_branch_a_2", "w_branch_b_2",
        "w_branch_m_2", "w_out_2"]


def kernel(**inputs):
    import concourse.bacc as _bacc
    from concourse.bass_utils import run_bass_kernel_spmd as _run

    nc = _bacc.Bacc("TRN2", target_bir_lowering=False, num_devices=1)
    arrays, args = {}, {}
    given = {name: np.ascontiguousarray(inputs[name]) for name in _INS}
    given["small"], given["big"] = SMALL, BIG
    for name, a in given.items():
        arrays[f"in_{name}_dram"] = a
        args[name] = nc.dram_tensor(f"in_{name}_dram", a.shape, mybir.dt.from_np(a.dtype), kind="ExternalInput").ap()
    out = nc.dram_tensor("out_0_dram", (1, SEQ, D), F32, kind="ExternalOutput").ap()
    program(nc, args, out)
    r = _run(nc, [arrays], core_ids=[0])
    return r.results[0]["out_0_dram"]
```

```python
from contextlib import ExitStack, contextmanager

import numpy as np

import concourse.bass as bass
from concourse import mybir

F32 = mybir.dt.float32
F32R = mybir.dt.float32r
I32 = mybir.dt.int32
U32 = mybir.dt.uint32
ALU = mybir.AluOpType
ACT = mybir.ActivationFunctionType
AX_X = mybir.AxisListType.X

P = 128
D = 1024
KD = D // P
SEQ = 512
CTX = 256
TT = SEQ // P
ALLT = SEQ + CTX
TA = ALLT // P
GRID_W = 64
GRID_H = SEQ // GRID_W
C = 512
HS = 64
SHIFT = 2048
FN = 512
E = 32
TOPK = 4
CH = 64
NCH = ALLT // CH
LATCH = SEQ // CH
LN_EPS = 1e-5
GN_EPS = 64e-5
RMS_EPS = 1e-6
ALPHA = 2.0 ** 0.25
LIMIT = 7.0
SW_ALPHA = 1.702
DECAY = -float(np.exp(-0.5))
NEG = -1e30
LAYERS = 2
ZW = 4896
MERGE0 = ZW
NCMP = 31


def constants():
    p = np.arange(P)[:, None]
    f = np.arange(P)[None, :]
    same = (p // CH) == (f // CH)
    small = {
        "ident": p == f,
        "upto": p <= f,
        "before": p < f,
        "ones": np.ones((P, P)),
        "iota": np.broadcast_to(f, (P, P)),
        "causal": np.where(f <= p, 0.0, NEG),
        "step": np.full((P, TT), P),
        "eye32": (p % E) == np.arange(E)[None, :],
    }
    mixing = {
        "headones": same,
        "dir0": np.concatenate([same & (p < f), same & (p <= f)] * 2, 1),
        "dir1": np.concatenate([same & (p > f), same & (p >= f)] * 2, 1),
        "restart": np.broadcast_to(np.arange(ALLT) % CH != 0, (P, ALLT)),
        "eye2": (p % CH) == np.arange(CH)[None, :],
    }
    for b in (1, 2, 4, 8, 16, 32):
        low = ((p // (2 * b)) == (f // (2 * b))) & ((p // b) % 2 == 1) & ((f // b) % 2 == 0)
        mixing[f"low{b}"] = low
        mixing[f"up{b}"] = low.T
    t = np.arange(SEQ)
    n = np.arange(32)
    ok = (n[None, :] < NCMP) & (n[None, :] * 16 + 31 <= t[:, None])

    def rows(a):
        return a.reshape(TT, P, -1).transpose(1, 0, 2).reshape(P, -1)

    small["cmpok"] = rows(ok)
    small["cmpadd"] = rows(np.where(ok, 0.0, NEG))
    half = 32
    ang = t[:, None].astype(np.float32) * (np.float32(10000.0) ** (-np.arange(half, dtype=np.float32) / half))
    small["cos"] = rows(np.cos(ang))
    small["sin"] = rows(np.sin(ang))
    k = 2 * np.pi * ((t[:, None] * t[None, :]) % SEQ) / SEQ
    j = np.arange(CH)
    q = 2 * np.pi * ((j[:, None] * j[None, :]) % CH) / CH
    norm = 1.0 / np.sqrt(SEQ * CH)
    big = {
        "dftc": rows(np.cos(k)),
        "dfts": rows(np.sin(k)),
        "chc": np.kron(np.eye(2), np.cos(q) * norm),
        "chs": np.kron(np.eye(2), -np.sin(q) * norm),
    }

    common = sum(a.shape[1] for a in small.values())
    small.update(mixing)

    def pack(tables):
        at, where, parts = 0, {}, []
        for name, a in tables.items():
            a = np.asarray(a, np.float32)
            where[name] = (at, a.shape[1])
            at += a.shape[1]
            parts.append(a)
        return np.ascontiguousarray(np.concatenate(parts, 1)), where

    return pack(small), pack(big), common


(SMALL, SMALL_AT), (BIG, BIG_AT), COMMON = constants()


class Chain:

    def __init__(self, eng, sem):
        self.eng, self.sem, self.n = eng, sem, 0

    def __call__(self, ins):
        ins.then_inc(self.sem, 1)
        self.n += 1
        self.eng.wait_ge(self.sem, self.n)


@contextmanager
def stage(nc, *names):
    with ExitStack() as keep:
        sems = [keep.enter_context(nc.semaphore(n)) for n in names]
        with nc.Block() as block:
            yield (block, *sems)
        for s in sems:
            nc.sync.sem_clear(s)
        nc.all_engine_barrier()


def bc(ap, axis, n):
    ap = ap.unsqueeze(axis)
    shape = list(ap.shape)
    shape[axis] = n
    return ap.to_broadcast(shape)


def turn(nc, bank, ident, groups):
    with stage(nc, "turned", "evac_v", "evac_a") as (block, turned, evac_v, evac_a):
        @block.tensor
        def _(pe):
            for g, (srcs, _) in enumerate(groups):
                if g >= 4:
                    pe.wait_ge(evac_v if g % 2 == 0 else evac_a, (g - 4) // 2 + 1)
                at = 0
                for s in srcs:
                    n, m = s.shape[0], s.shape[1]
                    last = pe.transpose(bank[g % 4][0:m, at:at + n], s, ident[0:n, 0:n])
                    at += n
                last.then_inc(turned, 1)

        def copies(eng, g):
            dst = groups[g][1]
            return dst, bank[g % 4][0:dst.shape[0], 0:dst.size() // dst.shape[0]]

        @block.vector
        def _(dve):
            for g in range(0, len(groups), 2):
                dve.wait_ge(turned, g + 1)
                dst, src = copies(dve, g)
                dve.tensor_copy(dst, src if dst.ndim == 2 else src.rearrange("p (a b) -> p a b", a=dst.shape[1])).then_inc(evac_v, 1)

        @block.scalar
        def _(act):
            for g in range(1, len(groups), 2):
                act.wait_ge(turned, g + 1)
                dst, src = copies(act, g)
                act.activation(dst, src if dst.ndim == 2 else src.rearrange("p (a b) -> p a b", a=dst.shape[1]), ACT.Copy).then_inc(evac_a, 1)


def turn_split(nc, bank, ident, groups, hi, lo):
    with stage(nc, "turned", "hi_done", "lo_done") as (block, turned, hi_done, lo_done):
        @block.tensor
        def _(pe):
            for g, (srcs, _) in enumerate(groups):
                if g >= 4:
                    pe.wait_ge(lo_done, g - 3)
                for i, s in enumerate(srcs):
                    last = pe.transpose(bank[g % 4][:, i * P:(i + 1) * P], s, ident)
                last.then_inc(turned, 1)

        @block.scalar
        def _(act):
            for g in range(len(groups)):
                act.wait_ge(turned, g + 1)
                act.activation(hi[:, g, :], bank[g % 4][:, :], ACT.Copy).then_inc(hi_done, 1)

        @block.vector
        def _(dve):
            for g in range(len(groups)):
                dve.wait_ge(hi_done, g + 1)
                dve.tensor_tensor(lo[:, g, :], bank[g % 4][:, :], hi[:, g, :].bitcast(F32), ALU.subtract).then_inc(lo_done, 1)


def layer_norm_stage(nc, x, n, gain, bias, stats, eps=LN_EPS):
    mv = stats[:, 0:2 * n].rearrange("p (t s) -> p t s", s=2)
    six = stats[:, 16:16 + 12 * n].rearrange("p (t h s) -> p t h s", h=2, s=6)
    with stage(nc, "dve_step", "var_ready", "root_ready") as (block, dve_step, var_ready, root_ready):
        @block.vector
        def _(dve):
            done = Chain(dve, dve_step)
            for t in range(n):
                for h in range(2):
                    done(dve.bn_stats(six[:, t, h, :], x[:, t, h * 512:(h + 1) * 512]))
                done(dve.bn_aggr(mv[:, t, :], six[:, t, :, :]))
            dve.tensor_scalar(mv[:, :, 1], mv[:, :, 1], eps, None, ALU.add).then_inc(var_ready, 1)
            dve.wait_ge(root_ready, 1)
            done(dve.reciprocal(mv[:, :, 1], mv[:, :, 1]))
            for t in range(n):
                done(dve.tensor_scalar(x[:, t, :], x[:, t, :], mv[:, t, 0:1], mv[:, t, 1:2], ALU.subtract, ALU.mult))
            done(dve.tensor_tensor(x[:, 0:n, :], x[:, 0:n, :], bc(gain, 1, n), ALU.mult))
            done(dve.tensor_tensor(x[:, 0:n, :], x[:, 0:n, :], bc(bias, 1, n), ALU.add))

        @block.scalar
        def _(act):
            act.wait_ge(var_ready, 1)
            act.activation(mv[:, :, 1], mv[:, :, 1], ACT.Sqrt).then_inc(root_ready, 1)


def modulation(nc, A, bank, T, ring):
    nb = len(ring)
    mod_names = [f"ada_in{i}" for i in range(nb)]
    with stage(nc, *mod_names, "small_in", "c_in", "bias_in", "sig_ready", "wide_ready", "prod", "prod_out", "dve_step") as sems:
        block, ada_in = sems[0], sems[1:1 + nb]
        small_in, c_in, bias_in, sig_ready, wide_ready, prod, prod_out, dve_step = sems[1 + nb:]
        w = A["w_ada"][0].rearrange("(k p) n -> p k n", p=P)
        jobs = [(n, v) for n in range(12) for v in ((0, 1) if n < 4 else (0,))]
        last_job = {n: max(i for i, (m, _) in enumerate(jobs) if m == n) for n in range(12)}

        @block.sync
        def _(sp):
            sp.dma_start(T["c2"][:, 0:KD], A["c"][0].rearrange("(k p) -> p k", p=P)).then_inc(c_in, 16)
            sp.dma_start(T["c2"][:, KD:2 * KD], A["c_ctx"].rearrange("(k p) -> p k", p=P)).then_inc(c_in, 16)
            sp.dma_start(T["adab"][:, :], A["b_ada"]).then_inc(bias_in, 16)
            for n in range(12):
                if n >= nb:
                    sp.wait_ge(prod, last_job[n - nb] + 1)
                sp.dma_start(ring[n % nb][:, :, :], w[:, :, n * 512:(n + 1) * 512]).then_inc(ada_in[n % nb], 16)

        @block.scalar
        def _(act):
            act.dma_start(T["small"][:, :], A["small"][:, 0:COMMON]).then_inc(small_in, 16)
            act.dma_start(T["mixing"][:, :], A["small"][:, COMMON:SMALL.shape[1]]).then_inc(small_in, 16)
            act.dma_start(T["xn"][:, 0:TT, :], A["x"][0].rearrange("(t p) d -> p t d", p=P)).then_inc(small_in, 16)
            act.dma_start(T["xn"][:, TT:TA, :], A["ctx"][0].rearrange("(t p) d -> p t d", p=P)).then_inc(small_in, 16)
            act.dma_start(T["gain"][:, :], A["ln0_g"].partition_broadcast(P)).then_inc(small_in, 16)
            act.dma_start(T["bias"][:, :], A["ln0_b"].partition_broadcast(P)).then_inc(small_in, 16)
            act.wait_ge(c_in, 32)
            act.activation(T["csig"][:, :], T["c2"][:, :], ACT.Sigmoid).then_inc(sig_ready, 1)
            for i, (n, v) in enumerate(jobs):
                act.wait_ge(prod, i + 1)
                dst = (T["modc"] if v else T["modb"])[:, n * 512:(n + 1) * 512]
                plus = 1.0 if n // 2 in (1, 4) else 0.0
                act.activation(dst, bank[i % 4][:, :], ACT.Copy, bias=plus).then_inc(prod_out, 1)
            act.wait_ge(small_in, 16 * 6)

        @block.vector
        def _(dve):
            done = Chain(dve, dve_step)
            done(dve.memset(T["onerow"][:, :], 1.0))
            dve.wait_ge(sig_ready, 1)
            done(dve.tensor_tensor(T["csig"][:, :], T["csig"][:, :], T["c2"][:, :], ALU.mult))
            dve.tensor_copy(T["cwide"][:, :, :], bc(T["csig"][:, :], 2, P)).then_inc(wide_ready, 1)

        @block.tensor
        def _(pe):
            pe.wait_ge(wide_ready, 1)
            pe.wait_ge(bias_in, 16)
            for i, (n, v) in enumerate(jobs):
                if v == 0:
                    pe.wait_ge(ada_in[n % nb], 16 * (n // nb + 1))
                if i >= 4:
                    pe.wait_ge(prod_out, i - 3)
                for k in range(KD):
                    pe.matmul(bank[i % 4][:, :], T["cwide"][:, KD * v + k, :], ring[n % nb][:, k, :], start=(k == 0), stop=False)
                pe.matmul(bank[i % 4][:, :], T["onerow"][:, :], T["adab"][:, n * 512:(n + 1) * 512],
                          start=False, stop=True).then_inc(prod, 1)


def modulate_stage(nc, dst, src, n, scale, shift):
    with stage(nc, "dve_step") as (block, dve_step):
        @block.vector
        def _(dve):
            done = Chain(dve, dve_step)
            done(dve.tensor_tensor(dst, src, bc(scale, 1, n), ALU.mult))
            done(dve.tensor_tensor(dst, dst, bc(shift, 1, n), ALU.add))


def project_in(nc, A, bank, T, hT, ring):
    nb = len(ring)
    names = [f"w_in{i}" for i in range(nb)]
    tiles = (SHIFT + FN) // P
    with stage(nc, *names, "mu_in", "mu_ready", "lat", "ctx", "padded", "kept", "dve_step", "padded_used", "shift_done") as sems:
        block, w_in = sems[0], sems[1:1 + nb]
        mu_in, mu_ready, lat, ctx, padded, kept, dve_step, padded_used, shift_done = sems[1 + nb:]
        w = A["w_in"][0].rearrange("(k p) n -> p k n", p=P)
        nshift = SHIFT // P

        @block.sync
        def _(sp):
            sp.dma_start(T["mu"][:, 0, :], A["mu_shift"][0].rearrange("(j p) -> p j", p=P)).then_inc(mu_in, 16)
            for n in range(tiles // 2):
                if n >= nb:
                    sp.wait_ge(lat, 2 * (n - nb) + 2)
                    if 2 * (n - nb) + 2 <= nshift:
                        sp.wait_ge(ctx, 2 * (n - nb) + 2)
                sp.dma_start(ring[n % nb][:, :, 0:256], w[:, :, n * 256:(n + 1) * 256]).then_inc(w_in[n % nb], 16)

        @block.tensor
        def _(pe):
            for j in range(tiles):
                if j % 2 == 0:
                    pe.wait_ge(w_in[j // 2 % nb], 16 * (j // 2 // nb + 1))
                if j >= 2:
                    pe.wait_ge(kept, j - 1)
                at = (j % 2) * P
                for k in range(KD):
                    last = pe.matmul(bank[2 * (j % 2)][:, :], ring[j // 2 % nb][:, k, at:at + P], hT[:, k, 0:SEQ],
                                     start=(k == 0), stop=(k == KD - 1))
                last.then_inc(lat, 1)
                if j < nshift:
                    for k in range(KD):
                        last = pe.matmul(bank[2 * (j % 2) + 1][:, 0:CTX], ring[j // 2 % nb][:, k, at:at + P],
                                         hT[:, k, SEQ:ALLT], start=(k == 0), stop=(k == KD - 1))
                    last.then_inc(ctx, 1)

        @block.scalar
        def _(act):
            act.wait_ge(mu_ready, 1)
            for j in range(tiles):
                g, c = T["padg"][j % 2], T["padc"][j % 2]
                act.wait_ge(lat, j + 1)
                src = bank[2 * (j % 2)][:, :]
                if j >= nshift:
                    act.activation(T["fT"][:, j - nshift, :], src, ACT.Copy).then_inc(kept, 1)
                    continue
                act.wait_ge(ctx, j + 1)
                if j >= 2:
                    act.wait_ge(padded_used, j - 1)
                act.activation(g[:, 1:1 + GRID_H, 1:1 + GRID_W], src.rearrange("p (a b) -> p a b", b=GRID_W), ACT.Copy)
                act.activation(c[:, 1:1 + CTX], bank[2 * (j % 2) + 1][:, 0:CTX], ACT.Copy).then_inc(padded, 1)
                act.activation(T["mT"][:, j, 0:SEQ], src, ACT.Copy, scale=T["mu"][:, 1, j:j + 1])
                act.activation(T["mT"][:, j, SEQ:ALLT], bank[2 * (j % 2) + 1][:, 0:CTX], ACT.Copy,
                               scale=T["mu"][:, 1, j:j + 1]).then_inc(kept, 1)

        @block.vector
        def _(dve):
            done = Chain(dve, dve_step)
            for i in range(2):
                done(dve.memset(T["padg"][i][:, :, :], 0.0))
                done(dve.memset(T["padc"][i][:, :], 0.0))
            dve.wait_ge(mu_in, 16)
            done(dve.tensor_scalar(T["mu"][:, 2, :], T["mu"][:, 0, :], 0.25, None, ALU.mult))
            done(dve.tensor_scalar(T["mu"][:, 3, :], T["mu"][:, 0, :], 0.5, None, ALU.mult))
            dve.tensor_scalar(T["mu"][:, 1, :], T["mu"][:, 0, :], -1.0, 1.0, ALU.mult, ALU.add).then_inc(mu_ready, 1)
            for j in range(nshift):
                g, c = T["padg"][j % 2], T["padc"][j % 2]
                nb1 = T["nbr"][:, 0:SEQ].rearrange("p (a b) -> p a b", b=GRID_W)
                nb2 = T["nbr"][:, SEQ:2 * SEQ].rearrange("p (a b) -> p a b", b=GRID_W)
                nc1 = T["nbr"][:, 2 * SEQ:2 * SEQ + CTX]
                dve.wait_ge(padded, j + 1)
                dve.tensor_tensor(nc1, c[:, 0:CTX], c[:, 2:2 + CTX], ALU.add)
                dve.tensor_tensor(nb1, g[:, 0:GRID_H, 1:1 + GRID_W], g[:, 2:2 + GRID_H, 1:1 + GRID_W], ALU.add)
                done(dve.tensor_tensor(nb2, g[:, 1:1 + GRID_H, 0:GRID_W], g[:, 1:1 + GRID_H, 2:2 + GRID_W], ALU.add))
                dve.tensor_tensor(nb1, nb1, nb2, ALU.add).then_inc(padded_used, 1)
                dve.wait_ge(kept, j + 1)
                dve.wait_ge(padded_used, j + 1)
                dve.scalar_tensor_tensor(out=T["mT"][:, j, SEQ:ALLT], in0=nc1, scalar=T["mu"][:, 3, j:j + 1],
                                         in1=T["mT"][:, j, SEQ:ALLT], op0=ALU.mult, op1=ALU.add)
                done(dve.scalar_tensor_tensor(out=T["mT"][:, j, 0:SEQ], in0=T["nbr"][:, 0:SEQ], scalar=T["mu"][:, 2, j:j + 1],
                                              in1=T["mT"][:, j, 0:SEQ], op0=ALU.mult, op1=ALU.add))


def rwkv_params(nc, A, T):
    with stage(nc, "par_in", "squashed") as (block, par_in, squashed):
        @block.sync
        def _(sp):
            n = 0
            for i, name in enumerate(("w0", "a0", "r_k")):
                for d in range(2):
                    v = A[name][0, d] if name != "r_k" else A[name][0, d].rearrange("h n -> (h n)")
                    sp.dma_start(T["par"][:, :, 2 * i + d], v.rearrange("(c p) -> p c", p=P)).then_inc(par_in, 16)
                    n += 1
            for i, name in enumerate(("k_k", "k_a")):
                sp.dma_start(T["par"][:, :, 6 + i], A[name][0].rearrange("(c p) -> p c", p=P)).then_inc(par_in, 16)
                n += 1
            sp.dma_start(T["w2"][:, :], A["w2_decay"][0].rearrange("d r c -> (d r) c")).then_inc(par_in, 16)
            sp.dma_start(T["a2"][:, :], A["a2_iclr"][0].rearrange("d r c -> (d r) c")).then_inc(par_in, 16)
            sp.dma_start(T["g2"][:, :, :], A["g2_gate"][0].rearrange("d r c -> r d c")).then_inc(par_in, 16)
            sp.dma_start(T["gng"][:, :], A["gn_g"][0].partition_broadcast(P)).then_inc(par_in, 16)
            sp.dma_start(T["gnb"][:, :], A["gn_b"][0].partition_broadcast(P)).then_inc(par_in, 16)
            n += 5
            sp.wait_ge(par_in, 16 * n)

        @block.scalar
        def _(act):
            act.activation(T["mT"][:, 12, :], T["mT"][:, 12, :], ACT.Tanh).then_inc(squashed, 1)
            act.activation(T["mT"][:, 14:16, 0:SEQ], T["mT"][:, 14:16, 0:SEQ], ACT.Sigmoid).then_inc(squashed, 1)
            act.wait_ge(squashed, 2)


def rwkv_prepare(nc, ps, T, W, c):
    S = T["s"]
    r, k = T["mT"][:, c, :], T["mT"][:, c + 4, :]
    par = W["par"]
    with stage(nc, "cur", "low", "sig", "sq_in", "sumsq", "capped", "root", "exp_in", "exps", "rk_ready", "rk_sum",
               "dve_step", "act_step") as (
            block, cur, low, sig, sq_in, sumsq, capped, root, exp_in, exps, rk_ready, rk_sum, dve_step, act_step):
        @block.gpsimd
        def _(pool):
            pool.tensor_copy(W["w2"][:, :], T["w2"][:, bass.ts(c, P)]).then_inc(cur, 1)
            pool.tensor_copy(W["a2"][:, :], T["a2"][:, bass.ts(c, P)]).then_inc(cur, 1)
            pool.tensor_copy(par[:, :], T["par"][:, c, :]).then_inc(cur, 1)
            pool.tensor_copy(W["v"][:, :], T["mT"][:, c + 8, :]).then_inc(cur, 1)
            pool.wait_ge(cur, 4)

        @block.tensor
        def _(pe):
            pe.wait_ge(cur, 2)
            for d in range(2):
                lo, hi = HS * d, HS * d + HS
                for i, (wt, row) in enumerate(((W["w2"], 12), (W["a2"], 13))):
                    b = 4 * d + 2 * i
                    pe.matmul(ps[:, b, :], wt[lo:hi, :], T["mT"][lo:hi, row, 0:SEQ], start=True, stop=True)
                    pe.matmul(ps[:, b + 1, 0:CTX], wt[lo:hi, :], T["mT"][lo:hi, row, SEQ:ALLT],
                              start=True, stop=True).then_inc(low, 1)
            pe.wait_ge(sq_in, 1)
            pe.wait_ge(sig, 1)
            pe.matmul(ps[:, 0, :], S("headones"), W["t0"][:, 0:SEQ], start=True, stop=True)
            pe.matmul(ps[:, 1, 0:CTX], S("headones"), W["t0"][:, SEQ:ALLT], start=True, stop=True).then_inc(sumsq, 1)
            pe.wait_ge(sig, 2)
            sel = S("headones").rearrange("p (h n) -> p h n", h=2)[:, :, 0]
            for d in range(2):
                pe.wait_ge(rk_ready, d + 1)
                for tt in range(TT):
                    at = (tt * 2 + d) * 2
                    last = pe.matmul(ps[:, 2, at:at + 2], W["rk"][:, d, tt * P:(tt + 1) * P], sel, start=True, stop=True)
            last.then_inc(rk_sum, 1)

        def wide(b):
            return ps[:, b:b + 2, :].rearrange("p a b -> p (a b)")[:, 0:ALLT]

        @block.scalar
        def _(act):
            act.wait_ge(cur, 3)
            for d in range(2):
                act.wait_ge(low, 2 * d + 1)
                act.activation(W["lw"][:, d, :], wide(4 * d), ACT.Sigmoid, bias=par[:, d:d + 1]).then_inc(sig, 1)
                act.wait_ge(low, 2 * d + 2)
                act.activation(W["a"][:, d, :], wide(4 * d + 2), ACT.Sigmoid, bias=par[:, 2 + d:3 + d]).then_inc(sig, 1)
            act.wait_ge(capped, 1)
            act.activation(W["t0"][:, :], W["t0"][:, :], ACT.Sqrt).then_inc(root, 1)
            act.wait_ge(exp_in, 1)
            act.activation(W["pc"][:, :, :], W["tot"][:, :, :], ACT.Exp)
            for d in range(2):
                act.activation(W["e1"][:, d, :], W["e1"][:, d, :], ACT.Exp)
                act.activation(W["lw"][:, d, :], W["ci"][:, d, :], ACT.Exp, scale=-1.0).then_inc(act_step, 1)
                act.wait_ge(act_step, d + 1)
                act.activation(W["ci"][:, d, :], W["ci"][:, d, :], ACT.Exp).then_inc(exps, 1)
            act.wait_ge(rk_sum, 1)
            act.activation(W["bon"][:, :], ps[:, 2, 0:16], ACT.Copy).then_inc(act_step, 1)
            act.wait_ge(act_step, 3)

        @block.vector
        def _(dve):
            done = Chain(dve, dve_step)
            dve.wait_ge(cur, 3)
            done(dve.tensor_scalar(W["kk"][:, :], k, par[:, 6:7], None, ALU.mult))
            dve.tensor_tensor(W["t0"][:, :], W["kk"][:, :], W["kk"][:, :], ALU.mult).then_inc(sq_in, 1)
            for d in range(2):
                dve.wait_ge(sig, 2 * d + 1)
                lw, ci = W["lw"][:, d, :], W["ci"][:, d, :]
                tot = W["tot"][:, d, :]
                done(dve.tensor_scalar(lw, lw, DECAY, None, ALU.mult))
                done(dve.tensor_tensor_scan(ci, S("restart"), lw, 0.0, ALU.mult, ALU.add))
                done(dve.tensor_copy(tot, ci.rearrange("p (n s) -> p n s", s=CH)[:, :, CH - 1]))
                if d == 1:
                    done(dve.tensor_tensor(ci, lw, ci, ALU.subtract))
                    v3 = ci.rearrange("p (n s) -> p n s", s=CH)
                    done(dve.tensor_tensor(v3, v3, bc(tot, 2, CH), ALU.add))
                done(dve.tensor_tensor(W["e1"][:, d, :], ci, lw, ALU.subtract))
            dve.wait_ge(sumsq, 1)
            dve.tensor_scalar(W["t0"][:, :], wide(0), 1e-24, None, ALU.max).then_inc(capped, 1)
            dve.wait_ge(root, 1)
            dve.reciprocal(W["t0"][:, :], W["t0"][:, :]).then_inc(exp_in, 1)
            dve.wait_ge(exp_in, 1)
            done(dve.tensor_tensor(W["kk"][:, :], W["kk"][:, :], W["t0"][:, :], ALU.mult))
            dve.wait_ge(sig, 4)
            for d in range(2):
                a, kd = W["a"][:, d, :], W["kd"][:, d, :]
                done(dve.tensor_scalar(kd, a, -1.0, par[:, 7:8], ALU.add, ALU.mult))
                done(dve.scalar_tensor_tensor(out=kd, in0=kd, scalar=1.0, in1=k, op0=ALU.add, op1=ALU.mult))
                dve.scalar_tensor_tensor(out=W["rk"][:, d, :], in0=kd[:, 0:SEQ], scalar=par[:, 4 + d:5 + d],
                                         in1=r[:, 0:SEQ], op0=ALU.mult, op1=ALU.mult).then_inc(rk_ready, 1)
                done(dve.tensor_tensor(a, a, W["kk"][:, :], ALU.mult))
            for d in range(2):
                dve.wait_ge(exps, d + 1)
                ar = W["ar"][:, d, :, :, :]

                def tiles(x):
                    return x.rearrange("p (t s) -> p t s", s=P)

                done(dve.scalar_tensor_tensor(out=ar[:, :, 0, :], in0=tiles(W["kk"][:, :]), scalar=-1.0,
                                              in1=tiles(W["e1"][:, d, :]), op0=ALU.mult, op1=ALU.mult))
                done(dve.tensor_tensor(ar[:, :, 1, :], tiles(r), tiles(W["ci"][:, d, :]), ALU.mult))
                done(dve.tensor_tensor(W["bt"][:, d, :], W["a"][:, d, :], W["lw"][:, d, :], ALU.mult))
                done(dve.tensor_tensor(W["kt"][:, d, :], W["kd"][:, d, :], W["lw"][:, d, :], ALU.mult))


def rwkv_chunks(nc, ps, T, W):
    S = T["s"]
    levels = (2, 4, 8, 16, 32)
    names = []
    for s in range(2):
        names += [f"scores{s}", f"masked{s}", f"near{s}", f"start{s}", f"y_prod{s}", f"y_out{s}", f"x_prod{s}", f"x_out{s}",
                  f"akv{s}", f"akv_out{s}", f"wu{s}", f"wu_out{s}", f"last{s}", f"last_v{s}", f"last_a{s}"]
    with stage(nc, *names, "dve_step") as sems:
        block, dve_step = sems[0], sems[-1]
        q = [dict(zip(("scores", "masked", "near", "start", "y_prod", "y_out", "x_prod", "x_out", "akv", "akv_out",
                       "wu", "wu_out", "last", "last_v", "last_a"), sems[1 + 15 * s:16 + 15 * s])) for s in range(2)]
        nq, nl = TA // 2, len(levels)

        def units(g):
            return [(u, 2 * g + u // 2, u % 2) for u in range(4)]

        @block.tensor
        def _(pe):
            for g in range(nq):
                for d in range(2):
                    if g:
                        pe.wait_ge(q[d]["last_v"], g)
                        pe.wait_ge(q[d]["last_a"], min(g, TT // 2))
                    for u, tt, h in units(g):
                        lo, hi = HS * h, HS * h + HS
                        tk = slice(tt * P, (tt + 1) * P)
                        both = W["ar"][lo:hi, d, tt, :, :].rearrange("p a b -> p (a b)")
                        pe.matmul(ps[:, 4 * d + u, 0:256], W["kt"][lo:hi, d, tk], both, start=True, stop=True)
                        last = pe.matmul(ps[:, 4 * d + u, 256:512], W["bt"][lo:hi, d, tk], both, start=True, stop=True)
                    last.then_inc(q[d]["scores"], 1)
                for d in range(2):
                    pe.wait_ge(q[d]["masked"], g + 1)
                    for u, tt, h in units(g):
                        lo, hi = HS * h, HS * h + HS
                        last = pe.matmul(ps[:, 4 * d + h, u // 2 * P:(u // 2 + 1) * P], W["ar"][lo:hi, d, tt, 0, :],
                                         W["bt"][lo:hi, d, tt * P:(tt + 1) * P], start=True, stop=True)
                    last.then_inc(q[d]["near"], 1)
                for l in range(nl):
                    for d in range(2):
                        pe.wait_ge(q[d]["start"], g + 1)
                        if g * nl + l:
                            pe.wait_ge(q[d]["x_out"], g * nl + l)
                        for u in range(4):
                            last = pe.matmul(ps[:, 4 * d + 1, u * P:(u + 1) * P], W["m"][:, d, u, 256:384],
                                             W["x"][:, d, u, :], start=True, stop=True)
                        last.then_inc(q[d]["y_prod"], 1)
                    for d in range(2):
                        pe.wait_ge(q[d]["y_out"], g * nl + l + 1)
                        for u in range(4):
                            if l < nl - 1:
                                pe.matmul(ps[:, 4 * d + 2, u * P:(u + 1) * P], W["xt"][:, d, u, :], W["y"][:, d, u, :],
                                          start=True, stop=True)
                            last = pe.matmul(ps[:, 4 * d + 3, u * P:(u + 1) * P], W["y"][:, d, u, :], W["xt"][:, d, u, :],
                                             start=True, stop=True)
                        last.then_inc(q[d]["x_prod"], 1)
                for d in range(2):
                    for u, tt, h in units(g):
                        last = pe.matmul(ps[:, 4 * d, u * HS:(u + 1) * HS], W["m"][:, d, u, 0:128],
                                         W["vrow"][:, tt, h * HS:(h + 1) * HS], start=True, stop=True)
                    last.then_inc(q[d]["akv"], 1)
                for d in range(2):
                    pe.wait_ge(q[d]["x_out"], (g + 1) * nl)
                    pe.wait_ge(q[d]["akv_out"], g + 1)
                    for u in range(4):
                        last = pe.matmul(ps[:, 4 * d + 1, u * P:(u + 1) * P], W["xt"][:, d, u, :], W["rhs"][:, d, u, :],
                                         start=True, stop=True)
                    last.then_inc(q[d]["wu"], 1)
                for d in range(2):
                    pe.wait_ge(q[d]["wu_out"], g + 1)
                    for u, tt, h in units(g):
                        lo, hi = HS * h, HS * h + HS
                        w, u2 = W["wu"][:, d, u, 0:HS], W["wu"][:, d, u, HS:P]
                        vr = W["vrow"][:, tt, lo:hi]
                        if 2 * g < TT:
                            pe.matmul(ps[lo:hi, 4 * d + 2, (u // 2) * P:(u // 2 + 1) * P], w, W["m"][:, d, u, 384:512],
                                      start=True, stop=True)
                            pe.matmul(ps[:, 4 * d + 3, u * HS:(u + 1) * HS], W["m"][:, d, u, 384:512], u2, start=True, stop=False)
                            pe.matmul(ps[:, 4 * d + 3, u * HS:(u + 1) * HS], W["m"][:, d, u, 128:256], vr, start=False, stop=True)
                        for c2 in range(2):
                            a, b = CH * c2, CH * c2 + CH
                            at = (u // 2) * HS
                            bk = 4 * d + c2
                            br, kr = W["brow"][a:b, d, tt, lo:hi], W["krow"][a:b, d, tt, lo:hi]
                            pe.matmul(ps[lo:hi, bk, at:at + HS], w[a:b, :], br, start=True, stop=True)
                            pe.matmul(ps[lo:hi, bk, P + at:P + at + HS], br, u2[a:b, :], start=True, stop=False)
                            last = pe.matmul(ps[lo:hi, bk, P + at:P + at + HS], kr, vr[a:b, :], start=False, stop=True)
                    last.then_inc(q[d]["last"], 1)

        @block.scalar
        def _(act):
            for g in range(nq):
                for l in range(nl):
                    for d in range(2):
                        act.wait_ge(q[d]["y_prod"], g * nl + l + 1)
                        act.activation(W["y"][:, d, :, :], ps[:, 4 * d + 1, :].rearrange("p (u s) -> p u s", u=4),
                                       ACT.Copy).then_inc(q[d]["y_out"], 1)
                for d in range(2):
                    act.wait_ge(q[d]["akv"], g + 1)
                    act.activation(W["rhs"][:, d, :, 0:HS],
                                   W["arow"][:, d, 2 * g:2 * g + 2, :].rearrange("p t (h s) -> p (t h) s", h=2), ACT.Copy)
                    act.activation(W["rhs"][:, d, :, HS:P], ps[:, 4 * d, 0:256].rearrange("p (u s) -> p u s", u=4),
                                   ACT.Copy).then_inc(q[d]["akv_out"], 1)
                for d in range(2):
                    act.wait_ge(q[d]["wu"], g + 1)
                    act.activation(W["wu"][:, d, :, :], ps[:, 4 * d + 1, :].rearrange("p (u s) -> p u s", u=4),
                                   ACT.Copy).then_inc(q[d]["wu_out"], 1)
                for d in range(2):
                    act.wait_ge(q[d]["last"], g + 1)
                    if 2 * g < TT:
                        act.activation(W["yr"][:, 2 * g:2 * g + 2, d, :],
                                       ps[:, 4 * d + 3, 0:256].rearrange("p (t s) -> p t s", t=2), ACT.Copy).then_inc(q[d]["last_a"], 1)

        @block.vector
        def _(dve):
            done = Chain(dve, dve_step)
            for g in range(nq):
                for d in range(2):
                    lowm, upm = ("low", "up") if d == 0 else ("up", "low")
                    dve.wait_ge(q[d]["scores"], g + 1)
                    dve.tensor_tensor(W["m"][:, d, :, :], ps[:, 4 * d:4 * d + 4, :], bc(S(f"dir{d}"), 1, 4),
                                      ALU.mult).then_inc(q[d]["masked"], 1)
                    done(dve.tensor_copy(W["x"][:, d, :, :], bc(S("ident"), 1, 4)))
                    done(dve.tensor_copy(W["xt"][:, d, :, :], bc(S("ident"), 1, 4)))
                    dve.wait_ge(q[d]["masked"], g + 1)
                    done(dve.copy_predicated(W["xt"][:, d, :, :], bc(S(f"{upm}1").bitcast(U32), 1, 4), W["m"][:, d, :, 256:384]))
                for d in range(2):
                    lowm, upm = ("low", "up") if d == 0 else ("up", "low")
                    dve.wait_ge(q[d]["near"], g + 1)
                    for h in range(2):
                        last = dve.copy_predicated(W["x"][:, d, h:4:2, :], bc(S(f"{lowm}1").bitcast(U32), 1, 2),
                                                   ps[:, 4 * d + h, 0:256].rearrange("p (u s) -> p u s", u=2))
                    last.then_inc(q[d]["start"], 1)
                for l, b in enumerate(levels):
                    for d in range(2):
                        lowm, upm = ("low", "up") if d == 0 else ("up", "low")
                        dve.wait_ge(q[d]["x_prod"], g * nl + l + 1)
                        if l < nl - 1:
                            done(dve.copy_predicated(W["x"][:, d, :, :], bc(S(f"{lowm}{b}").bitcast(U32), 1, 4),
                                                     ps[:, 4 * d + 2, :].rearrange("p (u s) -> p u s", u=4)))
                        dve.copy_predicated(W["xt"][:, d, :, :], bc(S(f"{upm}{b}").bitcast(U32), 1, 4),
                                            ps[:, 4 * d + 3, :].rearrange("p (u s) -> p u s", u=4)).then_inc(q[d]["x_out"], 1)
                for d in range(2):
                    dve.wait_ge(q[d]["last"], g + 1)
                    if 2 * g < TT:
                        done(dve.tensor_tensor(W["qt"][:, d, 2 * g:2 * g + 2, :],
                                               ps[:, 4 * d + 2, 0:256].rearrange("p (t s) -> p t s", t=2),
                                               W["ar"][:, d, 2 * g:2 * g + 2, 1, :], ALU.add))
                    for c2 in range(2):
                        last = dve.tensor_tensor(W["gt"][:, d, 4 * g + c2:4 * g + 4:2, :],
                                                 ps[:, 4 * d + c2, 0:P].rearrange("p (n s) -> p n s", n=2),
                                                 bc(S("eye2"), 1, 2), ALU.add)
                        mine = slice(4 * g + c2, 4 * g + 4, 2)
                        last = dve.tensor_tensor(W["hp"][:, d, mine, :], ps[:, 4 * d + c2, P:2 * P].rearrange("p (n s) -> p n s", n=2),
                                                 bc(W["pc"][:, d, mine], 2, HS), ALU.mult)
                    last.then_inc(q[d]["last_v"], 1)


def rwkv_scan(nc, ps, T, W):
    order = [[LATCH + i for i in range(NCH - LATCH)] + list(range(LATCH)),
             [NCH - 1 - i for i in range(NCH - LATCH)] + [LATCH - 1 - i for i in range(LATCH)]]
    first = NCH - LATCH
    with stage(nc, "zeroed", "moved", "state", "seen", "added") as (block, zeroed, moved, state, seen, added):
        @block.tensor
        def _(pe):
            pe.wait_ge(zeroed, 1)
            for n in range(NCH):
                if n:
                    pe.wait_ge(state, n)
                b = n % 2
                for d in range(2):
                    for h in range(2):
                        lo, hi = HS * h, HS * h + HS
                        last = pe.matmul(ps[lo:hi, b, d * HS:(d + 1) * HS], W["gt"][lo:hi, d, order[d][n], :],
                                         W["st"][lo:hi, b, d, :], start=True, stop=True)
                last.then_inc(moved, 1)
                if n >= first:
                    if n >= first + 2:
                        pe.wait_ge(added, n - first - 1)
                    for d in range(2):
                        ch = order[d][n]
                        tk = CH * (ch % 2)
                        for h in range(2):
                            lo, hi = HS * h, HS * h + HS
                            last = pe.matmul(ps[tk:tk + CH, 2 + 2 * b + h, d * HS:(d + 1) * HS],
                                             W["qt"][lo:hi, d, ch // 2, tk:tk + CH], W["st"][lo:hi, b, d, :], start=True, stop=True)
                    last.then_inc(seen, 1)

        @block.vector
        def _(dve):
            dve.memset(W["st"][:, 0, :, :], 0.0).then_inc(zeroed, 1)
            for n in range(NCH):
                dve.wait_ge(moved, n + 1)
                if n >= first + 1:
                    dve.wait_ge(seen, n - first)
                for d in range(2):
                    ch = order[d][n]
                    last = dve.scalar_tensor_tensor(out=W["st"][:, (n + 1) % 2, d, :], in0=ps[:, n % 2, d * HS:(d + 1) * HS],
                                                    scalar=W["pc"][:, d, ch:ch + 1], in1=W["hp"][:, d, ch, :],
                                                    op0=ALU.mult, op1=ALU.add)
                last.then_inc(state, 1)
                if n >= first:
                    dve.wait_ge(seen, n - first + 1)
                    for d in range(2):
                        ch = order[d][n]
                        tk = CH * (ch % 2)
                        y = W["yr"][tk:tk + CH, ch // 2, d, :].rearrange("p (h s) -> p h s", h=2)
                        at = 2 + 2 * (n % 2)
                        last = dve.tensor_tensor(y, ps[tk:tk + CH, at:at + 2, d * HS:(d + 1) * HS], y, ALU.add)
                    last.then_inc(added, 1)


def rwkv_output(nc, ps, T, W, c):
    S = T["s"]
    with stage(nc, "gates", "var_in", "root", "rw", "turned", "dve_step", "act_step") as (
            block, gates, var_in, root, rw, turned, dve_step, act_step):
        y = W["yr"][:, :, :, :].rearrange("p t d (h s) -> p (t d h) s", h=2)
        sq = W["big"][:, :].rearrange("p (g s) -> p g s", s=HS)

        @block.tensor
        def _(pe):
            for d in range(2):
                for tt in range(TT):
                    last = pe.matmul(ps[:, tt // 2, (tt % 2 * 2 + d) * P:(tt % 2 * 2 + d + 1) * P],
                                     T["mT"][:, 14 + d, tt * P:(tt + 1) * P], T["g2"][:, d, bass.ts(c, P)], start=True, stop=True)
            last.then_inc(gates, 1)
            pe.wait_ge(rw, 1)
            for tt in range(TT):
                last = pe.transpose(ps[:, 2, tt * P:(tt + 1) * P], W["rw"][:, tt, :], S("ident"))
            last.then_inc(turned, 1)

        @block.scalar
        def _(act):
            act.wait_ge(var_in, 1)
            act.activation(W["var"][:, :], W["var"][:, :], ACT.Sqrt).then_inc(root, 1)
            act.wait_ge(turned, 1)
            act.activation(T["mixT"][:, c, :], ps[:, 2, :], ACT.Copy).then_inc(act_step, 1)
            act.wait_ge(act_step, 1)

        @block.vector
        def _(dve):
            done = Chain(dve, dve_step)
            done(dve.tensor_reduce(W["mean"][:, :], y, AX_X, ALU.add))
            done(dve.tensor_scalar(W["mean"][:, :], W["mean"][:, :], 1.0 / HS, None, ALU.mult))
            done(dve.tensor_tensor(y, y, bc(W["mean"][:, :], 2, HS), ALU.subtract))
            done(dve.tensor_tensor(sq, y, y, ALU.mult))
            done(dve.tensor_reduce(W["var"][:, :], sq, AX_X, ALU.add))
            dve.tensor_scalar(W["var"][:, :], W["var"][:, :], 1.0 / HS, GN_EPS, ALU.mult, ALU.add).then_inc(var_in, 1)
            dve.wait_ge(root, 1)
            done(dve.reciprocal(W["var"][:, :], W["var"][:, :]))
            done(dve.tensor_tensor(y, y, bc(W["var"][:, :], 2, HS), ALU.mult))
            y3 = W["yr"][:, :, :, :].rearrange("p t d s -> p (t d) s")
            done(dve.tensor_tensor(y3, y3, bc(T["gng"][:, bass.ts(c, P)], 1, 8), ALU.mult))
            done(dve.tensor_tensor(y3, y3, bc(T["gnb"][:, bass.ts(c, P)], 1, 8), ALU.add))
            big = W["big"][:, :].rearrange("p (t d h s) -> p t d h s", d=2, h=2, s=HS)
            bon = W["bon"][:, :].rearrange("p (t d h) -> p t d h", d=2, h=2)
            for d in range(2):
                done(dve.tensor_tensor(big[:, :, d, :, :], W["vrow"][:, 0:TT, :].rearrange("p t (h s) -> p t h s", h=2),
                                       bc(bon[:, :, d, :], 3, HS), ALU.mult))
            done(dve.tensor_tensor(y3, y3, W["big"][:, :].rearrange("p (g s) -> p g s", s=P), ALU.add))
            dve.wait_ge(gates, 1)
            done(dve.tensor_tensor(y3, y3, ps[:, 0:2, :].rearrange("p a (g s) -> p (a g) s", s=P), ALU.mult))
            dve.tensor_tensor(W["rw"][:, :, :], W["yr"][:, :, 0, :], W["yr"][:, :, 1, :], ALU.add).then_inc(rw, 1)


def fourier(nc, A, ps, T, B):
    F = T["b"]
    with stage(nc, "tab_in", "zeroed", "wf_in", "chan", "chan_out", "pos", "pos_out", "maps", "maps_out") as (
            block, tab_in, zeroed, wf_in, chan, chan_out, pos, pos_out, maps, maps_out):
        @block.sync
        def _(sp):
            sp.dma_start(B["tab"][:, :], A["big"]).then_inc(tab_in, 16)
            sp.dma_start(B["bf"][:, :], A["b_fno"][0].rearrange("(j g) e -> (g e) j", g=2)).then_inc(tab_in, 16)
            sp.wait_ge(zeroed, 1)
            wf = A["w_fno"][0].rearrange("(j g) c e -> g c j e", g=2)
            for g in range(2):
                sp.dma_start(B["wf"][g * HS:(g + 1) * HS, :, g * HS:(g + 1) * HS], wf[g]).then_inc(wf_in, 16)

        @block.vector
        def _(dve):
            dve.memset(B["wf"][:, :, :], 0.0).then_inc(zeroed, 1)
            for j in range(4):
                dve.wait_ge(maps, j + 1)
                dve.tensor_scalar(T["mixT"][:, 4 + j, :], ps[:, 6 + j % 2, :], B["bf"][:, j:j + 1], None, ALU.add).then_inc(maps_out, 1)

        @block.tensor
        def _(pe):
            pe.wait_ge(tab_in, 32)
            for i in range(2 * TT):
                tt, part = i // 2, i % 2
                if i >= 2:
                    pe.wait_ge(chan_out, i - 1)
                for j in range(4):
                    last = pe.matmul(ps[:, i % 2, j * P:(j + 1) * P], T["fT"][:, j, tt * P:(tt + 1) * P],
                                     F("chs" if part else "chc"), start=True, stop=True)
                last.then_inc(chan, 1)
            pe.wait_ge(chan_out, 2 * TT)
            for j in range(4):
                if j >= 2:
                    pe.wait_ge(pos_out, j - 1)
                for part in range(2):
                    tab = F("dfts" if part else "dftc").rearrange("p (k t) -> p k t", k=TT)
                    for k in range(TT):
                        last = pe.matmul(ps[:, 4 + j % 2, :], B["f12"][:, part, k, j * P:(j + 1) * P], tab[:, k, :],
                                         start=(part + k == 0), stop=(part == 1 and k == TT - 1))
                last.then_inc(pos, 1)
            pe.wait_ge(wf_in, 32)
            for j in range(4):
                pe.wait_ge(pos_out, j + 1)
                if j >= 2:
                    pe.wait_ge(maps_out, j - 1)
                pe.matmul(ps[:, 6 + j % 2, :], B["wf"][:, j, :], B["spec"][:, j, :], start=True, stop=True).then_inc(maps, 1)

        @block.scalar
        def _(act):
            for i in range(2 * TT):
                act.wait_ge(chan, i + 1)
                act.activation(B["f12"][:, i % 2, i // 2, :], ps[:, i % 2, :], ACT.Copy).then_inc(chan_out, 1)
            for j in range(4):
                act.wait_ge(pos, j + 1)
                act.activation(B["spec"][:, j, :], ps[:, 4 + j % 2, :], ACT.Copy).then_inc(pos_out, 1)


def residual_stage(nc, x, y, gate, n):
    with stage(nc, "dve_step") as (block, dve_step):
        @block.vector
        def _(dve):
            done = Chain(dve, dve_step)
            done(dve.tensor_tensor(y, y, bc(gate, 1, n), ALU.mult))
            done(dve.scalar_tensor_tensor(out=x, in0=x, scalar=ALPHA, in1=y, op0=ALU.mult, op1=ALU.add))


def router(nc, A, ps, T, R):
    S = T["s"]
    with stage(nc, "in_", "logit", "logit_out", "top", "e4", "sel", "rank", "count", "gt_turned", "gt_out", "b2_prod", "dve_step") as (
            block, in_, logit, logit_out, top, e4, sel, rank, count, gt_turned, gt_out, b2_prod, dve_step):
        @block.sync
        def _(sp):
            sp.dma_start(R["wr"][:, :, :], A["w_router"][0].rearrange("(k p) e -> p k e", p=P)).then_inc(in_, 16)
            sp.dma_start(R["br"][:, :], A["b_router"]).then_inc(in_, 16)
            sp.dma_start(R["b2"][:, :], A["b2"][0]).then_inc(in_, 16)

        @block.tensor
        def _(pe):
            pe.wait_ge(in_, 48)
            for tt in range(TT):
                o = ps[:, 0, tt * E:(tt + 1) * E]
                for k in range(KD):
                    pe.matmul(o, T["hT"][:, k, tt * P:(tt + 1) * P], R["wr"][:, k, :], start=(k == 0), stop=False)
                last = pe.matmul(o, T["onerow"][:, :], R["br"][:, :], start=False, stop=True)
            last.then_inc(logit, 1)
            pe.wait_ge(sel, 1)
            for tt in range(TT):
                o = ps[:, 1, tt * E:(tt + 1) * E]
                for t2 in range(tt):
                    pe.matmul(o, S("ones"), R["sel"][:, t2, :], start=(t2 == 0), stop=False)
                pe.matmul(o, S("before"), R["sel"][:, tt, :], start=(tt == 0), stop=True)
            for tt in range(TT):
                last = pe.matmul(ps[:, 1, P:P + E], S("ones"), R["sel"][:, tt, :], start=(tt == 0), stop=(tt == TT - 1))
            last.then_inc(rank, 1)
            for tt in range(TT):
                last = pe.transpose(ps[0:E, 2, tt * P:(tt + 1) * P], R["gates"][:, tt, :], S("ident"))
            last.then_inc(gt_turned, 1)
            pe.wait_ge(gt_out, 1)
            for half in range(2):
                if half:
                    pe.wait_ge(b2_prod, 1)
                    pe.wait_ge(gt_out, 2)
                for tt in range(TT):
                    last = pe.matmul(ps[:, 4 + tt, :], R["gT"][:, tt * P:(tt + 1) * P], R["b2"][:, half * 512:(half + 1) * 512],
                                     start=True, stop=True)
                last.then_inc(b2_prod, 1)

        @block.scalar
        def _(act):
            act.wait_ge(logit, 1)
            act.activation(R["lg"][:, :, :], ps[:, 0, 0:TT * E].rearrange("p (t e) -> p t e", e=E), ACT.Copy).then_inc(logit_out, 1)
            act.wait_ge(top, 1)
            act.activation(R["g4"][:, :, :], R["g4"][:, :, :], ACT.Exp).then_inc(e4, 1)
            act.wait_ge(gt_turned, 1)
            act.activation(R["gT"][:, :], ps[0:E, 2, :], ACT.Copy).then_inc(gt_out, 1)
            for half in range(2):
                act.wait_ge(b2_prod, half + 1)
                act.activation(T["f"][:, :, half * 512:(half + 1) * 512], ps[:, 4:8, :], ACT.Copy).then_inc(gt_out, 1)
            act.wait_ge(gt_out, 3)

        @block.vector
        def _(dve):
            done = Chain(dve, dve_step)
            dve.wait_ge(logit_out, 1)
            for tt in range(TT):
                done(dve.max(R["m8"][:, tt, :], R["lg"][:, tt, :]))
                done(dve.max_index(R["i8"][:, tt, :], R["m8"][:, tt, :], R["lg"][:, tt, :]))
            done(dve.tensor_copy(R["i8f"][:, :, :], R["i8"][:, :, :]))
            dve.tensor_tensor(R["g4"][:, :, :], R["m8"][:, :, 0:TOPK], bc(R["m8"][:, :, 0], 2, TOPK), ALU.subtract).then_inc(top, 1)
            dve.wait_ge(e4, 1)
            done(dve.tensor_reduce(R["sum4"][:, :], R["g4"][:, :, :], AX_X, ALU.add))
            done(dve.reciprocal(R["sum4"][:, :], R["sum4"][:, :]))
            done(dve.tensor_tensor(R["g4"][:, :, :], R["g4"][:, :, :], bc(R["sum4"][:, :], 2, TOPK), ALU.mult))
            i32f = S("iota")[:, 0:E]
            for tt in range(TT):
                for k in range(TOPK):
                    ix, gv = R["i8f"][:, tt, k:k + 1], R["g4"][:, tt, k:k + 1]
                    if k == 0:
                        done(dve.tensor_scalar(R["gates"][:, tt, :], i32f, ix, gv, ALU.is_equal, ALU.mult))
                        done(dve.tensor_scalar(R["sel"][:, tt, :], i32f, ix, None, ALU.is_equal))
                    else:
                        done(dve.tensor_scalar(R["tmp"][:, :], i32f, ix, gv, ALU.is_equal, ALU.mult))
                        done(dve.tensor_tensor(R["gates"][:, tt, :], R["gates"][:, tt, :], R["tmp"][:, :], ALU.add))
                        last = dve.scalar_tensor_tensor(out=R["sel"][:, tt, :], in0=i32f, scalar=ix, in1=R["sel"][:, tt, :],
                                                        op0=ALU.is_equal, op1=ALU.add)
                        if (tt, k) == (TT - 1, TOPK - 1):
                            last.then_inc(sel, 1)
                        else:
                            done(last)
            dve.wait_ge(rank, 1)
            rk = ps[:, 1, 0:TT * E].rearrange("p (t e) -> p t e", e=E)
            done(dve.tensor_scalar(R["place"][:, :, :], rk, 1.0, None, ALU.add))
            done(dve.tensor_tensor(R["place"][:, :, :], R["place"][:, :, :], R["sel"][:, :, :], ALU.mult))
            done(dve.tensor_scalar(R["place"][:, :, :], R["place"][:, :, :], -1.0, None, ALU.add))
            cnt = ps[:, 1, P:P + E]
            done(dve.tensor_scalar(R["nblk"][:, :], cnt, float(P), 1.0, ALU.is_gt, ALU.add))
            for b in (2, 3):
                done(dve.tensor_scalar(R["tmp"][:, :], cnt, float(b * P), None, ALU.is_gt))
                done(dve.tensor_tensor(R["nblk"][:, :], R["nblk"][:, :], R["tmp"][:, :], ALU.add))
            done(dve.tensor_copy(R["nblki"][:, :], R["nblk"][:, :]))


def experts(nc, A, ps, T, R, M):
    S = T["s"]
    NS = 12
    NR = len(M["raw"])
    NH = len(M["hi"])
    POOL = M["pool_pieces"]
    nv, npool = NS - len(POOL), len(POOL)
    SPREAD = (6, 7, 4, 5, 6, 7, 4, 5)
    low_at = {s: (s in POOL, sum((q in POOL) == (s in POOL) for q in range(s))) for s in range(NS)}
    with stage(nc, *[f"raw_in{i}" for i in range(NR)], "hi_done", "lo_v", "lo_p", "used", "perm", "stepped", "cur_p", "picked",
               "turned", "gath", "x_hi", "x_done", "pt", "pt_out", "biased", "mixed", "sig", "acted", "at", "at_hi", "at_lo",
               "y_hi", "y_lo", "spread", "added", "cur", "row_a", "row_v") as sems:
        block, raw_in = sems[0], sems[1:1 + NR]
        (hi_done, lo_v, lo_p, used, perm, stepped, cur_p, picked, turned, gath, x_hi, x_done, pt, pt_out, biased, mixed, sig, acted,
         at, at_hi, at_lo, y_hi, y_lo, spread, added, cur, row_a, row_v) = sems[1 + NR:]


        def counter(eng, name):
            r = eng.alloc_register(name)
            eng.reg_mov(r, 0)
            return r, lambda: eng.snap(r, min_val=0, max_val=E * TT)

        def blocks_of(eng, e):
            return eng.value_load(R["nblki"][0:1, bass.ds(e, 1)], min_val=1, max_val=TT)

        def wait_low(eng, w, s, back=0):
            at_, wrap = (s - back, 1) if s >= back else (s - back + NS, 0)
            pool, n = low_at[at_]
            if pool:
                eng.wait_ge(lo_p, (w + wrap) * npool + n + 1)
            else:
                eng.wait_ge(lo_v, (w + wrap) * nv + n + 1)

        @block.sync
        def _(sp):
            r, now = counter(sp, "sp_blocks")
            with sp.Fori(0, E) as e:
                w1 = A["w1"][0, e].rearrange("(k p) n -> p k n", p=P)
                w2 = A["w2"][0, e].rearrange("(k p) n -> p k n", p=P)
                with sp.Fori(0, blocks_of(sp, e)) as _:
                    w = now()
                    for s in range(NS):
                        wait_low(sp, w, s, NR)
                        src, c, half = (w1, s // 2, s % 2) if s < 8 else (w2, s % 2, (s - 8) // 2)
                        sp.dma_start(M["raw"][s % NR][:, :, :], src[:, 4 * half:4 * half + 4, c * 512:(c + 1) * 512])\
                          .then_inc(raw_in[s % NR], 16)
                    sp.reg_add(r, r, 1)

        @block.gpsimd
        def _(pool):
            r, now = counter(pool, "pool_blocks")
            pool.sem_inc(lo_p, npool)
            with pool.Fori(0, E) as e:
                pool.tensor_copy(M["place"][:, :], R["place"][:, :, e]).then_inc(cur_p, 1)
                pool.wait_ge(cur_p, now() + e + 1)
                with pool.Fori(0, blocks_of(pool, e)) as _:
                    w = now()

                    def low(s):
                        pool.wait_ge(hi_done, w * NS + s + 1)
                        pool.wait_ge(used, w * NS + s + 1)
                        pool.tensor_tensor(M["lo"][s % NH][:, :, :], M["raw"][s % NR][:, :, :], M["hi"][s % NH][:, :, :].bitcast(F32),
                                           ALU.subtract).then_inc(lo_p, 1)

                    pool.wait_ge(pt, w + 1)
                    pool.tensor_tensor(M["next"][:, :], M["place"][:, :], S("step"), ALU.subtract).then_inc(stepped, 1)
                    for tt in range(TT):
                        last = pool.tensor_scalar(M["pm"][:, tt, :], S("iota"), M["place"][:, tt:tt + 1], None, ALU.is_equal)
                    last.then_inc(perm, 1)
                    pool.wait_ge(perm, w + 1)
                    pool.wait_ge(stepped, w + 1)
                    pool.tensor_tensor(M["place"][:, :], M["next"][:, :], S("ones")[:, 0:TT], ALU.mult).then_inc(cur_p, 1)
                    pool.wait_ge(cur_p, w + e + 2)
                    pool.wait_ge(used, w * NS + NH)
                    pool.tensor_tensor(M["pick"][:, :], S("eye32")[0:2 * E, bass.ds(e, 1)].to_broadcast([2 * E, P]), S("ones")[0:2 * E, :],
                                       ALU.mult).then_inc(picked, 1)
                    for s in POOL:
                        low(s)
                    pool.reg_add(r, r, 1)

        @block.tensor
        def _(pe):
            r, now = counter(pe, "pe_blocks")
            pe.sem_inc(used, NH)
            pe.sem_inc(pt, 1)

            def scatter(w, i):
                half, tt = i // TT, i % TT
                pe.wait_ge(y_lo, 2 * w + half + 1)
                if i == 3:
                    pe.wait_ge(y_lo, 2 * w + 2)
                if i >= 4:
                    pe.wait_ge(added, w * 8 + i - 3)
                o = ps[:, SPREAD[i], :]
                pe.matmul(o, M["pT"][:, tt * P:(tt + 1) * P], M["yh"][:, half * 512:(half + 1) * 512], start=True, stop=False)
                pe.matmul(o, M["pT"][:, tt * P:(tt + 1) * P], M["yl"][:, half * 512:(half + 1) * 512],
                          start=False, stop=True).then_inc(spread, 1)

            with pe.Fori(0, E) as e:
                with pe.Fori(0, blocks_of(pe, e)) as _:
                    w = now()

                    def piece(s):
                        wait_low(pe, w, s)
                        hi, lo = M["hi"][s % NH], M["lo"][s % NH]
                        if s < 8:
                            b, half, xh, xl = s // 2, s % 2, M["xh"], M["xl"]
                        else:
                            b, half, xh, xl = 4 + s % 2, (s - 8) // 2, M["ah"], M["al"]
                        if s < 8 and half == 0:
                            pe.matmul(ps[:, b, :], M["pick"][:, :], M["b12"][:, b * 512:(b + 1) * 512], start=True, stop=False)
                        for k in range(4):
                            first = s >= 8 and half == 0 and k == 0
                            pe.matmul(ps[:, b, :], xh[:, 4 * half + k, :], hi[:, k, :], start=first, stop=False)
                            pe.matmul(ps[:, b, :], xh[:, 4 * half + k, :], lo[:, k, :], start=False, stop=False)
                            mm = pe.matmul(ps[:, b, :], xl[:, 4 * half + k, :], hi[:, k, :], start=False, stop=(half == 1 and k == 3))
                        mm.then_inc(used, 1)

                    def turn_act(p):
                        pe.wait_ge(acted, 4 * w + p + 1)
                        if p >= 2:
                            pe.wait_ge(at_lo, 4 * w + p - 1)
                        for i in range(2):
                            mm = pe.transpose(ps[:, 6 + p % 2, i * P:(i + 1) * P], M["arow"][:, p % 2, i * P:(i + 1) * P], S("ident"))
                        mm.then_inc(at, 1)

                    pe.wait_ge(perm, w + 1)
                    for half in range(2):
                        for tt in range(TT):
                            at_ = slice(half * 512, (half + 1) * 512)
                            pe.matmul(ps[:, half, :], M["pm"][:, tt, :], M["hh"][:, tt, at_], start=(tt == 0), stop=False)
                            mm = pe.matmul(ps[:, half, :], M["pm"][:, tt, :], M["hl"][:, tt, at_], start=False, stop=(tt == TT - 1))
                        mm.then_inc(gath, 1)
                    scatter(w, 0)
                    scatter(w, 1)
                    for half in range(2):
                        if half == 0:
                            pe.wait_ge(row_a, w + 1)
                        else:
                            pe.wait_ge(row_v, w + 1)
                        for k in range(4):
                            mm = pe.transpose(ps[:, 2 + half, k * P:(k + 1) * P], M["xrow"][:, (4 * half + k) * P:(4 * half + k + 1) * P],
                                              S("ident"))
                        mm.then_inc(turned, 1)
                    scatter(w, 2)
                    scatter(w, 3)
                    pe.wait_ge(picked, w + 1)
                    pe.wait_ge(x_done, 2 * w + 1)
                    piece(0)
                    scatter(w, 4)
                    scatter(w, 5)
                    pe.wait_ge(x_done, 2 * w + 2)
                    piece(1)
                    scatter(w, 6)
                    scatter(w, 7)
                    piece(2)
                    pe.wait_ge(added, w * 8 + 8)
                    for tt in range(TT):
                        mm = pe.transpose(ps[:, 5, tt * P:(tt + 1) * P], M["pm"][:, tt, :].bitcast(F32), S("ident"))
                    mm.then_inc(pt, 1)
                    for s in range(3, 8):
                        piece(s)
                        if s % 2:
                            turn_act(s // 2 - 1)
                    pe.wait_ge(at_lo, 4 * w + 2)
                    piece(8)
                    turn_act(3)
                    pe.wait_ge(pt_out, w + 1)
                    piece(9)
                    pe.wait_ge(at_lo, 4 * w + 4)
                    piece(10)
                    piece(11)
                    pe.reg_add(r, r, 1)
            for i in range(8):
                scatter(now(), i)

        @block.scalar
        def _(act):
            r, now = counter(act, "act_blocks")

            def y_high(w, half):
                act.wait_ge(used, w * NS + NH - 1 + half)
                act.activation(M["yh"][:, half * 512:(half + 1) * 512], ps[:, 4 + half, :], ACT.Copy).then_inc(y_hi, 1)

            with act.Fori(0, E) as e:
                with act.Fori(0, blocks_of(act, e)) as _:
                    w = now()

                    def high(s):
                        act.wait_ge(raw_in[s % NR], 16 * (w * (NS // NR) + s // NR + 1))
                        act.wait_ge(used, w * NS + s + 1)
                        act.activation(M["hi"][s % NH][:, :, :], M["raw"][s % NR][:, :, :], ACT.Copy).then_inc(hi_done, 1)

                    def sigmoid(p):
                        act.wait_ge(biased, 4 * w + p + 1)
                        act.activation(M["arow"][:, p % 2, :], M["gl"][:, p % 2, 0, :], ACT.Sigmoid, scale=SW_ALPHA).then_inc(sig, 1)

                    def act_high(p):
                        act.wait_ge(at, 4 * w + p + 1)
                        act.activation(M["ah"][:, 2 * p:2 * p + 2, :], ps[:, 6 + p % 2, 0:256].rearrange("p (k s) -> p k s", k=2),
                                       ACT.Copy).then_inc(at_hi, 1)

                    high(0)
                    high(1)
                    y_high(w, 0)
                    high(2)
                    y_high(w, 1)
                    act.wait_ge(gath, 2 * w + 1)
                    act.activation(M["xrow"][:, 0:512], ps[:, 0, :], ACT.Copy).then_inc(row_a, 1)
                    high(3)
                    for half in range(2):
                        act.wait_ge(turned, w * 2 + half + 1)
                        act.activation(M["xh"][:, 4 * half:4 * half + 4, :], ps[:, 2 + half, :].rearrange("p (k s) -> p k s", k=4),
                                       ACT.Copy).then_inc(x_hi, 1)
                    high(4)
                    high(5)
                    act.wait_ge(pt, w + 2)
                    act.activation(M["pT"][:, :], ps[:, 5, :], ACT.Copy).then_inc(pt_out, 1)
                    sigmoid(0)
                    high(6)
                    sigmoid(1)
                    act_high(0)
                    high(7)
                    high(8)
                    sigmoid(2)
                    act_high(1)
                    high(9)
                    high(10)
                    sigmoid(3)
                    act_high(2)
                    high(11)
                    act_high(3)
                    act.reg_add(r, r, 1)
            for half in range(2):
                y_high(now(), half)

        @block.vector
        def _(dve):
            r, now = counter(dve, "dve_blocks")
            dve.sem_inc(lo_v, nv)

            def y_low(w, half):
                dve.wait_ge(y_hi, 2 * w + half + 1)
                at_ = slice(half * 512, (half + 1) * 512)
                dve.tensor_tensor(M["yl"][:, at_], ps[:, 4 + half, :], M["yh"][:, at_].bitcast(F32), ALU.subtract).then_inc(y_lo, 1)

            def add(w, i):
                half, tt = i // TT, i % TT
                dve.wait_ge(spread, w * 8 + i + 1)
                f = T["f"][:, tt, half * 512:(half + 1) * 512]
                dve.scalar_tensor_tensor(out=f, in0=ps[:, SPREAD[i], :], scalar=M["gate"][:, tt:tt + 1], in1=f,
                                         op0=ALU.mult, op1=ALU.add).then_inc(added, 1)

            with dve.Fori(0, E) as e:
                with dve.Fori(0, blocks_of(dve, e)) as _:
                    w = now()

                    def low(s):
                        if s in POOL:
                            return
                        dve.wait_ge(hi_done, w * NS + s + 1)
                        dve.wait_ge(used, w * NS + s + 1)
                        dve.tensor_tensor(M["lo"][s % NH][:, :, :], M["raw"][s % NR][:, :, :], M["hi"][s % NH][:, :, :].bitcast(F32),
                                          ALU.subtract).then_inc(lo_v, 1)

                    def swiglu(p):
                        dve.wait_ge(used, w * NS + NH + 2 * p + 2)
                        gl, li = M["gl"][:, p % 2, 0, :], M["gl"][:, p % 2, 1, :]
                        dve.tensor_scalar(li, ps[:, p, 1:512:2], LIMIT, -LIMIT, ALU.min, ALU.max)
                        dve.tensor_scalar(gl, ps[:, p, 0:511:2], LIMIT, None, ALU.min).then_inc(biased, 1)
                        dve.wait_ge(biased, 4 * w + p + 1)
                        dve.scalar_tensor_tensor(out=li, in0=li, scalar=1.0, in1=gl, op0=ALU.add, op1=ALU.mult).then_inc(mixed, 1)
                        dve.wait_ge(mixed, 4 * w + p + 1)
                        dve.wait_ge(sig, 4 * w + p + 1)
                        dve.tensor_tensor(M["arow"][:, p % 2, :], li, M["arow"][:, p % 2, :], ALU.mult).then_inc(acted, 1)

                    def act_low(p):
                        dve.wait_ge(at_hi, 4 * w + p + 1)
                        src = ps[:, 6 + p % 2, 0:256].rearrange("p (k s) -> p k s", k=2)
                        dve.tensor_tensor(M["al"][:, 2 * p:2 * p + 2, :], src, M["ah"][:, 2 * p:2 * p + 2, :].bitcast(F32),
                                          ALU.subtract).then_inc(at_lo, 1)

                    low(0)
                    low(1)
                    y_low(w, 0)
                    low(2)
                    y_low(w, 1)
                    dve.wait_ge(gath, 2 * w + 2)
                    dve.tensor_copy(M["xrow"][:, 512:1024], ps[:, 1, :]).then_inc(row_v, 1)
                    for half in range(2):
                        dve.wait_ge(x_hi, 2 * w + half + 1)
                        dve.tensor_tensor(M["xl"][:, 4 * half:4 * half + 4, :], ps[:, 2 + half, :].rearrange("p (k s) -> p k s", k=4),
                                          M["xh"][:, 4 * half:4 * half + 4, :].bitcast(F32), ALU.subtract).then_inc(x_done, 1)
                    add(w, 0)
                    add(w, 1)
                    low(3)
                    add(w, 2)
                    add(w, 3)
                    add(w, 4)
                    add(w, 5)
                    low(4)
                    add(w, 6)
                    add(w, 7)
                    low(5)
                    dve.wait_ge(added, w * 8 + 8)
                    dve.tensor_copy(M["gate"][:, :], R["gates"][:, :, e]).then_inc(cur, 1)
                    swiglu(0)
                    low(6)
                    swiglu(1)
                    act_low(0)
                    low(7)
                    low(8)
                    swiglu(2)
                    act_low(1)
                    low(9)
                    low(10)
                    swiglu(3)
                    act_low(2)
                    low(11)
                    act_low(3)
                    dve.reg_add(r, r, 1)
            for half in range(2):
                y_low(now(), half)
            dve.wait_ge(cur, now())
            for i in range(8):
                add(now(), i)


def split_stage(nc, jobs):
    with stage(nc, "hi_done", "lo_done") as (block, hi_done, lo_done):
        @block.scalar
        def _(act):
            for src, hi, _ in jobs:
                act.activation(hi, src, ACT.Copy).then_inc(hi_done, 1)

        @block.vector
        def _(dve):
            for i, (src, hi, lo) in enumerate(jobs):
                dve.wait_ge(hi_done, i + 1)
                dve.tensor_tensor(lo, src, hi.bitcast(F32), ALU.subtract).then_inc(lo_done, 1)
            dve.wait_ge(lo_done, len(jobs))


def split_jobs(src, hi, lo, n, step=2):
    return [(src[:, i:i + step, :], hi[:, i:i + step, :], lo[:, i:i + step, :]) for i in range(0, n, step)]


def split_gemm(nc, ps, w_piece, width, pieces, rows, hi_lhs, lo_lhs, raw, hi, lo, evac):
    nr, nh = len(raw), len(hi)
    step = raw[0].shape[1]
    parts = KD // step
    count = parts * pieces
    with stage(nc, *[f"raw_in{i}" for i in range(nr)], "hi_done", "lo_done", "used", "prod", "prod_out") as sems:
        block, raw_in, (hi_done, lo_done, used, prod, prod_out) = sems[0], sems[1:1 + nr], sems[1 + nr:]

        @block.sync
        def _(sp):
            for q in range(count):
                n, part = q // parts, q % parts
                if q >= nr:
                    sp.wait_ge(lo_done, q - nr + 1)
                sp.dma_start(raw[q % nr][:, :, 0:width(n)], w_piece(n)[:, step * part:step * part + step, :]).then_inc(raw_in[q % nr], 16)

        @block.tensor
        def _(pe):
            for q in range(count):
                n, part = q // parts, q % parts
                pe.wait_ge(lo_done, q + 1)
                for m in range(rows):
                    o = ps[:, (n % 2) * 4 + m, 0:width(n)]
                    if part == 0 and n >= 2:
                        pe.wait_ge(prod_out, (n - 2) * rows + m + 1)
                    for k in range(step):
                        kk = step * part + k
                        w_hi, w_lo = hi[q % nh][:, k, 0:width(n)], lo[q % nh][:, k, 0:width(n)]
                        pe.matmul(o, hi_lhs(kk, m), w_hi, start=(kk == 0), stop=False)
                        pe.matmul(o, hi_lhs(kk, m), w_lo, start=False, stop=False)
                        last = pe.matmul(o, lo_lhs(kk, m), w_hi, start=False, stop=(kk == KD - 1))
                    if part == parts - 1 and m < rows - 1:
                        last.then_inc(prod, 1)
                last.then_inc(used, 1)

        @block.scalar
        def _(act):
            def high(q):
                act.wait_ge(raw_in[q % nr], 16 * (q // nr + 1))
                if q >= nh:
                    act.wait_ge(used, q - nh + 1)
                act.activation(hi[q % nh][:, :, 0:width(q // parts)], raw[q % nr][:, :, 0:width(q // parts)], ACT.Copy).then_inc(hi_done, 1)

            for q in range(min(nh, count)):
                high(q)
            for q in range(count):
                if q + nh < count:
                    high(q + nh)
                if q % parts == parts - 1:
                    for m in range(rows):
                        if m < rows - 1:
                            act.wait_ge(prod, (q // parts) * (rows - 1) + m + 1)
                        else:
                            act.wait_ge(used, q + 1)
                        n = q // parts
                        evac(act, n, m, ps[:, (n % 2) * 4 + m, 0:width(n)]).then_inc(prod_out, 1)

        @block.vector
        def _(dve):
            for q in range(count):
                dve.wait_ge(hi_done, q + 1)
                if q >= nh:
                    dve.wait_ge(used, q - nh + 1)
                cut = (slice(None), slice(None), slice(0, width(q // parts)))
                dve.tensor_tensor(lo[q % nh][cut], raw[q % nr][cut], hi[q % nh][cut].bitcast(F32), ALU.subtract).then_inc(lo_done, 1)


def rms_rows(nc, h, x, gain, tmp, ss, n, width=D):
    with stage(nc, "sums", "mean_in", "root", "dve_step") as (block, sums, mean_in, root, dve_step):
        @block.scalar
        def _(act):
            for t in range(n):
                if t:
                    act.wait_ge(sums, t)
                act.activation(tmp[:, 0:width], x[:, t, :], ACT.Square, accum_out=ss[:, t:t + 1]).then_inc(sums, 1)
            act.wait_ge(mean_in, 1)
            act.activation(ss[:, 0:n], ss[:, 0:n], ACT.Sqrt).then_inc(root, 1)

        @block.vector
        def _(dve):
            done = Chain(dve, dve_step)
            dve.wait_ge(sums, n)
            dve.tensor_scalar(ss[:, 0:n], ss[:, 0:n], 1.0 / width, RMS_EPS, ALU.mult, ALU.add).then_inc(mean_in, 1)
            dve.wait_ge(root, 1)
            done(dve.reciprocal(ss[:, 0:n], ss[:, 0:n]))
            for t in range(n):
                done(dve.scalar_tensor_tensor(out=h[:, t, :], in0=x[:, t, :], scalar=ss[:, t:t + 1], in1=gain,
                                              op0=ALU.mult, op1=ALU.mult))


def head_norms(nc, jobs, sq, r, loads=()):
    with stage(nc, "mean_in", "root", "dve_step", "loaded") as (block, mean_in, root, dve_step, loaded):
        @block.sync
        def _(sp):
            for dst, src in loads:
                sp.dma_start(dst, src).then_inc(loaded, 16)
            if loads:
                sp.wait_ge(loaded, 16 * len(loads))

        at, spans = 0, []
        for src, dsts, gain, size in jobs:
            n = src.shape[1] * src.shape[2]
            spans.append((at, n))
            at += n

        @block.vector
        def _(dve):
            done = Chain(dve, dve_step)
            np_ = jobs[0][0].shape[0]
            for (src, dsts, gain, size), (a, n) in zip(jobs, spans):
                t, h = src.shape[1], src.shape[2]
                s4 = sq[0:np_, 0:n * size].rearrange("p (t h s) -> p t h s", t=t, h=h)
                done(dve.tensor_tensor(s4, src, src, ALU.mult))
                done(dve.tensor_reduce(r[0:np_, a:a + n].rearrange("p (t h) -> p t h", t=t), s4, AX_X, ALU.add))
                done(dve.tensor_scalar(r[0:np_, a:a + n], r[0:np_, a:a + n], 1.0 / size, RMS_EPS, ALU.mult, ALU.add))
            dve.tensor_copy(r[0:np_, at:at + 1], r[0:np_, 0:1]).then_inc(mean_in, 1)
            dve.wait_ge(root, 1)
            done(dve.reciprocal(r[0:np_, 0:at], r[0:np_, 0:at]))
            for (src, dsts, gain, size), (a, n) in zip(jobs, spans):
                t, h = src.shape[1], src.shape[2]
                r3 = r[0:np_, a:a + n].rearrange("p (t h) -> p t h", t=t)
                done(dve.tensor_tensor(src, src, bc(r3, 3, size), ALU.mult))
                for part, dst in dsts:
                    g3 = bc(bc(gain, 1, part.shape[2]), 1, t)
                    done(dve.tensor_tensor(dst, part, g3, ALU.mult))

        @block.scalar
        def _(act):
            act.wait_ge(mean_in, 1)
            act.activation(r[0:jobs[0][0].shape[0], 0:at], r[0:jobs[0][0].shape[0], 0:at], ACT.Sqrt).then_inc(root, 1)


def rope(nc, T, views, tmp):
    S = T["s"]
    with stage(nc, "dve_step") as (block, dve_step):
        @block.vector
        def _(dve):
            done = Chain(dve, dve_step)
            for v in views:
                h = v.shape[2]
                cos = bc(S("cos").rearrange("p (t s) -> p t s", t=TT), 2, h)
                sin = bc(S("sin").rearrange("p (t s) -> p t s", t=TT), 2, h)
                x1, x2 = v[:, :, :, 0:32], v[:, :, :, 32:64]
                n = TT * h * 32
                t1 = tmp[:, 0:n].rearrange("p (t h s) -> p t h s", t=TT, h=h)
                t2 = tmp[:, n:2 * n].rearrange("p (t h s) -> p t h s", t=TT, h=h)
                done(dve.tensor_tensor(t1, x1, sin, ALU.mult))
                done(dve.tensor_tensor(t2, x2, sin, ALU.mult))
                done(dve.tensor_tensor(x1, x1, cos, ALU.mult))
                done(dve.tensor_tensor(x2, x2, cos, ALU.mult))
                done(dve.tensor_tensor(x1, x1, t2, ALU.subtract))
                done(dve.tensor_tensor(x2, x2, t1, ALU.add))


def compress(nc, ps, T, L, Z):
    with stage(nc, "pe_t", "pe_out", "blk", "hid", "sg", "silu", "two", "two_out", "dve_step") as (
            block, pe_t, pe_out, blk, hid, sg, silu, two, two_out, dve_step):
        S = T["s"]

        @block.tensor
        def _(pe):
            for i in range(2):
                last = pe.transpose(ps[:, 0, i * 32:(i + 1) * 32], L["pe"][:, i, :, :].rearrange("p g d -> p (g d)"), S("ident")[0:32, 0:32])
            last.then_inc(pe_t, 1)
            for i in range(2):
                pe.wait_ge(blk, i + 1)
                for g in range(2):
                    for l in range(32):
                        last = pe.matmul(ps[:, 1 + 2 * i + g, 0:NCMP], L["cw1"][i][g * HS:(g + 1) * HS, l, :],
                                         Z["blk"][g * HS:(g + 1) * HS, i, l, 0:NCMP], start=(l == 0), stop=(l == 31))
                last.then_inc(hid, 1)
            pe.wait_ge(silu, 2)
            for g in range(2):
                pe.matmul(ps[0:32, 5, g * HS:(g + 1) * HS], Z["hid"][:, 0, g, :], L["cw2"][:, 0, :], start=True, stop=True)
                for o in range(4):
                    last = pe.matmul(ps[32 * o:32 * o + 32, 6, g * HS:(g + 1) * HS], Z["hid"][:, 1, g, :], L["cw2"][:, 1, :],
                                     start=True, stop=True)
            last.then_inc(two, 1)

        @block.vector
        def _(dve):
            done = Chain(dve, dve_step)
            done(dve.memset(Z["hid"][:, :, :, :], 0.0))
            dve.wait_ge(pe_out, 1)
            for i, src in enumerate((Z["kcT"], Z["vcT"])):
                v = src[:, :].rearrange("p (n s) -> p s n", s=16)
                dve.tensor_tensor(Z["blk"][:, i, 0:16, 0:NCMP], v[:, :, 0:NCMP], bc(Z["peT"][:, i, 0:16], 2, NCMP), ALU.add)
                dve.tensor_tensor(Z["blk"][:, i, 16:32, 0:NCMP], v[:, :, 1:NCMP + 1], bc(Z["peT"][:, i, 16:32], 2, NCMP),
                                  ALU.add).then_inc(blk, 1)
            for i in range(2):
                dve.wait_ge(sg, i + 1)
                dve.tensor_tensor(Z["hid"][:, i, :, 0:NCMP], ps[:, 1 + 2 * i:3 + 2 * i, 0:NCMP],
                                  Z["hsg"][:, i, :, 0:NCMP], ALU.mult).then_inc(silu, 1)

        @block.scalar
        def _(act):
            act.wait_ge(pe_t, 1)
            act.activation(Z["peT"][:, :, :], ps[:, 0, 0:64].rearrange("p (i l) -> p i l", i=2), ACT.Copy).then_inc(pe_out, 1)
            for i in range(2):
                act.wait_ge(hid, i + 1)
                act.activation(Z["hsg"][:, i, :, 0:NCMP], ps[:, 1 + 2 * i:3 + 2 * i, 0:NCMP],
                               ACT.Sigmoid).then_inc(sg, 1)
            act.wait_ge(two, 1)
            act.activation(Z["kcr"][:, :], ps[0:32, 5, 0:P], ACT.Copy).then_inc(two_out, 1)
            act.activation(Z["vc"][:, :], ps[:, 6, 0:P], ACT.Copy).then_inc(two_out, 1)
            act.wait_ge(two_out, 2)


def compressed_attention(nc, ps, T, Z):
    S = T["s"]
    with stage(nc, "scores", "shifted", "expd", "probs", "pt", "pt_out", "pv", "pv_out", "dve_step") as (
            block, scores, shifted, expd, probs, pt, pt_out, pv, pv_out, dve_step):
        @block.tensor
        def _(pe):
            for tt in range(TT):
                for h in range(8):
                    g, r = h // 4, h % 4
                    last = pe.matmul(ps[:, 4 * g + tt, r * 32:(r + 1) * 32],
                                     Z["qT"][g * HS:(g + 1) * HS, r, tt * P:(tt + 1) * P], Z["kc"][g * HS:(g + 1) * HS, :],
                                     start=True, stop=True)
            last.then_inc(scores, 1)
            pe.wait_ge(probs, 1)
            for tt in range(TT):
                for g in range(2):
                    last = pe.transpose(ps[:, 2 + g, tt * P:(tt + 1) * P],
                                        Z["cp"][:, tt, g * P:(g + 1) * P], S("ident"))
            last.then_inc(pt, 1)
            pe.wait_ge(pt_out, 1)
            for tt in range(TT):
                for h in range(8):
                    g, r = h // 4, h % 4
                    at = (tt * 2 + g) * HS
                    last = pe.matmul(ps[:, 4 + r, at:at + HS], Z["cpT"][32 * r:32 * r + 32, g, tt * P:(tt + 1) * P],
                                     Z["vc"][32 * r:32 * r + 32, g * HS:(g + 1) * HS], start=True, stop=True)
            last.then_inc(pv, 1)

        s4 = Z["cp"][:, :, :].rearrange("p t (h n) -> p t h n", n=32)
        s3 = Z["cp"][:, :, :].rearrange("p t (h n) -> p (t h) n", n=32)

        @block.vector
        def _(dve):
            done = Chain(dve, dve_step)
            dve.wait_ge(scores, 1)
            add = S("cmpadd").rearrange("p (t n) -> p t n", t=TT)
            ok = S("cmpok").rearrange("p (t n) -> p t n", t=TT)
            for g in range(2):
                done(dve.tensor_tensor(s4[:, :, 4 * g:4 * g + 4, :], ps[:, 4 * g:4 * g + 4, 0:P].rearrange("p t (r n) -> p t r n", r=4),
                                       bc(add, 2, 4), ALU.add))
            done(dve.tensor_reduce(Z["cm"][:, 0, :], s3, AX_X, ALU.max))
            dve.tensor_tensor(s3, s3, bc(Z["cm"][:, 0, :], 2, 32), ALU.subtract).then_inc(shifted, 1)
            dve.wait_ge(expd, 1)
            done(dve.tensor_tensor(s4, s4, bc(ok, 2, 8), ALU.mult))
            done(dve.tensor_reduce(Z["cm"][:, 0, :], s3, AX_X, ALU.add))
            done(dve.tensor_scalar(Z["cm"][:, 0, :], Z["cm"][:, 0, :], 1e-30, None, ALU.max))
            done(dve.reciprocal(Z["cm"][:, 0, :], Z["cm"][:, 0, :]))
            g0 = Z["gate"][:, :, :].rearrange("p t (h b) -> p t h b", b=3)[:, :, :, 0]
            c3 = Z["cm"][:, 0, :].rearrange("p (t h) -> p t h", t=TT)
            done(dve.tensor_tensor(c3, c3, g0, ALU.mult))
            dve.tensor_tensor(s3, s3, bc(Z["cm"][:, 0, :], 2, 32), ALU.mult).then_inc(probs, 1)

        @block.scalar
        def _(act):
            act.wait_ge(shifted, 1)
            act.activation(s3, s3, ACT.Exp).then_inc(expd, 1)
            act.wait_ge(pt, 1)
            act.activation(Z["cpT"][:, :, :], ps[:, 2:4, :], ACT.Copy).then_inc(pt_out, 1)
            act.wait_ge(pv, 1)
            for r in range(4):
                o = Z["o"][0].rearrange("p t (g r s) -> p t g r s", g=2, r=4)[:, :, :, r, :]
                act.activation(o, ps[:, 4 + r, :].rearrange("p (t g s) -> p t g s", t=TT, g=2), ACT.Copy).then_inc(pv_out, 1)
            act.wait_ge(pv_out, 4)


def attention(nc, ps, T, Z, units):
    S = T["s"]
    with stage(nc, "scores", "top", "probs", "pt", "pt_out", "pv", "pv_out", "dve_step") as (
            block, scores, top, probs, pt, pt_out, pv, pv_out, dve_step):
        n = len(units)

        @block.tensor
        def _(pe):
            def score(i):
                u = units[i]
                if i >= 3:
                    pe.wait_ge(probs, i - 2)
                o = ps[:, i % 3, 0:u["n"]]
                mm = pe.matmul(o, u["q"], u["k"], start=True, stop=not u["extra"])
                for x, (a, b, lo, hi) in enumerate(u["extra"]):
                    mm = pe.matmul(ps[:, i % 3, lo:hi], a, b, start=False, stop=(x == len(u["extra"]) - 1))
                mm.then_inc(scores, 1)

            def turn_probs(i):
                pe.wait_ge(probs, i + 1)
                if i >= 3:
                    pe.wait_ge(pt_out, i - 2)
                for b in range(units[i]["n"] // P):
                    mm = pe.transpose(ps[:, 3 + i % 3, b * P:(b + 1) * P], Z["p"][:, i % 3, b * P:(b + 1) * P], S("ident"))
                mm.then_inc(pt, 1)

            def values(i):
                u = units[i]
                nk = u["n"] // P
                pe.wait_ge(pt_out, i + 1)
                if i >= 2:
                    pe.wait_ge(pv_out, i - 1)
                for b in range(nk):
                    mm = pe.matmul(ps[:, 6 + i % 2, 0:u["w"]], Z["pT"][:, i % 2, b * P:(b + 1) * P], u["v"][b],
                                   start=(b == 0), stop=(b == nk - 1))
                mm.then_inc(pv, 1)

            score(0)
            score(1)
            turn_probs(0)
            for i in range(n):
                if i + 2 < n:
                    score(i + 2)
                if i + 1 < n:
                    turn_probs(i + 1)
                values(i)

        @block.scalar
        def _(act):
            def exponentials(i):
                u = units[i]
                act.wait_ge(top, i + 1)
                if i >= 3:
                    act.wait_ge(pt, i - 2)
                act.activation(Z["p"][:, i % 3, 0:u["n"]], ps[:, i % 3, 0:u["n"]], ACT.Exp, bias=Z["nm"][:, i % 4:i % 4 + 1],
                               accum_out=Z["sum"][:, i % 4:i % 4 + 1]).then_inc(probs, 1)

            def turned_out(i):
                u = units[i]
                act.wait_ge(pt, i + 1)
                if i >= 2:
                    act.wait_ge(pv, i - 1)
                act.activation(Z["pT"][:, i % 2, 0:u["n"]], ps[:, 3 + i % 3, 0:u["n"]], ACT.Copy).then_inc(pt_out, 1)

            exponentials(0)
            exponentials(1)
            turned_out(0)
            for i in range(n):
                if i + 2 < n:
                    exponentials(i + 2)
                if i + 1 < n:
                    turned_out(i + 1)

        @block.vector
        def _(dve):
            done = Chain(dve, dve_step)

            def maximum(i):
                u = units[i]
                dve.wait_ge(scores, i + 1)
                done(dve.tensor_reduce(Z["mx"][:, i % 4:i % 4 + 1], ps[:, i % 3, 0:u["n"]], AX_X, ALU.max))
                dve.tensor_scalar(Z["nm"][:, i % 4:i % 4 + 1], Z["mx"][:, i % 4:i % 4 + 1], -1.0, None, ALU.mult).then_inc(top, 1)

            maximum(0)
            maximum(1)
            for i, u in enumerate(units):
                if i + 2 < n:
                    maximum(i + 2)
                rs = Z["rs"][:, i % 4:i % 4 + 1]
                dve.wait_ge(probs, i + 1)
                done(dve.reciprocal(rs, Z["sum"][:, i % 4:i % 4 + 1]))
                src = ps[:, 6 + i % 2, 0:u["w"]]
                if u["gate"] is None:
                    dve.wait_ge(pv, i + 1)
                    dve.tensor_scalar(u["o"], src, rs, None, ALU.mult).then_inc(pv_out, 1)
                else:
                    done(dve.tensor_scalar(rs, rs, u["gate"], None, ALU.mult))
                    dve.wait_ge(pv, i + 1)
                    dve.scalar_tensor_tensor(out=u["o"], in0=src, scalar=rs, in1=u["o"], op0=ALU.mult, op1=ALU.add).then_inc(pv_out, 1)


def forget_bias(nc, ps, T, Z, L):
    S = T["s"]
    with stage(nc, "eased", "sq", "logf", "cum", "cum_out", "dve_step") as (
            block, eased, sq, logf, cum, cum_out, dve_step):
        f = Z["z"][:, :, 3352:3360]

        @block.vector
        def _(dve):
            done = Chain(dve, dve_step)
            done(dve.tensor_tensor(Z["lf"][:, 0, :, :], f, bc(L["fb"][:, :], 1, TT), ALU.add))
            done(dve.tensor_scalar(Z["lf"][:, 1, :, :], Z["lf"][:, 0, :, :], -1.0, None, ALU.mult))
            dve.tensor_tensor(Z["lf"][:, 1, :, :], Z["lf"][:, 0, :, :], Z["lf"][:, 1, :, :], ALU.min).then_inc(eased, 1)
            dve.wait_ge(sq, 2)
            done(dve.tensor_scalar(Z["lf"][:, 0, :, :], Z["lf"][:, 0, :, :], 0.0, None, ALU.min))
            dve.tensor_tensor(Z["lf"][:, 0, :, :], Z["lf"][:, 0, :, :], Z["lf"][:, 1, :, :], ALU.subtract).then_inc(logf, 1)
            dve.wait_ge(cum_out, 2)
            done(dve.tensor_tensor(Z["cl"][:, 0, :], ps[0:8, 0, :], Z["ch"][:, 0, :].bitcast(F32), ALU.subtract))
            done(dve.scalar_tensor_tensor(out=Z["cl"][:, 1, :], in0=ps[0:8, 0, :], scalar=-1.0, in1=Z["ch"][:, 1, :].bitcast(F32),
                                          op0=ALU.mult, op1=ALU.subtract))

        @block.scalar
        def _(act):
            act.wait_ge(eased, 1)
            act.activation(Z["lf"][:, 1, :, :], Z["lf"][:, 1, :, :], ACT.Exp).then_inc(sq, 1)
            act.wait_ge(sq, 1)
            act.activation(Z["lf"][:, 1, :, :], Z["lf"][:, 1, :, :], ACT.Ln, bias=1.0).then_inc(sq, 1)
            act.wait_ge(cum, 1)
            act.activation(Z["ch"][:, 0, :], ps[0:8, 0, :], ACT.Copy).then_inc(cum_out, 1)
            act.activation(Z["ch"][:, 1, :], ps[0:8, 0, :], ACT.Copy, scale=-1.0).then_inc(cum_out, 1)
            act.wait_ge(cum_out, 2)

        @block.tensor
        def _(pe):
            pe.wait_ge(logf, 1)
            for tt in range(TT):
                for t2 in range(tt + 1):
                    last = pe.matmul(ps[0:8, 0, tt * P:(tt + 1) * P], Z["lf"][:, 0, t2, :],
                                     S("ones") if t2 < tt else S("upto"), start=(t2 == 0), stop=(t2 == tt))
            last.then_inc(cum, 1)


def gate_outputs(nc, Z):
    cols = (1304, 3360, 4384)
    with stage(nc, "sg", "dve_step") as (block, sg, dve_step):
        @block.scalar
        def _(act):
            for b, c in enumerate(cols):
                act.activation(Z["sgl"][:, b, :, :], Z["z"][:, :, c:c + 512], ACT.Sigmoid).then_inc(sg, 1)

        @block.vector
        def _(dve):
            done = Chain(dve, dve_step)
            for b, c in enumerate(cols):
                dve.wait_ge(sg, b + 1)
                o = Z["o"][b]
                done(dve.tensor_tensor(o, o, Z["z"][:, :, c:c + 512], ALU.mult))
                done(dve.tensor_tensor(o, o, Z["sgl"][:, b, :, :], ALU.mult))


def merge(nc, A, ps, T, U, l, raw, hi, lo):
    nr, nh = len(raw), len(hi)
    jobs = [(n, b) for n in range(2) for b in range(3)]
    names = ("w_branch_a_2", "w_branch_b_2", "w_branch_m_2")
    count = 3 * len(jobs)
    with stage(nc, *[f"raw_in{i}" for i in range(nr)], "hi_done", "lo_done", "used", "gates", "branch", "sg", "mul", "dve_step") as sems:
        block, raw_in, (hi_done, lo_done, used, gates, branch, sg, mul, dve_step) = sems[0], sems[1:1 + nr], sems[1 + nr:]

        @block.sync
        def _(sp):
            for q in range(count):
                (n, b), part = jobs[q // 3], q % 3
                if q >= nr:
                    sp.wait_ge(lo_done, q - nr + 1)
                if part < 2:
                    a = MERGE0 + b * D + n * 512
                    src = A["w_in_2"][l].rearrange("(k p) n -> p k n", p=P)[:, 4 * part:4 * part + 4, a:a + 512]
                else:
                    src = A[names[b]][l].rearrange("(k p) n -> p k n", p=P)[:, :, n * 512:(n + 1) * 512]
                sp.dma_start(raw[q % nr][:, :, :], src).then_inc(raw_in[q % nr], 16)

        @block.tensor
        def _(pe):
            for q in range(count):
                (n, b), part = jobs[q // 3], q % 3
                pe.wait_ge(lo_done, q + 1)
                for tt in range(TT):
                    m = (q // 3) * TT + tt
                    if m >= TT and part == 0:
                        pe.wait_ge(sg, m - TT + 1)
                    if m >= TT and part == 2:
                        pe.wait_ge(mul, m - TT + 1)
                    if part < 2:
                        o, xh, xl, base, last_k = ps[:, tt, :], U["hh"], U["hl"], 4 * part, 7
                    else:
                        o, xh, xl, base, last_k = ps[:, 4 + tt, :], U["oh"], U["ol"], 4 * b, 4 * b + 3
                    for k in range(4):
                        kk, at = base + k, slice(tt * P, (tt + 1) * P)
                        pe.matmul(o, xh[:, kk, at], hi[q % nh][:, k, :], start=(part != 1 and k == 0), stop=False)
                        pe.matmul(o, xh[:, kk, at], lo[q % nh][:, k, :], start=False, stop=False)
                        mm = pe.matmul(o, xl[:, kk, at], hi[q % nh][:, k, :], start=False, stop=(kk == last_k))
                    if part == 1:
                        mm.then_inc(gates, 1)
                    elif part == 2:
                        mm.then_inc(branch, 1)
                    elif tt == TT - 1:
                        mm.then_inc(used, 1)

        def wait_used(eng, q):
            if q % 3 == 0:
                eng.wait_ge(used, q // 3 + 1)
            else:
                eng.wait_ge(gates if q % 3 == 1 else branch, (q // 3 + 1) * TT)

        @block.scalar
        def _(act):
            def high(q):
                act.wait_ge(raw_in[q % nr], 16 * (q // nr + 1))
                if q >= nh:
                    wait_used(act, q - nh)
                act.activation(hi[q % nh][:, :, :], raw[q % nr][:, :, :], ACT.Copy).then_inc(hi_done, 1)

            for q in range(nh):
                high(q)
            for q in range(count):
                if q + nh < count:
                    high(q + nh)
                if q % 3 == 1:
                    for tt in range(TT):
                        m = (q // 3) * TT + tt
                        act.wait_ge(gates, m + 1)
                        if m >= TT:
                            act.wait_ge(mul, m - TT + 1)
                        act.activation(U["sg"][:, tt, :], ps[:, tt, :], ACT.Sigmoid).then_inc(sg, 1)

        @block.vector
        def _(dve):
            done = Chain(dve, dve_step)

            def low(q):
                dve.wait_ge(hi_done, q + 1)
                if q >= nh:
                    wait_used(dve, q - nh)
                dve.tensor_tensor(lo[q % nh][:, :, :], raw[q % nr][:, :, :], hi[q % nh][:, :, :].bitcast(F32), ALU.subtract).then_inc(lo_done, 1)

            for q in range(nh):
                low(q)
            for q in range(count):
                if q + nh < count:
                    low(q + nh)
                if q % 3 == 2:
                    n, b = jobs[q // 3]
                    for tt in range(TT):
                        m = (q // 3) * TT + tt
                        dve.wait_ge(sg, m + 1)
                        dve.wait_ge(branch, m + 1)
                        u = U["u"][:, tt, n * 512:(n + 1) * 512]
                        if b == 0:
                            dve.tensor_tensor(u, U["sg"][:, tt, :], ps[:, 4 + tt, :], ALU.mult).then_inc(mul, 1)
                        else:
                            dve.tensor_tensor(U["tmp"][:, :], U["sg"][:, tt, :], ps[:, 4 + tt, :], ALU.mult).then_inc(mul, 1)
                            dve.wait_ge(mul, m + 1)
                            done(dve.tensor_tensor(u, u, U["tmp"][:, :], ALU.add))


def add_stage(nc, x, y):
    with stage(nc, "dve_step") as (block, dve_step):
        @block.vector
        def _(dve):
            Chain(dve, dve_step)(dve.tensor_tensor(x, x, y, ALU.add))


def load_stage(nc, pairs):
    with stage(nc, "moved") as (block, moved):
        @block.sync
        def _(sp):
            for dst, src in pairs:
                sp.dma_start(dst, src).then_inc(moved, 16)
            sp.wait_ge(moved, 16 * len(pairs))


def split_ring(s, sb, tag, place, step, n):
    raw = [place[:, step * i:step * i + step, :] for i in range(12 // step)]
    hi = [sb(s, f"{tag}hi{i}", [P, step, 512], F32R) for i in range(n)]
    lo = [sb(s, f"{tag}lo{i}", [P, step, 512], F32R) for i in range(n)]
    return raw, hi, lo


def copy_evac(dst):
    def evac(act, n, m, psum):
        return act.activation(dst(n, m), psum, ACT.Copy)
    return evac


def tiles4(dst, src, cols, nt):
    out = []
    for c in range(cols):
        for t0 in range(0, nt, 4):
            ts = range(t0, min(t0 + 4, nt))
            out.append(([src(t, c) for t in ts], dst[:, c, t0 * P:(t0 + len(ts)) * P]))
    return out


def program(nc, A, out):
    spill = nc.dram_tensor("kept_rows", (P, 8192), F32).ap()
    with ExitStack() as top:
        def sb(ctx, name, shape, dt=F32):
            return ctx.enter_context(nc.sbuf_tensor(name, shape, dt))

        top.enter_context(nc.allow_non_contiguous_dma(reason="vectors of a few thousand elements, channel by partition"))
        psum = top.enter_context(nc.psum_tensor("ps", [P, 8, 512], F32))
        ps = psum[:, :, :]
        bank = [psum[:, i, :] for i in range(8)]
        T = {}
        T["small"] = sb(top, "small", [P, COMMON])

        def table(n):
            at, width = SMALL_AT[n]
            return T["small"][:, at:at + width] if at < COMMON else T["mixing"][:, at - COMMON:at - COMMON + width]

        T["s"] = table
        T["onerow"] = sb(top, "onerow", [1, P])
        ident = T["s"]("ident")

        with ExitStack() as mix:
            T["mixing"] = sb(mix, "mixing", [P, SMALL.shape[1] - COMMON])
            T["mixT"] = sb(mix, "mixT", [P, KD, SEQ])
            with ExitStack() as mt:
                T["mT"] = sb(mt, "mT", [P, SHIFT // P, ALLT])
                with ExitStack() as ft:
                    T["fT"] = sb(ft, "fT", [P, FN // P, SEQ])
                    with ExitStack() as one:
                        T["xn"] = sb(one, "xn", [P, TA, D])
                        T["modb"] = sb(one, "modb", [P, 6 * D])
                        T["modc"] = sb(one, "modc", [P, 2 * D])
                        with ExitStack() as s:
                            T["c2"] = sb(s, "c2", [P, 2 * KD])
                            T["csig"] = sb(s, "csig", [P, 2 * KD])
                            T["cwide"] = sb(s, "cwide", [P, 2 * KD, P])
                            T["gain"] = sb(s, "gain", [P, D])
                            T["bias"] = sb(s, "bias", [P, D])
                            T["stats"] = sb(s, "stats", [P, 96])
                            mt_flat = T["mT"][:, :, :].rearrange("p a b -> p (a b)")
                            ring = [mt_flat[:, i * 4096:(i + 1) * 4096].rearrange("p (k n) -> p k n", k=KD) for i in range(3)]
                            T["adab"] = sb(s, "adab", [1, 6 * D])
                            modulation(nc, A, bank, T, ring)
                            layer_norm_stage(nc, T["xn"][:, :, :], TA, T["gain"][:, :], T["bias"][:, :], T["stats"])
                        load_stage(nc, [(spill[:, 0:4096].rearrange("p (t d) -> p t d", t=TT), T["xn"][:, 0:TT, :]),
                                        (spill[:, 4096:8192], T["modb"][:, 2 * D:6 * D])])
                        modulate_stage(nc, T["xn"][:, 0:TT, :], T["xn"][:, 0:TT, :], TT, T["modb"][:, D:2 * D], T["modb"][:, 0:D])
                        modulate_stage(nc, T["xn"][:, TT:TA, :], T["xn"][:, TT:TA, :], 2, T["modc"][:, D:2 * D], T["modc"][:, 0:D])
                        with ExitStack() as s:
                            hT = sb(s, "hT", [P, KD, ALLT])
                            turn(nc, bank, ident, tiles4(hT, lambda t, c: T["xn"][:, t, c * P:(c + 1) * P], KD, TA))
                            T["mu"] = sb(s, "mu", [P, 4, SHIFT // P])
                            T["padg"] = [sb(s, f"padg{i}", [P, GRID_H + 2, GRID_W + 2]) for i in range(2)]
                            T["padc"] = [sb(s, f"padc{i}", [P, CTX + 2]) for i in range(2)]
                            T["nbr"] = sb(s, "nbr", [P, 2 * SEQ + CTX])
                            ring_flat = T["modb"][:, :]
                            ring = [ring_flat[:, i * 2048:(i + 1) * 2048].rearrange("p (k n) -> p k n", k=KD) for i in range(3)]
                            project_in(nc, A, bank, T, hT, ring)
                    with ExitStack() as s:
                        B = {"tab": sb(s, "tab", [P, BIG.shape[1]]), "bf": sb(s, "bf", [P, 4]), "wf": sb(s, "wf", [P, 4, P]),
                             "f12": sb(s, "f12", [P, 2, TT, FN]), "spec": sb(s, "spec", [P, 4, SEQ])}
                        T["b"] = lambda n: B["tab"][:, BIG_AT[n][0]:BIG_AT[n][0] + BIG_AT[n][1]]
                        fourier(nc, A, ps, T, B)
                with ExitStack() as s:
                    T["par"] = sb(s, "par", [P, 4, 8])
                    T["w2"] = sb(s, "w2", [P, C])
                    T["a2"] = sb(s, "a2", [P, C])
                    T["g2"] = sb(s, "g2", [P, 2, C])
                    T["gng"] = sb(s, "gng", [P, C])
                    T["gnb"] = sb(s, "gnb", [P, C])
                    rwkv_params(nc, A, T)
                    W = {n: sb(s, "cur_" + n, shape) for n, shape in {
                        "w2": [P, P], "a2": [P, P], "par": [P, 8], "ar": [P, 2, TA, 2, P], "bt": [P, 2, ALLT], "kt": [P, 2, ALLT],
                        "vrow": [P, TA, P], "arow": [P, 2, TA, P], "brow": [P, 2, TA, P], "krow": [P, 2, TA, P],
                        "qt": [P, 2, TT, P], "gt": [P, 2, NCH, HS], "hp": [P, 2, NCH, HS], "yr": [P, TT, 2, P],
                        "pc": [P, 2, NCH], "tot": [P, 2, NCH], "bon": [P, 16], "st": [P, 2, 2, HS]}.items()}
                    with nc.Fori(0, 4) as c:
                        with ExitStack() as q:
                            for n, shape in {"v": [P, ALLT], "lw": [P, 2, ALLT], "a": [P, 2, ALLT], "ci": [P, 2, ALLT],
                                             "e1": [P, 2, ALLT], "kd": [P, 2, ALLT], "kk": [P, ALLT], "t0": [P, ALLT],
                                             "rk": [P, 2, SEQ]}.items():
                                W[n] = sb(q, "prep_" + n, shape)
                            rwkv_prepare(nc, ps, T, W, c)
                            groups = []
                            for t0 in (0, 4):
                                ts = range(t0, min(t0 + 4, TA))
                                groups.append(([W["v"][:, t * P:(t + 1) * P] for t in ts], W["vrow"][:, ts[0]:ts[-1] + 1, :]))
                                for d in range(2):
                                    groups.append(([W["ar"][:, d, t, 0, :] for t in ts], W["arow"][:, d, ts[0]:ts[-1] + 1, :]))
                                    groups.append(([W["bt"][:, d, t * P:(t + 1) * P] for t in ts], W["brow"][:, d, ts[0]:ts[-1] + 1, :]))
                                    groups.append(([W["kt"][:, d, t * P:(t + 1) * P] for t in ts], W["krow"][:, d, ts[0]:ts[-1] + 1, :]))
                            turn(nc, bank, ident, groups)
                        with ExitStack() as q:
                            for n, shape in {"m": [P, 2, 4, 512], "x": [P, 2, 4, P], "xt": [P, 2, 4, P], "y": [P, 2, 4, P],
                                             "rhs": [P, 2, 4, P], "wu": [P, 2, 4, P]}.items():
                                W[n] = sb(q, "unit_" + n, shape)
                            rwkv_chunks(nc, ps, T, W)
                        rwkv_scan(nc, ps, T, W)
                        with ExitStack() as q:
                            for n, shape in {"mean": [P, 16], "var": [P, 16], "big": [P, 1024], "rw": [P, TT, P]}.items():
                                W[n] = sb(q, "out_" + n, shape)
                            rwkv_output(nc, ps, T, W, c)
            with ExitStack() as s:
                mo = sb(s, "mo", [P, TT, D])
                with ExitStack() as g:
                    mh, ml = sb(g, "mixh", [P, KD, SEQ], F32R), sb(g, "mixl", [P, KD, SEQ], F32R)
                    split_stage(nc, split_jobs(T["mixT"], mh, ml, KD))
                    w = A["w_out"][0].rearrange("(k p) n -> p k n", p=P)
                    split_gemm(nc, ps, lambda n: w[:, :, n * 512:(n + 1) * 512], lambda n: 512, 2, TT,
                               lambda k, m: mh[:, k, m * P:(m + 1) * P], lambda k, m: ml[:, k, m * P:(m + 1) * P],
                               *split_ring(g, sb, "o", sb(g, "oraw", [P, 12, 512]), 4, 2),
                               copy_evac(lambda n, m: mo[:, m, n * 512:(n + 1) * 512]))
                x1 = sb(s, "x1", [P, TT, D])
                g1 = sb(s, "g1", [P, D])
                gain = sb(s, "gain1", [P, D])
                bias = sb(s, "bias1", [P, D])
                stats = sb(s, "stats1", [P, 96])
                load_stage(nc, [(x1[:, :, :], spill[:, 0:4096].rearrange("p (t d) -> p t d", t=TT)),
                                (g1[:, :], spill[:, 4096:5120]),
                                (gain[:, :], A["ln1_g"][0].partition_broadcast(P)), (bias[:, :], A["ln1_b"][0].partition_broadcast(P))])
                residual_stage(nc, x1[:, :, :], mo[:, :, :], g1[:, :], TT)
                layer_norm_stage(nc, x1[:, :, :], TT, gain[:, :], bias[:, :], stats)
                load_stage(nc, [(spill[:, 0:4096].rearrange("p (t d) -> p t d", t=TT), x1[:, :, :])])
        with ExitStack() as moe:
            T["f"] = sb(moe, "f", [P, TT, D])
            R = {"gates": sb(moe, "gates", [P, TT, E]), "place": sb(moe, "place", [P, TT, E]), "nblki": sb(moe, "nblki", [P, E], I32)}
            M = {n: sb(moe, "ex_" + n, shape, F32R) for n, shape in {"hh": [P, TT, D], "hl": [P, TT, D], "b12": [2 * E, 2 * D]}.items()}
            with ExitStack() as s:
                mod = sb(s, "mod2", [P, 2 * D])
                hrow = sb(s, "hrow", [P, TT, D])
                b1r = sb(s, "b1r", [2 * E, 2 * D])
                load_stage(nc, [(mod[:, :], spill[:, 5120:7168]), (hrow[:, :, :], spill[:, 0:4096].rearrange("p (t d) -> p t d", t=TT)),
                                (b1r[0:E, :], A["b1"][0]), (b1r[E:2 * E, :], A["b1"][0])])
                modulate_stage(nc, hrow[:, :, :], hrow[:, :, :], TT, mod[:, D:2 * D], mod[:, 0:D])
                split_stage(nc, split_jobs(hrow, M["hh"], M["hl"], TT, 1))
                with stage(nc, "high", "low_") as (block, high, low_):
                    @block.scalar
                    def _(act):
                        act.activation(M["b12"][:, :], b1r[:, :], ACT.Copy).then_inc(high, 1)

                    @block.vector
                    def _(dve):
                        dve.wait_ge(high, 1)
                        dve.tensor_tensor(M["b12"][E:2 * E, :], b1r[E:2 * E, :], M["b12"][E:2 * E, :].bitcast(F32),
                                          ALU.subtract).then_inc(low_, 1)
                        dve.wait_ge(low_, 1)
                T["hT"] = sb(s, "hT2", [P, KD, SEQ])
                turn(nc, bank, ident, tiles4(T["hT"], lambda t, c: hrow[:, t, c * P:(c + 1) * P], KD, TT))
                for n, shape in {"wr": [P, KD, E], "br": [1, E], "b2": [E, D], "lg": [P, TT, E], "m8": [P, TT, 8], "i8f": [P, TT, 8],
                                 "g4": [P, TT, TOPK], "sum4": [P, TT], "sel": [P, TT, E], "tmp": [P, E], "nblk": [P, E],
                                 "gT": [E, SEQ]}.items():
                    R[n] = sb(s, "rt_" + n, shape)
                R["i8"] = sb(s, "rt_i8", [P, TT, 8], U32)
                router(nc, A, ps, T, R)
            with ExitStack() as s:
                for n, shape in {"arow": [P, 2, 256], "gl": [P, 2, 2, 256], "place": [P, TT], "next": [P, TT], "gate": [P, TT]}.items():
                    M[n] = sb(s, "ex_" + n, shape)
                for n, shape in {"xh": [P, KD, P], "xl": [P, KD, P], "ah": [P, KD, P], "al": [P, KD, P], "yh": [P, D], "yl": [P, D],
                                 "pm": [P, TT, P], "pT": [P, SEQ], "pick": [2 * E, P]}.items():
                    M[n] = sb(s, "ex_" + n, shape, F32R)
                M["raw"] = [sb(s, f"raw{i}", [P, 4, 512]) for i in range(4)]
                M["hi"] = [sb(s, f"whi{i}", [P, 4, 512], F32R) for i in range(4)]
                M["lo"] = [sb(s, f"wlo{i}", [P, 4, 512], F32R) for i in range(4)]
                M["xrow"] = M["gl"].rearrange("p a b c -> p (a b c)")
                M["pool_pieces"] = (3, 6, 8, 10)
                with stage(nc, "zero") as (block, zero):
                    @block.vector
                    def _(dve):
                        dve.memset(M["gate"][:, :], 0.0)
                        dve.memset(ps[:, 4:6, :], 0.0).then_inc(zero, 1)
                        dve.wait_ge(zero, 1)
                        dve.tensor_copy(M["pT"][:, :], ps[:, 4, :]).then_inc(zero, 1)
                        dve.wait_ge(zero, 2)
                experts(nc, A, ps, T, R, M)
            x1 = sb(moe, "x1b", [P, TT, D])
            g2 = sb(moe, "g2f", [P, D])
            gain = sb(moe, "gain2", [P, D])
            bias = sb(moe, "bias2", [P, D])
            stats = sb(moe, "stats2", [P, 96])
            load_stage(nc, [(g2[:, :], spill[:, 7168:8192]), (gain[:, :], A["ln2_g"][0].partition_broadcast(P)),
                            (bias[:, :], A["ln2_b"][0].partition_broadcast(P)),
                            (x1[:, :, :], spill[:, 0:4096].rearrange("p (t d) -> p t d", t=TT))])
            residual_stage(nc, x1[:, :, :], T["f"][:, :, :], g2[:, :], TT)
            layer_norm_stage(nc, x1[:, :, :], TT, gain[:, :], bias[:, :], stats)
            load_stage(nc, [(spill[:, 0:4096].rearrange("p (t d) -> p t d", t=TT), x1[:, :, :])])
        x = sb(top, "x", [P, TT, D])
        load_stage(nc, [(x[:, :, :], spill[:, 0:4096].rearrange("p (t d) -> p t d", t=TT))])

        T["mask"] = sb(top, "mask", [P, 2, P], F32R)
        with stage(nc, "copied") as (block, copied):
            @block.vector
            def _(dve):
                dve.tensor_copy(T["mask"][:, 0, :], ident).then_inc(copied, 1)
                dve.tensor_copy(T["mask"][:, 1, :], T["s"]("causal")).then_inc(copied, 1)
                dve.wait_ge(copied, 2)
        with nc.Fori(0, LAYERS) as l:
            layer(nc, A, ps, bank, T, x, l, sb)
        load_stage(nc, [(out[0].rearrange("(t p) d -> p t d", p=P), x[:, :, :])])


def layer(nc, A, ps, bank, T, x, l, sb):
    S = T["s"]
    ident = S("ident")
    with ExitStack() as lay:
        L = {n: sb(lay, "ly_" + n, shape) for n, shape in {
            "qg": [P, HS], "kg": [P, 3, HS], "fqg": [P, HS], "fkg": [P, HS], "mqg": [P, P], "mkg": [P, P], "fb": [P, 8]}.items()}
        kmT = sb(lay, "kmT", [P, 4, 256])
        vm = sb(lay, "vm", [P, 2, 512])
        hT = sb(lay, "hT3", [P, KD, SEQ])
        oT = sb(lay, "oT", [P, 12, SEQ])
        ss = sb(lay, "ss", [P, 4])
        r = sb(lay, "headr", [P, 100])
        with ExitStack() as s:
            ng, mg = sb(s, "ng", [P, D]), sb(s, "mg", [P, D])
            mem, memT = sb(s, "mem", [P, 2, D]), sb(s, "memT", [P, KD, 256])
            kv = sb(s, "kv", [P, 2, D])
            h = sb(s, "h3", [P, TT, D])
            tmp = sb(s, "tmp3", [P, D])
            load_stage(nc, [(mem[:, :, :], A["mem_2"][0].rearrange("(t p) d -> p t d", p=P)),
                            (ng[:, :], A["norm_g_2"][l].partition_broadcast(P)), (mg[:, :], A["mem_norm_g_2"][l].partition_broadcast(P)),
                            (L["qg"][:, :], A["nsa_q_norm_2"][l].partition_broadcast(P)),
                            (L["kg"][:, :, :], A["nsa_k_norm_2"][l].partition_broadcast(P)),
                            (L["fqg"][:, :], A["fox_q_norm_2"][l].partition_broadcast(P)),
                            (L["fkg"][:, :], A["fox_k_norm_2"][l].partition_broadcast(P)),
                            (L["mqg"][:, :], A["mem_q_norm_2"][l].partition_broadcast(P)),
                            (L["mkg"][:, :], A["mem_k_norm_2"][l].partition_broadcast(P)),
                            (L["fb"][:, :], A["fox_f_bias_2"][l].partition_broadcast(P))])
            with stage(nc, "scaled") as (block, scaled):
                @block.vector
                def _(dve):
                    dve.tensor_scalar(L["qg"][:, :], L["qg"][:, :], HS ** -0.5, None, ALU.mult).then_inc(scaled, 1)
                    dve.tensor_scalar(L["fqg"][:, :], L["fqg"][:, :], HS ** -0.5, None, ALU.mult).then_inc(scaled, 1)
                    dve.tensor_scalar(L["mqg"][:, :], L["mqg"][:, :], P ** -0.5, None, ALU.mult).then_inc(scaled, 1)
                    dve.wait_ge(scaled, 3)
            rms_rows(nc, mem, mem, mg[:, :], tmp, ss, 2)
            rms_rows(nc, h, x, ng[:, :], tmp, ss, TT)
            turn(nc, bank, ident, tiles4(memT, lambda t, c: mem[:, t, c * P:(c + 1) * P], KD, 2)
                 + tiles4(hT, lambda t, c: h[:, t, c * P:(c + 1) * P], KD, TT))
            mh, ml = sb(s, "memh", [P, KD, 256], F32R), sb(s, "meml", [P, KD, 256], F32R)
            split_stage(nc, split_jobs(memT, mh, ml, KD, 4))
            w = A["w_mem_kv_2"][l].rearrange("(k p) n -> p k n", p=P)
            split_gemm(nc, ps, lambda n: w[:, :, n * 512:(n + 1) * 512], lambda n: 512, 2, 2,
                      lambda k, m: mh[:, k, m * P:(m + 1) * P], lambda k, m: ml[:, k, m * P:(m + 1) * P], *split_ring(s, sb, "m", oT, 4, 2),
                      copy_evac(lambda n, m: kv[:, m, 0:512] if n == 0 else vm[:, m, :]))
            km = kv[:, :, 0:512].rearrange("p t (h s) -> p t h s", h=4)
            head_norms(nc, [(km, [(km, km)], L["mkg"][:, :], P)], h[:, :, :].rearrange("p a b -> p (a b)"), r)
            turn(nc, bank, ident, tiles4(kmT, lambda t, c: kv[:, t, c * P:(c + 1) * P], 4, 2))
        with ExitStack() as zs:
            z = sb(zs, "z", [P, TT, ZW])
            Z = {"z": z, "gate": sb(zs, "gate", [P, TT, 24])}
            with ExitStack() as s:
                hh, hl = sb(s, "hh_z", [P, KD, SEQ], F32R), sb(s, "hl_z", [P, KD, SEQ], F32R)
                split_stage(nc, split_jobs(hT, hh, hl, KD))
                w = A["w_in_2"][l].rearrange("(k p) n -> p k n", p=P)
                npc = -(-ZW // 512)
                split_gemm(nc, ps, lambda n: w[:, :, n * 512:min(n * 512 + 512, ZW)], lambda n: min(512, ZW - n * 512), npc, TT,
                          lambda k, m: hh[:, k, m * P:(m + 1) * P], lambda k, m: hl[:, k, m * P:(m + 1) * P],
                          *split_ring(s, sb, "z", oT, 2, 3),
                          copy_evac(lambda n, m: z[:, m, n * 512:min(n * 512 + 512, ZW)]))

            def cols(a, heads, size=HS):
                return z[:, :, a:a + heads * size].rearrange("p t (h s) -> p t h s", h=heads)

            Z["o"] = [z[:, :, 0:512], z[:, :, 1816:2328], z[:, :, 3872:4384]]
            with ExitStack() as nsa:
                Z["qT"] = sb(nsa, "qT", [P, 4, SEQ])
                for n in ("kcT", "vcT", "ksT", "kwT"):
                    Z[n] = sb(nsa, n, [P, SEQ])
                L["cw1"] = [oT[:, 0:KD, :].rearrange("p a b -> p (a b)").rearrange("p (l h) -> p l h", h=P),
                            sb(nsa, "cw1", [P, 32, P])[:, :, :]]
                L["cw2"] = sb(nsa, "cw2", [P, 2, HS])
                L["pe"] = sb(nsa, "pe", [32, 2, 2, HS])
                loads = []
                for i, name in enumerate("kv"):
                    for g in range(2):
                        w1 = A[f"cmp_w1_{name}_2"][l].rearrange("(l d) h -> d l h", d=HS)
                        loads.append((L["cw1"][i][g * HS:(g + 1) * HS, :, :], w1))
                        loads.append((L["pe"][:, i, g, :], A[f"cmp_pe_{name}_2"][l]))
                    loads.append((L["cw2"][:, i, :], A[f"cmp_w2_{name}_2"][l]))
                with ExitStack() as s:
                    qn = sb(s, "qn", [P, TT, 4, 2, HS])
                    sq = sb(s, "sqh", [P, 2048])
                    jobs = [(cols(0, 8), [(cols(g * 256, 4), qn[:, :, :, g, :]) for g in range(2)], L["qg"][:, :], HS)]
                    for a, i in ((768, 1), (1024, 2)):
                        jobs.append((cols(a, 2), [(cols(a, 2), cols(a, 2))], L["kg"][:, i, :], HS))
                    head_norms(nc, jobs, sq, r, loads)
                    qr = qn[:, :, :, :, :].rearrange("p t r g s -> p t (r g) s")
                    rope(nc, T, [qr, cols(512, 2), cols(768, 2), cols(1024, 2)], sq)
                    q2 = qn[:, :, :, :, :].rearrange("p t r g s -> p t r (g s)")
                    groups = tiles4(Z["qT"], lambda t, c: q2[:, t, c, :], 4, TT)
                    for n, a in (("kcT", 512), ("vcT", 640), ("ksT", 768), ("kwT", 1024)):
                        groups.append(([z[:, t, a:a + P] for t in range(TT)], Z[n][:, :]))
                    turn(nc, bank, ident, groups)
                    with stage(nc, "sg") as (block, sg):
                        @block.scalar
                        def _(act):
                            act.activation(Z["gate"][:, :, :], z[:, :, 1280:1304], ACT.Sigmoid).then_inc(sg, 1)
                            act.wait_ge(sg, 1)
                with ExitStack() as s:
                    for n, shape in {"blk": [P, 2, 32, 32], "hid": [P, 2, 2, 32], "hsg": [P, 2, 2, 32], "peT": [P, 2, 32],
                                     "kcr": [32, P], "vc": [P, P], "kc": [P, 32]}.items():
                        Z[n] = sb(s, "cp_" + n, shape)
                    compress(nc, ps, T, L, Z)
                    sq = sb(s, "sqc", [P, P])
                    kc4 = Z["kcr"][:, :].rearrange("p (t h s) -> p t h s", t=1, h=2)
                    head_norms(nc, [(kc4, [(kc4, kc4)], L["kg"][0:32, 0, :], HS)], sq, r)
                    turn(nc, bank, ident, [([Z["kcr"][:, :]], Z["kc"][:, :])])
                    Z["cp"] = sb(s, "cp", [P, TT, 256])
                    Z["cpT"] = sb(s, "cpT", [P, 2, SEQ])
                    Z["cm"] = sb(s, "cm", [P, 1, 32])
                    compressed_attention(nc, ps, T, Z)

                def common(s, tag):
                    for n, shape in {"p": [P, 3, SEQ], "pT": [P, 2, SEQ], "nm": [P, 4], "mx": [P, 4], "sum": [P, 4], "rs": [P, 4]}.items():
                        Z[n] = sb(s, f"{tag}_{n}", shape)

                def masked(i):
                    return T["mask"][:, 0, :], T["mask"][:, 1, :], i * P, (i + 1) * P

                with ExitStack() as s:
                    common(s, "nsa")
                    units = []
                    for kT, va, b in ((Z["ksT"], 896, 1), (Z["kwT"], 1152, 2)):
                        for h in range(8):
                            g, rr = h // 4, h % 4
                            for i in range(TT):
                                n = (i + 1) * P
                                units.append({
                                    "n": n, "w": HS, "q": Z["qT"][g * HS:(g + 1) * HS, rr, i * P:n], "k": kT[g * HS:(g + 1) * HS, 0:n],
                                    "extra": [masked(i)],
                                    "v": [z[:, kb, va + g * HS:va + (g + 1) * HS] for kb in range(i + 1)],
                                    "gate": Z["gate"][:, i, 3 * h + b:3 * h + b + 1], "o": Z["o"][0][:, i, h * HS:(h + 1) * HS]})
                    attention(nc, ps, T, Z, units)
            with ExitStack() as fox:
                fq, fk = sb(fox, "fqT", [P, 4, SEQ]), sb(fox, "fkT", [P, 4, SEQ])
                Z["lf"] = sb(fox, "lf", [P, 2, TT, 8])
                Z["ch"], Z["cl"] = sb(fox, "ch", [8, 2, SEQ], F32R), sb(fox, "cl", [8, 2, SEQ], F32R)
                with ExitStack() as s:
                    sq = sb(s, "sqf", [P, 2048])
                    head_norms(nc, [(cols(1816, 8), [(cols(1816, 8), cols(1816, 8))], L["fqg"][:, :], HS),
                                    (cols(2328, 8), [(cols(2328, 8), cols(2328, 8))], L["fkg"][:, :], HS)], sq, r)
                turn(nc, bank, ident, tiles4(fq, lambda t, c: z[:, t, 1816 + c * P:1816 + (c + 1) * P], 4, TT)
                     + tiles4(fk, lambda t, c: z[:, t, 2328 + c * P:2328 + (c + 1) * P], 4, TT))
                forget_bias(nc, ps, T, Z, L)
                common(fox, "fox")
                units = []
                for h in range(8):
                    lo, hi = HS * (h % 2), HS * (h % 2) + HS
                    pick = T["mask"][0:8, 0, h:h + 1]
                    for i in range(TT):
                        n = (i + 1) * P
                        units.append({
                            "n": n, "w": HS, "q": fq[lo:hi, h // 2, i * P:n], "k": fk[lo:hi, h // 2, 0:n],
                            "extra": [(Z["ch"][:, 0, i * P:n], pick.to_broadcast([8, n]), 0, n),
                                      (Z["cl"][:, 0, i * P:n], pick.to_broadcast([8, n]), 0, n),
                                      (pick.to_broadcast([8, P]), Z["ch"][:, 1, 0:n], 0, n),
                                      (pick.to_broadcast([8, P]), Z["cl"][:, 1, 0:n], 0, n), masked(i)],
                            "v": [z[:, kb, 2840 + h * HS:2840 + (h + 1) * HS] for kb in range(i + 1)],
                            "gate": None, "o": Z["o"][1][:, i, h * HS:(h + 1) * HS]})
                attention(nc, ps, T, Z, units)
            with ExitStack() as mm:
                mq = sb(mm, "mqT", [P, 4, SEQ])
                common(mm, "mem")
                sq = sb(mm, "sqm", [P, 2048])
                head_norms(nc, [(cols(3872, 4, P), [(cols(3872, 4, P), cols(3872, 4, P))], L["mqg"][:, :], P)], sq, r)
                turn(nc, bank, ident, tiles4(mq, lambda t, c: z[:, t, 3872 + c * P:3872 + (c + 1) * P], 4, TT))
                units = []
                for h in range(4):
                    for i in range(TT):
                        units.append({
                            "n": 256, "w": P, "q": mq[:, h, i * P:(i + 1) * P], "k": kmT[:, h, :], "extra": [],
                            "v": [vm[:, kb, h * P:(h + 1) * P] for kb in range(2)],
                            "gate": None, "o": Z["o"][2][:, i, h * P:(h + 1) * P]})
                attention(nc, ps, T, Z, units)
            with ExitStack() as s:
                Z["sgl"] = sb(s, "sgl", [P, 3, TT, 512])
                gate_outputs(nc, Z)
            groups = []
            for b in range(3):
                groups += tiles4(oT[:, 4 * b:4 * b + 4, :], lambda t, c, b=b: Z["o"][b][:, t, c * P:(c + 1) * P], 4, TT)
            turn(nc, bank, ident, groups)
        with ExitStack() as s:
            U = {"u": hT.rearrange("p k t -> p (k t)").rearrange("p (t d) -> p t d", t=TT),
                 "sg": sb(s, "usg", [P, TT, 512]), "tmp": sb(s, "utmp", [P, 512])}
            for n, k in (("hh", KD), ("hl", KD), ("oh", 12), ("ol", 12)):
                U[n] = sb(s, "u_" + n, [P, k, SEQ], F32R)
            split_stage(nc, split_jobs(hT, U["hh"], U["hl"], KD) + split_jobs(oT, U["oh"], U["ol"], 12))
            ring = split_ring(s, sb, "u", oT, 4, 2)
            merge(nc, A, ps, T, U, l, *ring)
            turn_split(nc, bank, ident, tiles4(U["hh"], lambda t, c: U["u"][:, t, c * P:(c + 1) * P], KD, TT), U["hh"], U["hl"])
            w = A["w_out_2"][l].rearrange("(k p) n -> p k n", p=P)
            split_gemm(nc, ps, lambda n: w[:, :, n * 512:(n + 1) * 512], lambda n: 512, 2, TT,
                      lambda k, m: U["hh"][:, k, m * P:(m + 1) * P], lambda k, m: U["hl"][:, k, m * P:(m + 1) * P], *ring,
                      copy_evac(lambda n, m: U["u"][:, m, n * 512:(n + 1) * 512]))
            add_stage(nc, x[:, :, :], U["u"][:, :, :])


_INS = ["x", "c", "ctx", "c_ctx", "ln0_g", "ln0_b", "w_ada", "b_ada", "w_in", "mu_shift", "w0", "w2_decay", "a0", "a2_iclr",
        "g2_gate", "r_k", "k_k", "k_a", "gn_g", "gn_b", "w_fno", "b_fno", "w_out", "ln1_g", "ln1_b", "w_router", "b_router",
        "w1", "b1", "w2", "b2", "ln2_g", "ln2_b", "mem_2", "norm_g_2", "mem_norm_g_2", "w_in_2", "nsa_q_norm_2",
        "nsa_k_norm_2", "cmp_pe_k_2", "cmp_w1_k_2", "cmp_w2_k_2", "cmp_pe_v_2", "cmp_w1_v_2", "cmp_w2_v_2", "fox_q_norm_2",
        "fox_k_norm_2", "fox_f_bias_2", "mem_q_norm_2", "mem_k_norm_2", "w_mem_kv_2", "w_branch_a_2", "w_branch_b_2",
        "w_branch_m_2", "w_out_2"]


def kernel(**inputs):
    import concourse.bacc as _bacc
    from concourse.bass_utils import run_bass_kernel_spmd as _run

    nc = _bacc.Bacc("TRN2", target_bir_lowering=False, num_devices=1)
    arrays, args = {}, {}
    given = {name: np.ascontiguousarray(inputs[name]) for name in _INS}
    given["small"], given["big"] = SMALL, BIG
    for name, a in given.items():
        arrays[f"in_{name}_dram"] = a
        args[name] = nc.dram_tensor(f"in_{name}_dram", a.shape, mybir.dt.from_np(a.dtype), kind="ExternalInput").ap()
    out = nc.dram_tensor("out_0_dram", (1, SEQ, D), F32, kind="ExternalOutput").ap()
    program(nc, args, out)
    r = _run(nc, [arrays], core_ids=[0])
    return r.results[0]["out_0_dram"]
```
